# Optimizing a Trainium2 kernel written in Bass

```python
import math
import jax, jax.numpy as jnp
from jax import lax
import numpy as np

D_MODEL = 1024
BATCH = 1
SEQ = 512
DEPTH = 2

D_FF = 4 * D_MODEL
EPS = 1e-6
NEG_BIG = -1e30
M_HEADS = 4
M_DIM = D_MODEL // 16
M_WIDTH = M_HEADS * M_DIM
M_CONV = 4
M_CHUNK = 128
A_HEADS = 4
A_DIM = D_MODEL // 16
A_WIDTH = A_HEADS * 2 * A_DIM
ROT_DIM = A_DIM // 4
ROPE_THETA = 500000.0
Q_BLOCK = 128
H_HEADS = 4
H_DK = D_MODEL // 16
H_DV = D_MODEL // 16
H_WIDTH = H_HEADS * H_DV
H_CHUNK = 64
D_MIX = M_WIDTH + A_WIDTH + H_WIDTH
M_COLS = 4 * M_WIDTH + 2 * M_HEADS
A_COLS = 3 * A_WIDTH
H_COLS = 4 * H_WIDTH
D_IN = M_COLS + A_COLS + H_COLS


def rmsnorm(x, g):
    xf = x.astype(jnp.float32)
    y = xf * lax.rsqrt(jnp.mean(xf * xf, axis=-1, keepdims=True) + EPS)
    return (y * g.astype(jnp.float32)).astype(x.dtype)

def causal_dwconv(x, w):
    K = w.shape[0]
    T = x.shape[1]
    xp = jnp.pad(x, ((0, 0), (K - 1, 0), (0, 0)))
    out = xp[:, 0:T] * w[0]
    for j in range(1, K):
        out = out + xp[:, j:j + T] * w[j]
    return out

def partial_rope(x, pos):
    half = ROT_DIM // 2
    inv = ROPE_THETA ** (-jnp.arange(half, dtype=jnp.float32) / half)
    ang = pos.astype(jnp.float32)[:, None] * inv[None, :]
    cos = jnp.cos(ang)[:, None, :]
    sin = jnp.sin(ang)[:, None, :]
    x1 = x[..., :half]
    x2 = x[..., half:ROT_DIM]
    r1 = x1 * cos - x2 * sin
    r2 = x2 * cos + x1 * sin
    return jnp.concatenate([r1, r2, x[..., ROT_DIM:]], axis=-1)

def to_chunks(a, L):
    B, H, T = a.shape[:3]
    a = a.reshape((B, H, T // L, L) + a.shape[3:])
    return jnp.moveaxis(a, 2, 0)

def from_chunks(a):
    a = jnp.moveaxis(a, 0, 2)
    B, H, NC, L = a.shape[:4]
    return a.reshape((B, H, NC * L) + a.shape[4:])

def mlstm_chunkwise(q, k, v, i_pre, f_pre):
    B, H, T, d = q.shape
    L = M_CHUNK
    k = k * (d ** -0.5)
    logf = jax.nn.log_sigmoid(f_pre)
    xs = (to_chunks(q, L), to_chunks(k, L), to_chunks(v, L), to_chunks(i_pre, L), to_chunks(logf, L))
    causal = jnp.tril(jnp.ones((L, L), dtype=bool))

    def step(carry, xs_c):
        C, n, m = carry
        qb, kb, vb, ib, fb = xs_c
        b = jnp.cumsum(fb, axis=-1)
        D = b[..., :, None] - b[..., None, :] + ib[..., None, :]
        D = jnp.where(causal, D, NEG_BIG)
        inter = b + m[..., None]
        m_t = jnp.maximum(jnp.max(D, axis=-1), inter)
        S = jnp.einsum('bhtd,bhsd->bhts', qb, kb) * jnp.exp(D - m_t[..., None])
        scale = jnp.exp(inter - m_t)
        num = jnp.einsum('bhts,bhsv->bhtv', S, vb) + scale[..., None] * jnp.einsum('bhvk,bhtk->bhtv', C, qb)
        den = jnp.sum(S, axis=-1) + scale * jnp.einsum('bhk,bhtk->bht', n, qb)
        h = num / jnp.maximum(jnp.abs(den), jnp.exp(-m_t))[..., None]
        bL = b[..., -1]
        g = bL[..., None] - b + ib
        m_new = jnp.maximum(bL + m, jnp.max(g, axis=-1))
        w_s = jnp.exp(g - m_new[..., None])
        decay = jnp.exp(bL + m - m_new)
        C_new = decay[..., None, None] * C + jnp.einsum('bhs,bhsv,bhsk->bhvk', w_s, vb, kb)
        n_new = decay[..., None] * n + jnp.einsum('bhs,bhsk->bhk', w_s, kb)
        return (C_new, n_new, m_new), h

    init = (jnp.zeros((B, H, d, d), jnp.float32), jnp.zeros((B, H, d), jnp.float32), jnp.zeros((B, H), jnp.float32))
    _, h = lax.scan(step, init, xs)
    return from_chunks(h)

def mlstm_mixer(q_pre, k_pre, v, o_pre, i_pre, f_pre, conv_w, gate_b, norm_g):
    B, T, _ = q_pre.shape
    f32 = jnp.float32
    qk = jax.nn.silu(causal_dwconv(jnp.concatenate([q_pre, k_pre], axis=-1).astype(f32), conv_w.astype(f32)))
    q, k = qk[..., :M_WIDTH], qk[..., M_WIDTH:]
    heads = lambda a: a.reshape(B, T, M_HEADS, M_DIM).transpose(0, 2, 1, 3)
    gb = gate_b.astype(f32)
    i_g = (i_pre.astype(f32) + gb[0]).transpose(0, 2, 1)
    f_g = (f_pre.astype(f32) + gb[1]).transpose(0, 2, 1)
    h = mlstm_chunkwise(heads(q), heads(k), heads(v.astype(f32)), i_g, f_g)
    h = rmsnorm(h.transpose(0, 2, 1, 3), norm_g)
    h = jax.nn.sigmoid(o_pre.astype(f32)).reshape(B, T, M_HEADS, M_DIM) * h
    return h.reshape(B, T, M_WIDTH)

def diff_attention(q, k, v, qn_g, kn_g, lam_vec, subln_g, lambda_init):
    B, T, _ = q.shape
    f32 = jnp.float32
    pos = jnp.arange(T)
    q = rmsnorm(q.astype(f32).reshape(B, T, A_HEADS, 2, A_DIM), qn_g)
    k = rmsnorm(k.astype(f32).reshape(B, T, A_HEADS, 2, A_DIM), kn_g)
    q = partial_rope(q.reshape(B, T, A_HEADS * 2, A_DIM), pos).reshape(B, T, A_HEADS, 2, A_DIM)
    k = partial_rope(k.reshape(B, T, A_HEADS * 2, A_DIM), pos).reshape(B, T, A_HEADS, 2, A_DIM)
    q = q * (A_DIM ** -0.5)
    v = v.astype(f32).reshape(B, T, A_HEADS, 2 * A_DIM).transpose(0, 2, 1, 3)
    kt = k.transpose(0, 2, 3, 1, 4)
    lv = lam_vec.astype(f32)
    lam = jnp.exp(jnp.sum(lv[0] * lv[1])) - jnp.exp(jnp.sum(lv[2] * lv[3])) + lambda_init
    NB = T // Q_BLOCK
    qb = q.reshape(B, NB, Q_BLOCK, A_HEADS, 2, A_DIM).transpose(1, 0, 3, 4, 2, 5)
    kpos = jnp.arange(T)

    def block(args):
        qi, bi = args
        s = jnp.einsum('bhcqd,bhckd->bhcqk', qi, kt)
        qpos = bi * Q_BLOCK + jnp.arange(Q_BLOCK)
        mask = qpos[:, None] >= kpos[None, :]
        p = jax.nn.softmax(jnp.where(mask, s, NEG_BIG), axis=-1)
        a = p[:, :, 0] - lam * p[:, :, 1]
        return jnp.einsum('bhqk,bhkv->bhqv', a, v)

    o = lax.map(block, (qb, jnp.arange(NB)))
    o = o.transpose(1, 0, 3, 2, 4).reshape(B, T, A_HEADS, 2 * A_DIM)
    o = rmsnorm(o, subln_g) * (1.0 - lambda_init)
    return o.reshape(B, T, A_WIDTH)

def hgrn2_chunkwise(q, logf, k, v):
    B, H, T, dk = q.shape
    dv = v.shape[-1]
    L = H_CHUNK
    xs = (to_chunks(q, L), to_chunks(logf, L), to_chunks(k, L), to_chunks(v, L))
    causal = jnp.tril(jnp.ones((L, L), dtype=bool))[..., None]

    def step(S, xs_c):
        qb, gb, kb, vb = xs_c
        Bc = jnp.cumsum(gb, axis=-2)
        diff = Bc[..., :, None, :] - Bc[..., None, :, :]
        decay = jnp.exp(jnp.where(causal, diff, NEG_BIG))
        A = jnp.einsum('bhtk,bhsk,bhtsk->bhts', qb, kb, decay)
        o = jnp.einsum('bhts,bhsv->bhtv', A, vb) + jnp.einsum('bhtk,bhkv->bhtv', qb * jnp.exp(Bc), S)
        BL = Bc[..., -1:, :]
        S_new = jnp.exp(BL[..., 0, :])[..., None] * S + jnp.einsum('bhsk,bhsv->bhkv', kb * jnp.exp(BL - Bc), vb)
        return S_new, o

    _, o = lax.scan(step, jnp.zeros((B, H, dk, dv), jnp.float32), xs)
    return from_chunks(o)

def hgrn2_mixer(q_pre, f_pre, i_pre, g_pre, lb, norm_g):
    B, T, _ = q_pre.shape
    f32 = jnp.float32
    heads = lambda a, dd: a.astype(f32).reshape(B, T, H_HEADS, dd).transpose(0, 2, 1, 3)
    q = jax.nn.silu(heads(q_pre, H_DK))
    fp = heads(f_pre, H_DK)
    lbh = lb.reshape(H_HEADS, 1, H_DK)
    f = lbh + (1.0 - lbh) * jax.nn.sigmoid(fp)
    logf = jnp.log(f)
    k = (1.0 - lbh) * jax.nn.sigmoid(-fp)
    v = heads(i_pre, H_DV)
    o = hgrn2_chunkwise(q, logf, k, v).transpose(0, 2, 1, 3)
    o = rmsnorm(o, norm_g) * jax.nn.silu(g_pre.astype(f32)).reshape(B, T, H_HEADS, H_DV)
    return o.reshape(B, T, H_WIDTH)

def first_inputs(seed: int = 0) -> dict:
    key = jax.random.key(seed)
    ks = jax.random.split(key, 20)
    f32 = jnp.float32
    nrm = lambda k, shp, s: jax.random.normal(k, shp, f32) * s
    f_bias = jnp.broadcast_to(jnp.linspace(3.0, 6.0, M_HEADS, dtype=f32), (DEPTH, M_HEADS))
    mlstm_gate_b = jnp.stack([nrm(ks[4], (DEPTH, M_HEADS), 0.1), f_bias + nrm(ks[5], (DEPTH, M_HEADS), 0.1)], axis=1)
    return {
        'x': jax.random.normal(ks[0], (BATCH, SEQ, D_MODEL), f32),
        'norm1_g': 1.0 + nrm(ks[1], (DEPTH, D_MODEL), 0.02),
        'w_in': nrm(ks[2], (DEPTH, D_MODEL, D_IN), D_MODEL ** -0.5),
        'mlstm_conv_w': nrm(ks[3], (DEPTH, M_CONV, 2 * M_WIDTH), M_CONV ** -0.5),
        'mlstm_gate_b': mlstm_gate_b,
        'mlstm_norm_g': 1.0 + nrm(ks[6], (DEPTH, M_DIM), 0.02),
        'diff_q_norm_g': 1.0 + nrm(ks[7], (DEPTH, A_DIM), 0.02),
        'diff_k_norm_g': 1.0 + nrm(ks[8], (DEPTH, A_DIM), 0.02),
        'diff_lambda': nrm(ks[9], (DEPTH, 4, A_DIM), 0.1),
        'diff_subln_g': 1.0 + nrm(ks[10], (DEPTH, 2 * A_DIM), 0.02),
        'hgrn_lb_param': nrm(ks[11], (DEPTH, H_HEADS * H_DK), 1.0),
        'hgrn_norm_g': 1.0 + nrm(ks[12], (DEPTH, H_DV), 0.02),
        'w_out': nrm(ks[13], (DEPTH, D_MIX, D_MODEL), D_MIX ** -0.5),
        'norm2_g': 1.0 + nrm(ks[14], (DEPTH, D_MODEL), 0.02),
        'w_up': nrm(ks[15], (DEPTH, D_MODEL, D_FF), D_MODEL ** -0.5),
        'w_down': nrm(ks[16], (DEPTH, D_FF, D_MODEL), D_FF ** -0.5),
    }

def first_block(x, norm1_g, w_in, mlstm_conv_w, mlstm_gate_b, mlstm_norm_g, diff_q_norm_g, diff_k_norm_g,
              diff_lambda, diff_subln_g, hgrn_lb_param, hgrn_norm_g, w_out, norm2_g, w_up, w_down):
    sm = jax.nn.softmax(hgrn_lb_param.astype(jnp.float32), axis=0)
    lower_bounds = jnp.cumsum(sm, axis=0) - sm[0]
    split_at = np.cumsum([M_WIDTH, M_WIDTH, M_WIDTH, M_WIDTH, M_HEADS, M_HEADS,
                          A_WIDTH, A_WIDTH, A_WIDTH,
                          H_WIDTH, H_WIDTH, H_WIDTH])
    for l in range(DEPTH):
        lambda_init = 0.8 - 0.6 * math.exp(-0.3 * l)
        h = rmsnorm(x, norm1_g[l])
        u = jnp.einsum('btd,de->bte', h, w_in[l])
        (mq, mk, mv, mo, mi, mf, aq, ak, av, hq, hf, hi, hg) = jnp.split(u, split_at, axis=-1)
        y_m = mlstm_mixer(mq, mk, mv, mo, mi, mf, mlstm_conv_w[l], mlstm_gate_b[l], mlstm_norm_g[l])
        y_a = diff_attention(aq, ak, av, diff_q_norm_g[l], diff_k_norm_g[l], diff_lambda[l], diff_subln_g[l], lambda_init)
        y_h = hgrn2_mixer(hq, hf, hi, hg, lower_bounds[l], hgrn_norm_g[l])
        mix = jnp.concatenate([y_m, y_a, y_h], axis=-1).astype(x.dtype)
        x = x + jnp.einsum('bte,ed->btd', mix, w_out[l])
        h2 = rmsnorm(x, norm2_g[l])
        a = jnp.square(jax.nn.relu(jnp.einsum('btd,df->btf', h2, w_up[l])))
        x = x + jnp.einsum('btf,fd->btd', a, w_down[l])
    return x


N_A_LAYERS = DEPTH // 2
N_B_LAYERS = DEPTH - N_A_LAYERS

D_FF_2 = ((8 * D_MODEL // 3 + 255) // 256) * 256
N_FFN_PER_LAYER = 2

POOL_WINDOWS = (2, 4, 8, 16)
POOL_GROUPS = len(POOL_WINDOWS)
POOL_GROUP_DIM = D_MODEL // POOL_GROUPS

ATTN_GROUPS = ((128, 1), (512, 4), (2048, 16))
N_ATTN_GROUPS = len(ATTN_GROUPS)
HEAD_DIM = 64
HEADS_PER_GROUP = D_MODEL // (2 * HEAD_DIM)
QKV_WIDTH = N_ATTN_GROUPS * HEADS_PER_GROUP * HEAD_DIM
O_WIDTH = HEADS_PER_GROUP * HEAD_DIM
ROPE_THETA_2 = 10000.0

N_NORMS_PER_LAYER = 6
RMS_EPS = 1e-6
NEG_BIG_2 = -1e30


def rms_norm(x, gain):
    x32 = x.astype(jnp.float32)
    y = x32 * lax.rsqrt(jnp.mean(x32 * x32, axis=-1, keepdims=True) + RMS_EPS) * gain.astype(jnp.float32)
    return y.astype(x.dtype)

def swiglu(h, w_gate, w_up, w_down):
    return (jax.nn.silu(h @ w_gate) * (h @ w_up)) @ w_down

def rope_tables(positions):
    inv_freq = ROPE_THETA_2 ** (-jnp.arange(0, HEAD_DIM, 2, dtype=jnp.float32) / HEAD_DIM)
    ang = positions.astype(jnp.float32)[..., None] * inv_freq
    return jnp.cos(ang), jnp.sin(ang)

def apply_rope(x, cos, sin):
    extra = x.ndim - 3
    shape = cos.shape[:2] + (1,) * extra + cos.shape[-1:]
    c = cos.reshape(shape)
    s = sin.reshape(shape)
    x32 = x.astype(jnp.float32)
    x1, x2 = jnp.split(x32, 2, axis=-1)
    out = jnp.concatenate([x1 * c - x2 * s, x2 * c + x1 * s], axis=-1)
    return out.astype(x.dtype)

def pool_mixer(h, w_in, w_group, scale, w_out):
    B, S, _ = h.shape
    u = h @ w_in
    u32 = u.astype(jnp.float32)
    csum = jnp.cumsum(u32, axis=1)
    t = jnp.arange(S)
    pooled = []
    for g, w in enumerate(POOL_WINDOWS):
        lo, hi = g * POOL_GROUP_DIM, (g + 1) * POOL_GROUP_DIM
        c = csum[..., lo:hi]
        c_prev = jnp.pad(c, ((0, 0), (w, 0), (0, 0)))[:, :S]
        count = jnp.minimum(t + 1, w).astype(jnp.float32)[None, :, None]
        pooled.append((c - c_prev) / count - u32[..., lo:hi])
    p = jnp.stack(pooled, axis=2).astype(u.dtype)
    y = jnp.einsum('bsgc,gcd->bsgd', p, w_group).reshape(B, S, D_MODEL) * scale
    return y @ w_out

def dilated_window_attention(q, k, v, window, dilation):
    B, S, H, Dh = q.shape
    blk = window // dilation
    span = blk * dilation
    s_pad = -(-S // span) * span
    nb = s_pad // span

    def split(a):
        a = jnp.pad(a, ((0, 0), (0, s_pad - S), (0, 0), (0, 0)))
        return a.reshape(B, nb, blk, dilation, H, Dh)

    def with_prev(a):
        prev = jnp.pad(a[:, :-1], ((0, 0), (1, 0), (0, 0), (0, 0), (0, 0), (0, 0)))
        return jnp.concatenate([prev, a], axis=2)

    qb = split(q)
    kc = with_prev(split(k))
    vc = with_prev(split(v))
    s = jnp.einsum('bnqrhd,bnkrhd->bnrhqk', qb, kc, preferred_element_type=jnp.float32) * (Dh ** -0.5)
    qi = jnp.arange(blk)[:, None]
    kj = jnp.arange(2 * blk)[None, :]
    band = (kj >= qi) & (kj <= qi + blk)
    valid_prev = (jnp.arange(nb)[:, None, None] > 0) | (kj[None] >= blk)
    mask = band[None] & valid_prev
    s = jnp.where(mask[None, :, None, None], s, NEG_BIG_2)
    m = jnp.max(s, axis=-1, keepdims=True)
    p = jnp.exp(s - m)
    den = jnp.sum(p, axis=-1, keepdims=True)
    o = jnp.einsum('bnrhqk,bnkrhd->bnqrhd', (p / den).astype(v.dtype), vc)
    lse = (m + jnp.log(den))[..., 0]
    o = o.reshape(B, s_pad, H, Dh)[:, :S]
    lse = lse.transpose(0, 1, 4, 2, 3).reshape(B, s_pad, H)[:, :S]
    return o, lse

def shared_kv(h, kv_gain, w_k, w_v, cos, sin):
    B, S, _ = h.shape
    hk = rms_norm(h, kv_gain)
    k = (hk @ w_k).reshape(B, S, N_ATTN_GROUPS, HEADS_PER_GROUP, HEAD_DIM)
    v = (hk @ w_v).reshape(B, S, N_ATTN_GROUPS, HEADS_PER_GROUP, HEAD_DIM)
    return apply_rope(k, cos, sin), v

def dilated_mixer(h, cos, sin, w_q, k_sh, v_sh, w_o):
    B, S, _ = h.shape
    q = (h @ w_q).reshape(B, S, N_ATTN_GROUPS, HEADS_PER_GROUP, HEAD_DIM)
    q = apply_rope(q, cos, sin)
    outs, lses = [], []
    for g, (window, dilation) in enumerate(ATTN_GROUPS):
        o, l = dilated_window_attention(q[:, :, g], k_sh[:, :, g], v_sh[:, :, g], window, dilation)
        outs.append(o)
        lses.append(l)
    wts = jax.nn.softmax(jnp.stack(lses, axis=0), axis=0)
    o = jnp.sum(wts[..., None] * jnp.stack(outs, axis=0).astype(jnp.float32), axis=0).astype(h.dtype)
    return o.reshape(B, S, O_WIDTH) @ w_o

def second_inputs(seed: int = 0) -> dict:
    key = jax.random.key(seed)
    ks = jax.random.split(key, 16)
    f32 = jnp.float32

    def w(k, shape, fan_in):
        return jax.random.normal(k, shape, f32) * (fan_in ** -0.5)

    x = jax.random.normal(ks[0], (BATCH, SEQ, D_MODEL), f32)
    offset = jax.random.randint(ks[1], (BATCH, 1), 0, 1024, dtype=jnp.int32)
    positions = (jnp.arange(SEQ, dtype=jnp.int32)[None, :] + offset).astype(jnp.int32)
    norm_gain = 1.0 + 0.05 * jax.random.normal(ks[2], (DEPTH, N_NORMS_PER_LAYER, D_MODEL), f32)
    ffn_w_gate = w(ks[3], (DEPTH, N_FFN_PER_LAYER, D_MODEL, D_FF_2), D_MODEL)
    ffn_w_up = w(ks[4], (DEPTH, N_FFN_PER_LAYER, D_MODEL, D_FF_2), D_MODEL)
    ffn_w_down = w(ks[5], (DEPTH, N_FFN_PER_LAYER, D_FF_2, D_MODEL), D_FF_2)
    pool_w_in = w(ks[6], (N_A_LAYERS, D_MODEL, D_MODEL), D_MODEL)
    pool_w_group = w(ks[7], (N_A_LAYERS, POOL_GROUPS, POOL_GROUP_DIM, POOL_GROUP_DIM), POOL_GROUP_DIM)
    pool_scale = 1.0 + 0.1 * jax.random.normal(ks[8], (N_A_LAYERS, D_MODEL), f32)
    pool_w_out = w(ks[9], (N_A_LAYERS, D_MODEL, D_MODEL), D_MODEL)
    kv_norm_gain = 1.0 + 0.05 * jax.random.normal(ks[10], (D_MODEL,), f32)
    w_k = w(ks[11], (D_MODEL, QKV_WIDTH), D_MODEL)
    w_v = w(ks[12], (D_MODEL, QKV_WIDTH), D_MODEL)
    attn_w_q = w(ks[13], (N_B_LAYERS, D_MODEL, QKV_WIDTH), D_MODEL)
    attn_w_o = w(ks[14], (N_B_LAYERS, O_WIDTH, D_MODEL), O_WIDTH)
    return {
        "x": x, "positions": positions, "norm_gain": norm_gain,
        "ffn_w_gate": ffn_w_gate, "ffn_w_up": ffn_w_up, "ffn_w_down": ffn_w_down,
        "pool_w_in": pool_w_in, "pool_w_group": pool_w_group, "pool_scale": pool_scale,
        "pool_w_out": pool_w_out, "kv_norm_gain": kv_norm_gain, "w_k": w_k, "w_v": w_v,
        "attn_w_q": attn_w_q, "attn_w_o": attn_w_o,
    }

def second_block(x, positions, norm_gain, ffn_w_gate, ffn_w_up, ffn_w_down, pool_w_in, pool_w_group,
              pool_scale, pool_w_out, kv_norm_gain, w_k, w_v, attn_w_q, attn_w_o):
    cos, sin = rope_tables(positions)
    h = x
    k_sh = None
    v_sh = None
    for layer in range(DEPTH):
        g = norm_gain[layer]
        f = swiglu(rms_norm(h, g[0]), ffn_w_gate[layer, 0], ffn_w_up[layer, 0], ffn_w_down[layer, 0])
        h = h + 0.5 * rms_norm(f, g[1])
        hm = rms_norm(h, g[2])
        if layer < N_A_LAYERS:
            mix = pool_mixer(hm, pool_w_in[layer], pool_w_group[layer], pool_scale[layer], pool_w_out[layer])
        else:
            b = layer - N_A_LAYERS
            mix = dilated_mixer(hm, cos, sin, attn_w_q[b], k_sh, v_sh, attn_w_o[b])
        h = h + rms_norm(mix, g[3])
        f = swiglu(rms_norm(h, g[4]), ffn_w_gate[layer, 1], ffn_w_up[layer, 1], ffn_w_down[layer, 1])
        h = h + 0.5 * rms_norm(f, g[5])
        if layer == N_A_LAYERS - 1:
            k_sh, v_sh = shared_kv(h, kv_norm_gain, w_k, w_v, cos, sin)
    return h


def setup_inputs(seed=0):
    out = dict(first_inputs(seed))
    for name, value in second_inputs(seed + 1).items():
        if name != "x":
            out[name + "_2"] = value
    return out


def reference(
    x, norm1_g, w_in, mlstm_conv_w, mlstm_gate_b, mlstm_norm_g, diff_q_norm_g, diff_k_norm_g,
    diff_lambda, diff_subln_g, hgrn_lb_param, hgrn_norm_g, w_out, norm2_g, w_up, w_down,
    positions_2, norm_gain_2, ffn_w_gate_2, ffn_w_up_2, ffn_w_down_2, pool_w_in_2,
    pool_w_group_2, pool_scale_2, pool_w_out_2, kv_norm_gain_2, w_k_2, w_v_2, attn_w_q_2,
    attn_w_o_2,
):
    x = first_block(
        x, norm1_g, w_in, mlstm_conv_w, mlstm_gate_b, mlstm_norm_g, diff_q_norm_g,
        diff_k_norm_g, diff_lambda, diff_subln_g, hgrn_lb_param, hgrn_norm_g, w_out, norm2_g,
        w_up, w_down,
    )
    return second_block(
        x, positions_2, norm_gain_2, ffn_w_gate_2, ffn_w_up_2, ffn_w_down_2, pool_w_in_2,
        pool_w_group_2, pool_scale_2, pool_w_out_2, kv_norm_gain_2, w_k_2, w_v_2, attn_w_q_2,
        attn_w_o_2,
    )


_drawn_inputs = setup_inputs


def setup_inputs(seed=0):
    import zlib

    import numpy as np

    out = dict(_drawn_inputs(seed))
    spreads = {}
    factors = {'mlstm_norm_g': 22.603,
     'diff_q_norm_g': 4.649,
     'diff_k_norm_g': 4.394,
     'diff_subln_g': 4.06,
     'hgrn_lb_param': 2.904,
     'hgrn_norm_g': 24.03,
     'kv_norm_gain_2': 61.357,
     'norm2_g': 2.84,
     'pool_scale_2': 23.56,
     'norm_gain_2': 4.376}
    for name, (base, spread) in spreads.items():
        noise = np.random.default_rng([zlib.crc32(name.encode()), seed]).standard_normal(out[name].shape)
        drawn = base * np.exp(spread * noise) if base else spread * noise
        out[name] = __import__('jax').numpy.asarray(drawn.astype(out[name].dtype))
    for name, factor in factors.items():
        out[name] = (out[name] * factor).astype(out[name].dtype)
    return out
```

```python
import math
from contextlib import ExitStack, contextmanager

import numpy as np

import concourse.bass as bass
from concourse import mybir

F32 = mybir.dt.float32
F32R = mybir.dt.float32r
U8 = mybir.dt.uint8
I32 = mybir.dt.int32
ALU = mybir.AluOpType
ACT = mybir.ActivationFunctionType
AX = mybir.AxisListType

P = 128
D = 1024
T = 512
DEPTH = 2
KC = D // P
HD = 64
NB = T // P
M_TILES, A_TILES, H_TILES = 2, 4, 2
M_COLS = 4 * 256 + 8
D_IN = M_COLS + 3 * 512 + 4 * 256
GATES = 4 * 256
F1 = 4 * D
F1_GROUPS = (16, 16)
F2 = 2816
F2_GROUPS = (12, 10)
QKV = 3 * 8 * HD
OW = 8 * HD
EPS = 1e-6
NEG = -1e30
POOL_WINDOWS = (2, 4, 8, 16)
LEVELS = (1, 2, 4, 8, 16, 32, 64)
SLOT = 2048
TWO_PI = 2 * math.pi

MQ, MK, MV, MO = 0, 2, 4, 6
AQ, AK, AV = 8, 12, 16
HQ, HF, HI, HG = 20, 22, 24, 26
U_TILES = 28

C_IDENT, C_BLOCK, C_CAUSAL, C_PAST, C_CAUSAL4, C_LATER, C_ROT_A, C_ROT_B, C_IND = range(9)
N_CONST = 9

R_NORM1, R_NORM2, R_GAIN2 = 0, 16, 32
R_KV, R_POOL, R_CONV, R_LB, R_MN, R_QN, R_KN, R_HN, R_SUB = [P + r for r in (0, 8, 16, 48, 52, 54, 56, 58, 60)]
N_ROWS = P + 62


def constants():
    c = np.zeros((P, N_CONST, P), np.float32)
    k, q = np.arange(P)[None, :], np.arange(P)[:, None]
    c[:, C_IDENT] = np.eye(P)
    c[:, C_BLOCK] = (k // HD) == (q // HD)
    c[:, C_CAUSAL] = np.where(k <= q, 0, NEG)
    c[:, C_PAST] = np.where(k >= q, 0, NEG)
    c[:, C_CAUSAL4] = np.where((k <= q) & (k % 4 == q % 4), 0, NEG)
    c[:, C_LATER] = np.where(q > k, -NEG, 0)
    for m, half, width in ((C_ROT_A, 8, 16), (C_ROT_B, 32, 64)):
        for p in range(P):
            r = p % HD
            if r < half:
                c[p + half, m, p] = -1
            elif r < width:
                c[p - half, m, p] = 1
    for j in range(8):
        for p in range(P):
            c[p, C_IND, 16 * j + 2 * j + p // HD] = 1
    sel = np.zeros((16, 8, P), np.float32)
    for j in range(8):
        sel[2 * j, j, :HD] = 1
        sel[2 * j + 1, j, HD:] = 1
    half = 8
    inv_a = (np.float32(500000.0) ** (-np.arange(half, dtype=np.float32) / np.float32(half))).astype(np.float32)
    inv_b = (np.float32(10000.0) ** (-np.arange(0, HD, 2, dtype=np.float32) / np.float32(HD))).astype(np.float32)
    p = np.arange(P)
    freq = inv_b[p % 32][:, None].astype(np.float32)
    ang = np.arange(T, dtype=np.float32)[None, :] * inv_a[:, None]
    rot = np.zeros((P, 2, T), np.float32)
    turned = p % HD < 2 * half
    rot[:, 0] = np.where(turned[:, None], np.cos(ang)[p % half], 1)
    rot[:, 1] = np.where(turned[:, None], np.sin(ang)[p % half], 0)
    t = np.arange(T)
    inv_count = np.stack([1.0 / np.minimum(t + 1, w) for w in POOL_WINDOWS]).astype(np.float32)
    level = np.zeros((P, len(LEVELS), P), np.float32)
    s, u = np.arange(P)[:, None], np.arange(P)[None, :]
    for n, b in enumerate(LEVELS):
        level[:, n] = (s // (2 * b) == u // (2 * b)) & (s // b % 2 == 0) & (u // b % 2 == 1)
    return c.reshape(P, -1), sel.reshape(16, -1), freq, rot.reshape(P, -1), inv_count, level.reshape(P, -1)


class Count:

    def __init__(self, handle):
        self.handle, self.n = handle, 0


class Mark:

    def __init__(self, count, n, loops):
        self.count, self.n, self.loops = count, n, loops


class Flow:

    def __init__(self, nc):
        self.nc, self.loops, self.counts, self.engines = nc, [], [], []

    def count(self, name):
        c = Count(self.nc.alloc_semaphore(name))
        self.counts.append(c)
        return c

    def at(self, count, back=0):
        return Mark(count, count.n - back, tuple(self.loops))

    def value(self, mark):
        v = mark.n
        for loop in mark.loops:
            per = loop["per"].get(mark.count, 0)
            if per:
                v = v + (loop["turn"] * per if loop in self.loops else per * (loop["turns"] - 1))
        return v

    @contextmanager
    def turns(self, turns, per):
        entry = {c: c.n for c in self.counts}
        for e in self.engines:
            e.forget()
        with self.nc.Fori(0, turns) as turn:
            loop = {"turn": turn, "turns": turns, "per": per}
            self.loops.append(loop)
            yield turn
            self.loops.pop()
        for e in self.engines:
            e.forget()
        for c in self.counts:
            got = c.n - entry[c]
            assert got == per.get(c, 0), f"{c.handle}: a turn counts {got}, not {per.get(c, 0)}"
            c.n = entry[c] + got * turns


class Engine:

    def __init__(self, flow, queue, count, fixed=None):
        self.flow, self.queue, self.count, self.fixed = flow, queue, count, fixed
        self.passed = {}
        flow.engines.append(self)

    def forget(self):
        self.passed = {}

    def after(self, *marks):
        moving = False
        for m in marks:
            if m is None:
                continue
            v = self.flow.value(m)
            if isinstance(v, int):
                if self.passed.get(m.count, 0) >= v:
                    continue
                self.passed[m.count] = v
            else:
                moving = True
            self.queue.wait_ge(m.count.handle, v)
        if moving and self.fixed is not None:
            self.queue.wait_ge(self.fixed.handle, 1)
        return self.queue

    def did(self, instruction, count=None, by=1):
        count = count or self.count
        instruction.then_inc(count.handle, by)
        count.n += by
        return self.flow.at(count)


def tile(buf, j):
    if isinstance(j, int):
        return buf[:, j, :]
    return buf[:, bass.ds(j, 1), :].rearrange("p a t -> p (a t)")


BASE = 16512
TILE = T * 4
RING_AT = BASE
X_AT = RING_AT + 6 * SLOT * 4
XH_AT = X_AT + KC * TILE
XL_AT = XH_AT + KC * TILE
BIG_AT = XL_AT + KC * TILE
SMALL_AT = BIG_AT + 44 * TILE
END = 229344


def plan():
    out = []
    for l in range(DEPTH):
        out += [(f"in_m{l}", 4, KC, 2), (f"gates{l}", 1, KC, 0), (f"in_ah{l}", 10, KC, 2), (f"out{l}", KC // 2, KC, 2)]
        for g, n in enumerate(F1_GROUPS):
            out += [(f"up{l}{g}", n // 2, KC, 2), (f"down{l}{g}", KC, n, 1)]

    def ffn(name):
        return [x for g, n in enumerate(F2_GROUPS)
                for x in ((f"gateup{name}{g}", n, KC, 2), (f"back{name}{g}", KC, n, 1))]
    out += ffn("a")
    out += [("pool_in", KC // 2, KC, 2), ("pool_group", 4, 2, 2), ("pool_out", KC // 2, KC, 2)]
    out += ffn("b")
    out += [("k", 6, KC, 2), ("v", 6, KC, 2)]
    out += ffn("c")
    out += [("q", 6, KC, 2), ("o", KC // 2, OW // P, 2)]
    out += ffn("d")
    return out


PLAN = plan()


def words(phase):
    _, _, nk, tiles = phase
    return nk * (tiles * P if tiles else HD)


class Kernel:

    def __init__(self, nc, dram):
        self.nc, self.dram = nc, dram
        f = self.flow = Flow(nc)
        at = nc.alloc_sbuf_tensor_at

        self.raw = [at(f"raw{s}", [P, SLOT], F32, offset=RING_AT + s * SLOT * 4) for s in range(2)]
        self.whi = [at(f"whi{s}", [P, SLOT], F32R, offset=RING_AT + (2 + s) * SLOT * 4) for s in range(2)]
        self.wlo = [at(f"wlo{s}", [P, SLOT], F32R, offset=RING_AT + (4 + s) * SLOT * 4) for s in range(2)]
        self.x = at("x", [P, KC, T], F32, offset=X_AT)
        self.xh = at("xh", [P, KC, T], F32R, offset=XH_AT)
        self.xl = at("xl", [P, KC, T], F32R, offset=XL_AT)
        self.scr = at("scr", [P, 2 * KC, T], F32, offset=XH_AT)
        self.u = at("u", [P, U_TILES, T], F32, offset=BIG_AT)
        self.mh = at("mh", [P, KC, T], F32R, offset=BIG_AT + 28 * TILE)
        self.ml = at("ml", [P, KC, T], F32R, offset=BIG_AT + 36 * TILE)
        self.spare = at("spare", [P, 2 * KC, T], F32, offset=BIG_AT + 28 * TILE)
        self.ah = at("ah", [P, 16, T], F32R, offset=BIG_AT)
        self.al = at("al", [P, 16, T], F32R, offset=BIG_AT + 16 * TILE)
        self.al2 = at("al2", [P, 12, T], F32R, offset=BIG_AT + 12 * TILE)
        self.f = at("f", [P, KC, T], F32, offset=BIG_AT + 26 * TILE)
        self.qkv = at("qkv", [P, 36, T], F32, offset=BIG_AT)
        self.oh = at("oh", [P, 4, T], F32R, offset=BIG_AT + 36 * TILE)
        self.ol = at("ol", [P, 4, T], F32R, offset=BIG_AT + 40 * TILE)
        self.small = SMALL_AT
        self.const = self.keep("const", [P, N_CONST, P], F32)
        self.sel = self.keep("sel", [16, 8, P], F32)
        self.ones = self.keep("ones", [P, P], F32)
        self.cols = self.keep("cols", [P, N_ROWS], F32)
        self.rs = self.keep("rs", [P, T], F32)
        self.sqacc = self.keep("sqacc", [P, T], F32)
        self.ta = [self.keep(f"ta{i}", [P, T], F32) for i in range(2)]
        self.tb = [self.keep(f"tb{i}", [P, T], F32) for i in range(2)]
        self.level = self.keep("level", [P, len(LEVELS), P], U8)
        self.freq = self.keep("freq", [P, 1], F32)
        self.gate_b = self.keep("gate_b", [4, 4], F32)
        self.lb = self.keep("lb", [P, 8], F32)
        self.tiny = self.keep("tiny", [P, 64], F32)
        assert self.small <= END, self.small - END
        self.bank = [nc.alloc_psum_tensor(f"bank{i}", [P, T], F32) for i in range(8)]

        self.c_pe, self.c_dve, self.c_act, self.c_pool = [f.count(n) for n in ("pe", "dve", "act", "pool")]
        self.c_fixed = f.count("fixed")
        self.c_raw = [f.count("raw_landed0"), f.count("raw_landed1")]
        self.c_hi, self.c_lo, self.c_mm, self.c_ev = [f.count(n) for n in ("hi_made", "lo_made", "tiles_done", "tiles_read")]
        self.c_tab, self.c_kv = f.count("tables_loaded"), f.count("keys_values_loaded")
        self.c_load, self.c_spill, self.c_out = f.count("loaded"), f.count("spilled"), f.count("stored")
        self.pe = Engine(f, nc.tensor, self.c_pe)
        self.v = Engine(f, nc.vector, self.c_dve)
        self.a = Engine(f, nc.scalar, self.c_act, self.c_fixed)
        self.g = Engine(f, nc.gpsimd, self.c_pool)
        self.sp = Engine(f, nc.sync, self.c_load)
        nc.scalar.sem_inc(self.c_fixed.handle, 1)
        for e, c, n in ((nc.gpsimd, self.c_lo, 2), (nc.tensor, self.c_mm, 4), (nc.vector, self.c_ev, 4)):
            e.sem_inc(c.handle, n)
            c.n = n
        self.unit = 0
        self.phase = 0
        self.free = [None] * 8

    def keep(self, name, shape, dtype):
        size = math.prod(shape[1:]) * (1 if dtype == U8 else 4)
        t = self.nc.alloc_sbuf_tensor_at(name, shape, dtype, offset=self.small)
        self.small += -(-size // 32) * 32
        return t

    def c(self, which):
        return self.const[:, which, :]


    def dense(self, name, loads, rhs, evacuate, per=None, ready=None, gate=None):
        phase = PLAN[self.phase]
        assert phase[0] == name, (phase[0], name)
        _, count, nk, tiles = phase
        own = words(phase)
        last = self.phase + 1 == len(PLAN)
        after = own if last else words(PLAN[self.phase + 1])
        self.phase += 1
        base = {self.c_mm: 2, self.c_ev: 2, self.c_hi: 1, self.c_lo: 1}
        both = {c: 2 * n for c, n in base.items()}
        both.update({self.c_raw[0]: 32, self.c_raw[1]: 32})
        for c, n in (per or {}).items():
            both[c] = both.get(c, 0) + 2 * n

        def one(j, first=False, final=False):
            f, slot = self.flow, self.unit % 2
            for view, source in loads(j):
                sp = self.sp.after(f.at(self.c_lo, 1))
                self.sp.did(sp.dma_start(view(self.raw[slot]), source), self.c_raw[slot], 16)
            if not final:
                a = self.a.after(f.at(self.c_raw[1 - slot], -32), f.at(self.c_mm))
                n = max(own, after)
                self.a.did(a.activation(self.whi[1 - slot][:, 0:n], self.raw[1 - slot][:, 0:n], ACT.Copy), self.c_hi)
            g = self.g.after(f.at(self.c_hi, 0 if final else 1))
            self.g.did(g.tensor_tensor(self.wlo[slot][:, 0:own], self.raw[slot][:, 0:own],
                                       self.whi[slot][:, 0:own].bitcast(F32), ALU.subtract), self.c_lo)
            self.pe.after(f.at(self.c_lo), f.at(self.c_ev, 2))
            if tiles == 0:
                gate(slot)
                self.unit += 1
                return
            w = tiles * P

            def chunk(t, k):
                hi = self.whi[slot][:, k * w + t * P:k * w + t * P + P]
                lo = self.wlo[slot][:, k * w + t * P:k * w + t * P + P]
                bank = self.bank[2 * slot + t][:]
                xh, xl = rhs(k)
                self.nc.tensor.matmul(bank, hi, xh, start=k == 0, stop=False)
                self.nc.tensor.matmul(bank, hi, xl, start=False, stop=False)
                mm = self.nc.tensor.matmul(bank, lo, xh, start=False, stop=k == nk - 1)
                if k == nk - 1 or (tiles == 1 and k == nk // 2 - 1):
                    return self.pe.did(mm, self.c_mm)

            marks = [None] * tiles
            if first and ready is not None:
                for k in range(nk):
                    self.pe.after(*ready(k))
                    for t in range(tiles):
                        marks[t] = chunk(t, k)
            else:
                for t in range(tiles):
                    for k in range(nk):
                        marks[t] = chunk(t, k)
            for t in range(tiles):
                evacuate(j, t, self.bank[2 * slot + t], marks[t])
            self.unit += 1

        j = 0
        if ready is not None or count < 3:
            one(0, first=True, final=last and count == 1)
            j = 1
        pairs = (count - j - (1 if last else 0)) // 2
        if pairs == 1 or count <= 4:
            pairs = 0
        if pairs:
            with self.flow.turns(pairs, both) as i:
                one(i * 2 + j)
                one(i * 2 + (j + 1))
            j += 2 * pairs
        while j < count:
            one(j, final=last and j == count - 1)
            j += 1


    def square(self, src, mark):
        f, sq = self.flow, self.tb[1]
        m = self.a.did(self.a.after(mark, f.at(self.c_dve)).activation(sq[:], src, ACT.Square))
        v = self.v.after(m, f.at(self.c_dve))
        return self.v.did(v.tensor_tensor(self.sqacc[:], self.sqacc[:], sq[:], ALU.add))

    def clear_sum(self):
        self.v.did(self.v.after(self.flow.at(self.c_pe)).memset(self.sqacc[:], 0.0))

    def split(self, src, gain, hi, lo, mark, wait=()):
        a = self.a.after(mark, *wait)
        m = self.a.did(a.activation(hi, src, ACT.Copy, scale=gain) if gain is not None
                       else a.activation(hi, src, ACT.Copy))
        v = self.v.after(m, mark, *wait)
        if gain is not None:
            i = v.scalar_tensor_tensor(lo, src, gain, hi.bitcast(F32), ALU.mult, ALU.subtract)
        else:
            i = v.tensor_tensor(lo, src, hi.bitcast(F32), ALU.subtract)
        return self.v.did(i)

    def finish_norm(self, mark):
        nc, f = self.nc, self.flow
        col, bc = self.bank[6], self.bank[7]
        self.pe.after(mark, self.free[6], self.free[7])
        for b in range(NB):
            mm = nc.tensor.matmul(col[:, b:b + 1], self.sqacc[:, b * P:b * P + P], self.ones[:, 0:1],
                                  start=b == 0, stop=b == NB - 1, skip_group_check=True)
        m = self.pe.did(mm)
        t = self.tiny
        m = self.v.did(self.v.after(m).tensor_scalar(t[:, 0:4], col[:, 0:4], 1.0 / D, EPS, ALU.mult, ALU.add))
        m = self.a.did(self.a.after(m).activation(t[:, 4:8], t[:, 0:4], ACT.Sqrt))
        m = self.v.did(self.v.after(m).reciprocal(t[:, 8:12], t[:, 4:8]))
        self.v.after(m, f.at(self.c_act))
        diag = self.ta[0]
        for b in range(NB):
            i = self.v.queue.tensor_scalar(diag[:, b * P:b * P + P], self.c(C_IDENT), t[:, 8 + b:9 + b], None, ALU.mult)
        m = self.v.did(i)
        self.pe.after(m)
        for b in range(NB):
            mm = nc.tensor.matmul(bc[:, b * P:b * P + P], self.ones[:], diag[:, b * P:b * P + P],
                                  start=b == 0, stop=b == NB - 1, skip_group_check=True)
        m = self.pe.did(mm)
        m = self.v.did(self.v.after(m).tensor_copy(self.rs[:], bc[:]))
        self.free[6] = self.free[7] = m
        return m


    def halves(self, weights, nk, w, row=0):
        def loads(col):
            h = nk // 2
            out = []
            for s in range(2):
                rows = weights[row + s * h * P:row + (s + 1) * h * P, :].rearrange("(k p) n -> p k n", p=P)
                cols = rows[:, :, bass.ds(col, w)] if not isinstance(col, int) else rows[:, :, col:col + w]
                out.append((lambda raw, s=s: raw[:, s * h * w:(s + 1) * h * w].rearrange("p (k n) -> p k n", n=w), cols))
            return out
        return loads

    def operand(self, hi, lo, first=0):
        return lambda k: (hi[:, first + k, :], lo[:, first + k, :])

    def to_residual(self, gain, last=True, tiles=2):
        def evacuate(j, t, bank, mark):
            f = self.flow
            jj = j * tiles + t
            x = tile(self.x, jj)
            v = self.v.after(mark, f.at(self.c_act), f.at(self.c_dve))
            m = self.v.did(v.tensor_tensor(x, bank[:], x, ALU.add), self.c_ev, 3 - tiles)
            if last:
                self.square(x, m)
                self.split(x, self.gain_col(gain, jj), tile(self.xh, jj), tile(self.xl, jj), m)
        n = tiles if last else 0
        return evacuate, {self.c_dve: 2 * n, self.c_act: 2 * n}

    def gain_col(self, row, j):
        if isinstance(j, int):
            return self.cols[:, row + j:row + j + 1]
        return self.cols[:, bass.ds(j + row, 1)]

    def scaled(self, dst, first=0):
        def evacuate(j, t, bank, mark):
            v = self.v.after(mark, self.rs_made, self.dst_free)
            self.v.did(v.tensor_tensor(tile(dst, j * 2 + (t + first)), bank[:], self.rs[:], ALU.mult), self.c_ev)
        return evacuate, {}

    def relu_squared(self, j, t, bank, mark):
        f, r, s = self.flow, self.ta[t], self.tb[t]
        v = self.v.after(mark, self.rs_made, f.at(self.c_act))
        m = self.v.did(v.scalar_tensor_tensor(r[:], bank[:], 0.0, self.rs[:], ALU.max, ALU.mult), self.c_ev)
        m = self.a.did(self.a.after(m, f.at(self.c_dve)).activation(s[:], r[:], ACT.Square))
        self.split(s[:], None, tile(self.ah, j * 2 + t), tile(self.al, j * 2 + t), m)

    def swiglu(self, j, t, bank, mark):
        f, r = self.flow, self.ta[t]
        v = self.v.after(mark, self.rs_made, f.at(self.c_act), f.at(self.c_dve))
        m = self.v.did(v.tensor_tensor(r[:], bank[:], self.rs[:], ALU.mult), self.c_ev)
        if t == 0:
            self.silu_made = self.a.did(self.a.after(m, f.at(self.c_dve)).activation(self.tb[0][:], r[:], ACT.Silu))
        else:
            m = self.v.did(self.v.after(m, self.silu_made).tensor_tensor(r[:], r[:], self.tb[0][:], ALU.mult))
            self.split(r[:], None, tile(self.ah, j), tile(self.al2, j), m)

    def to_f(self, add, last, tiles):
        def evacuate(j, t, bank, mark):
            f = self.flow
            dst = tile(self.f, j * tiles + t)
            v = self.v.after(mark, f.at(self.c_act), f.at(self.c_dve))
            i = v.tensor_tensor(dst, bank[:], dst, ALU.add) if add else v.tensor_copy(dst, bank[:])
            m = self.v.did(i, self.c_ev, 3 - tiles)
            if last:
                self.square(dst, m)
        n = tiles if last else 0
        return evacuate, {self.c_dve: n, self.c_act: n}


    def load_constants(self):
        nc, d = self.nc, self.dram
        sp, f = self.sp, self.flow
        rows = self.u[:, 26, 0:2 * P].rearrange("p (a n) -> p a n", a=2)

        def load(dst, src):
            sp.did(nc.sync.dma_start(dst, src), self.c_load, 16)
        load(self.const[:].rearrange("p a b -> p (a b)"), d["const"])
        load(self.sel[:].rearrange("p a b -> p (a b)"), d["sel"])
        level = self.u[:, 24:26, :].rearrange("p a t -> p (a t)")[:, 0:len(LEVELS) * P]
        load(level, d["level"])
        load(self.freq[:], d["freq"])
        long = lambda a: a.rearrange("l (c p) -> (l c) p", p=P)
        for at, src in ((R_NORM1, long(d["norm1_g"])), (R_NORM2, long(d["norm2_g"])),
                        (R_GAIN2, d["norm_gain_2"].rearrange("l g (c p) -> (l g c) p", p=P))):
            load(rows[at:at + src.shape[0], 0, :], src)
        second = ((R_KV, d["kv_norm_gain_2"].rearrange("(c p) -> c p", p=P)), (R_POOL, long(d["pool_scale_2"])),
                  (R_CONV, d["mlstm_conv_w"].rearrange("l k (c p) -> (l k c) p", p=P)),
                  (R_LB, long(d["hgrn_lb_param"])), (R_SUB, d["diff_subln_g"]))
        for at, src in second:
            load(rows[at - P:at - P + src.shape[0], 1, :], src)
        for at, name in ((R_MN, "mlstm_norm_g"), (R_QN, "diff_q_norm_g"), (R_KN, "diff_k_norm_g"), (R_HN, "hgrn_norm_g")):
            for h in range(2):
                load(rows[at - P:at - P + 2, 1, h * HD:h * HD + HD], d[name])
        with nc.allow_non_contiguous_dma(reason="sixteen numbers"):
            load(self.gate_b[:].rearrange("h (a b) -> h a b", a=1), d["mlstm_gate_b"].rearrange("l g (h a) -> h a (l g)", a=1))
        self.v.did(nc.vector.memset(self.ones[:], 1.0))
        m = f.at(self.c_dve)
        self.pe.after(m, f.at(self.c_load))
        bank = self.bank[5]
        nc.tensor.transpose(bank[:, 0:P], rows[:, 0, :], self.c(C_IDENT))
        n = N_ROWS - P
        t = self.pe.did(nc.tensor.transpose(bank[:, P:P + n], rows[0:n, 1, :], self.const[0:n, C_IDENT, 0:n]))
        m = self.v.did(self.v.after(t).tensor_copy(self.cols[:], bank[:, 0:N_ROWS]))
        self.v.queue.tensor_copy(self.level[:].rearrange("p a b -> p (a b)"), level)
        self.v.after(m)
        for l in range(DEPTH):
            for g in (1, 5):
                r = R_GAIN2 + (l * 6 + g) * KC
                nc.vector.tensor_scalar(self.cols[:, r:r + KC], self.cols[:, r:r + KC], 0.5, None, ALU.mult)
        self.free[5] = self.v.did(nc.vector.tensor_scalar(self.cols[:, R_QN:R_QN + 2], self.cols[:, R_QN:R_QN + 2],
                                                          HD ** -0.5, None, ALU.mult))

    def load_x(self):
        nc, f = self.nc, self.flow
        xt = self.u[:, 0:8, :].rearrange("p (b h) t -> p b (h t)", b=NB)
        m = self.sp.did(nc.sync.dma_start(xt, self.dram["x"][0].rearrange("(b p) d -> p b d", p=P)), self.c_spill, 16)
        self.clear_sum()
        self.pe.after(m)
        for j in range(KC):
            bank = self.bank[4 + j % 2]
            self.pe.after(self.free[4 + j % 2])
            for b in range(NB):
                mm = nc.tensor.transpose(bank[:, b * P:b * P + P], xt[:, b, j * P:j * P + P], self.c(C_IDENT))
            m = self.pe.did(mm)
            x = self.x[:, j, :]
            m = self.free[4 + j % 2] = self.v.did(self.v.after(m).tensor_copy(x, bank[:]))
            self.square(x, m)
            self.split(x, self.gain_col(R_NORM1, j), self.xh[:, j, :], self.xl[:, j, :], m)
        self.rs_made = self.finish_norm(f.at(self.c_dve))

    def store_x(self):
        nc = self.nc
        out = self.u[:, 0:8, :].rearrange("p (b h) t -> p b (h t)", b=NB)
        for j in range(KC):
            bank = self.bank[4 + j % 2]
            self.pe.after(self.x_made[j], self.free[4 + j % 2])
            for b in range(NB):
                mm = nc.tensor.transpose(bank[:, b * P:b * P + P], self.x[:, j, b * P:b * P + P], self.c(C_IDENT))
            m = self.pe.did(mm)
            m = self.free[4 + j % 2] = self.a.did(self.a.after(m).activation(
                out[:, :, j * P:j * P + P], bank[:].rearrange("p (b t) -> p b t", b=NB), ACT.Copy))
            sp = self.sp.after(m)
            m = self.sp.did(sp.dma_start(self.dram["out"][0].rearrange("(b p) d -> p b d", p=P)[:, :, j * P:j * P + P],
                                         out[:, :, j * P:j * P + P]), self.c_out, 16)
        self.sp.after(m)

    def post_norm(self, gain, next_gain):
        f = self.flow
        rs = self.finish_norm(f.at(self.c_dve))
        self.clear_sum()
        self.x_made = []
        for j in range(KC):
            t, x = self.ta[j % 2], self.x[:, j, :]
            v = self.v.after(rs, f.at(self.c_act))
            m = self.v.did(v.scalar_tensor_tensor(t[:], self.f[:, j, :], self.gain_col(gain, j), self.rs[:], ALU.mult, ALU.mult))
            m = self.v.did(self.v.after(m).tensor_tensor(x, x, t[:], ALU.add))
            self.x_made.append(m)
            if next_gain is not None:
                self.split_made[j] = self.split(x, self.gain_col(next_gain, j), self.xh[:, j, :], self.xl[:, j, :], m)
                self.square(x, m)
        if next_gain is not None:
            self.rs_made = self.finish_norm(f.at(self.c_dve))

    def relu_ffn(self, l, next_gain):
        d, f = self.dram, self.flow
        first = 0
        for g, n in enumerate(F1_GROUPS):
            up = self.halves(d["w_up"][l], KC, 2 * P)
            self.dense(f"up{l}{g}", lambda j: up(j * (2 * P) + first * P), self.operand(self.xh, self.xl),
                       self.relu_squared, {self.c_act: 4, self.c_dve: 2})
            last = g == len(F1_GROUPS) - 1
            down = self.halves(d["w_down"][l], n, P, first * P)
            if last:
                self.clear_sum()
            ev, per = self.to_residual(next_gain, last, 1)
            made = f.at(self.c_dve)
            self.dense(f"down{l}{g}", lambda j: down(j * P), self.operand(self.ah, self.al), ev, per,
                       ready=lambda k: [made])
            first += n
        self.rs_made = self.finish_norm(f.at(self.c_dve))

    def swiglu_ffn(self, name, l, i, gain, next_gain):
        d, f = self.dram, self.flow
        wg, wu, wd = d["ffn_w_gate_2"][l, i], d["ffn_w_up_2"][l, i], d["ffn_w_down_2"][l, i]
        first = 0
        for g, n in enumerate(F2_GROUPS):
            def loads(j):
                out = []
                for s, w in enumerate((wg, wu)):
                    col = j * P + first * P
                    rows = w.rearrange("(k p) n -> p k n", p=P)
                    cols = rows[:, :, col:col + P] if isinstance(col, int) else rows[:, :, bass.ds(col, P)]
                    out.append((lambda raw, s=s: raw[:].rearrange("p (k s n) -> p k s n", s=2, n=P)[:, :, s, :], cols))
                return out
            ready = None
            if g == 0:
                made = list(self.split_made)
                ready = lambda k: [made[k]]
            self.dense(f"gateup{name}{g}", loads, self.operand(self.xh, self.xl), self.swiglu,
                       {self.c_act: 2, self.c_dve: 2}, ready=ready)
            last = g == len(F2_GROUPS) - 1
            down = self.halves(wd, n, P, first * P)
            if last:
                self.clear_sum()
            ev, per = self.to_f(g > 0, last, 1)
            made2 = f.at(self.c_dve)
            self.dense(f"back{name}{g}", lambda j: down(j * P), self.operand(self.ah, self.al2), ev, per,
                       ready=lambda k: [made2])
            first += n
        self.post_norm(gain, next_gain)

    def pool_mixer(self):
        d, f, nc = self.dram, self.flow, self.nc
        made = list(self.split_made)
        w_in = self.halves(d["pool_w_in_2"][0], KC, 2 * P)
        self.dst_free = None
        inv = self.ta[0]
        self.pooled = []

        ev, _ = self.scaled(self.u)

        def evacuate(j, t, bank, mark):
            ev(j, t, bank, mark)
            u, s = self.u[:, 2 * j + t, :], [self.u[:, 8 + 2 * t, :], self.u[:, 9 + 2 * t, :]]
            v, src = self.v, u
            m = f.at(self.c_ev)
            w = 1
            n = 0
            while w < POOL_WINDOWS[j]:
                dst = s[n % 2]
                v.after(m)
                nc.vector.tensor_copy(dst[:, 0:w], src[:, 0:w])
                m = v.did(nc.vector.tensor_tensor(dst[:, w:T], src[:, w:T], src[:, 0:T - w], ALU.add))
                src = dst
                w *= 2
                n += 1
            dst = s[n % 2]
            m = v.did(v.after(m, self.inv_loaded[j]).tensor_tensor(dst, src, self.inv[:, j, :], ALU.mult))
            m = v.did(v.after(m, f.at(self.c_act)).tensor_tensor(dst, dst, u, ALU.subtract))
            self.pooled.append(self.split(dst, None, self.mh[:, 2 * j + t, :], self.ml[:, 2 * j + t, :], m))
        self.inv = self.u[:, 14:18, :]
        self.inv_loaded = []
        for g in range(4):
            a = self.a.after(f.at(self.c_dve))
            src = d["inv_count"][g:g + 1, :].to_broadcast([P, T])
            self.inv_loaded.append(self.a.did(a.dma_start(self.inv[:, g, :], src), self.c_spill, 16))
        self.inv_loaded = [self.inv_loaded[-1]] * 4
        self.dense("pool_in", lambda j: w_in(j * 2 * P), self.operand(self.xh, self.xl), evacuate,
                   ready=lambda k: [made[k]])
        wg = d["pool_w_group_2"][0]
        grouped = []

        def ev_group(j, t, bank, mark):
            jj = 2 * j + t
            r = self.ta[t]
            v = self.v.after(mark, f.at(self.c_act), f.at(self.c_dve))
            m = self.v.did(v.tensor_scalar(r[:], bank[:], self.gain_col(R_POOL, jj), None, ALU.mult), self.c_ev)
            grouped.append(self.split(r[:], None, self.xh[:, jj, :], self.xl[:, jj, :], m))
        pooled = self.pooled
        jnow = [0]

        def loads_group(j):
            jnow[0] = j
            return self.halves(wg[j], 2, 2 * P)(0)
        self.dense("pool_group", loads_group, lambda k: (self.mh[:, 2 * jnow[0] + k, :], self.ml[:, 2 * jnow[0] + k, :]),
                   ev_group, ready=lambda k: [pooled[-1]])
        self.clear_sum()
        w_out = self.halves(d["pool_w_out_2"][0], KC, 2 * P)
        ev, per = self.to_f(False, True, 2)
        self.dense("pool_out", lambda j: w_out(j * 2 * P), self.operand(self.xh, self.xl), ev, per,
                   ready=lambda k: [grouped[k]])

    def keys_and_values(self):
        d, f = self.dram, self.flow
        made = list(self.split_made)
        self.dst_free = None
        for n, name in enumerate(("k", "v")):
            w = self.halves(d[f"w_{name}_2"], KC, 2 * P)
            ev, per = self.scaled(self.qkv, 12 * n)
            self.dense(name, lambda j: w(j * 2 * P), self.operand(self.xh, self.xl), ev, per,
                       ready=(lambda k: [made[k]]) if n == 0 else None)
        sp = self.sp.after(f.at(self.c_ev))
        self.spilled = self.sp.did(sp.dma_start(d["kv"].rearrange("j p t -> p j t"), self.qkv[:, 0:24, :]), self.c_spill, 16)


    def act(self, out, in_, fn, *marks, **kw):
        return self.a.did(self.a.after(*marks).activation(out, in_, fn, **kw))

    def tt(self, out, a, b, op, *marks):
        return self.v.did(self.v.after(*marks).tensor_tensor(out, a, b, op))

    def ts(self, out, a, s1, s2, op0, op1, *marks):
        v = self.v.after(*marks)
        return self.v.did(v.tensor_scalar(out, a, s1, s2, op0, op1) if op1 is not None
                          else v.tensor_scalar(out, a, s1, None, op0))

    def stt(self, out, a, s, b, op0, op1, *marks):
        return self.v.did(self.v.after(*marks).scalar_tensor_tensor(out, a, s, b, op0, op1))

    def mm(self, out, lhsT, rhs, start=True, stop=True):
        return self.nc.tensor.matmul(out, lhsT, rhs, start=start, stop=stop, skip_group_check=True)

    def tokens_first(self, src, dst, bank, *marks):
        self.pe.after(*marks, self.free[bank])
        for b in range(NB):
            mm = self.nc.tensor.transpose(self.bank[bank][:, b * P:b * P + P], src[:, b * P:b * P + P], self.c(C_IDENT))
        m = self.pe.did(mm)
        self.free[bank] = m = self.act(dst, self.bank[bank][:], ACT.Copy, m)
        return m

    def head_rstd(self, tiles, rows, bank, *marks):
        n = 2 * len(tiles)
        ps = self.bank[bank]
        w = 16 if n > 4 else 4
        self.pe.after(self.free[bank])
        for j, t in enumerate(tiles):
            sq = (self.ta + self.tb)[j % 4]
            m = self.act(sq[:], t, ACT.Square, *marks, self.flow.at(self.c_pe), self.flow.at(self.c_dve))
            self.pe.after(m)
            m = self.pe.did(self.mm(ps[0:w, :], self.const[:, C_IND, 16 * j:16 * j + w], sq[:], j == 0, j == len(tiles) - 1))
        m = self.free[bank] = self.ts(rows[0:w, :], ps[0:w, :], 1.0 / HD, EPS, ALU.mult, ALU.add, m)
        m = self.act(rows[0:w, :], rows[0:w, :], ACT.Sqrt, m)
        return self.v.did(self.v.after(m).reciprocal(rows[0:w, :], rows[0:w, :]))

    def spread(self, rows, n, j, bank, *marks):
        self.pe.after(*marks, self.free[bank])
        return self.pe.did(self.mm(self.bank[bank][:], self.sel[0:n, j, :], rows[0:n, :]))

    def into_mix(self, j, t, gain, bank, factor, *marks):
        m = self.free[bank] = self.stt(t, t, gain, self.bank[bank][:], ALU.mult, ALU.mult, *marks)
        if factor is not None:
            m = self.tt(t, t, factor, ALU.mult, m)
        self.mix_made[j] = self.split(t, None, self.mh[:, j, :], self.ml[:, j, :], m)


    def mlstm(self, l):
        f, s = self.flow, lambda k: self.scr[:, k, :]
        r0, r1, r2 = [self.spare[0:4, k, :] for k in (13, 14, 15)]
        begin = [f.at(self.c_ev), f.at(self.c_mm), f.at(self.c_dve), f.at(self.c_act)]
        for j in range(4):
            u, t = self.u[:, MQ + j, :], self.ta[j % 2]
            w = lambda k: self.gain_col(R_CONV + (l * 4 + k) * 4, j)
            m = self.ts(t[:], u, w(3), None, ALU.mult, None, f.at(self.c_act), *begin)
            for shift in (1, 2, 3):
                m = self.stt(t[:, shift:], u[:, 0:T - shift], w(3 - shift), t[:, shift:], ALU.mult, ALU.add, m)
            qk_made = self.act(u, t[:], ACT.Silu, m)
        m = self.ts(r0, r0, self.gate_b[0:4, 2 * l:2 * l + 1], None, ALU.add, None, f.at(self.c_dve))
        m = self.ts(r1, r1, self.gate_b[0:4, 2 * l + 1:2 * l + 2], None, ALU.add, None, m)
        m = self.stt(r2, r1, -1.0, r1, ALU.mult, ALU.max, m)
        m = self.act(r2, r2, ACT.Exp, m, scale=-1.0)
        m = self.act(r2, r2, ACT.Ln, m, bias=1.0)
        m = self.stt(r1, r1, 0.0, r2, ALU.min, ALU.subtract, m)
        ones = s(2)[0:4, :]
        o = self.v.did(self.v.after(*begin).memset(ones, 1.0))
        m = self.v.did(self.v.after(m, o).tensor_tensor_scan(r2, ones, r1, 0.0, ALU.mult, ALU.add))
        a_made = self.tt(r0, r0, r2, ALU.subtract, m)
        big_made = self.v.did(self.v.after(a_made).tensor_tensor_scan(r1, r0, r0, 0.0, ALU.max, ALU.max))
        m_made = self.tt(r2, r2, r1, ALU.add, big_made)
        hot = s(3)[0:4, :].rearrange("p (h n) -> p h n", h=4)
        for h in range(4):
            hot_made = self.v.did(self.v.queue.tensor_copy(hot[:, h, :], self.const[0:4, C_IDENT, h:h + 1].to_broadcast([4, P])))
        self.pe.after(a_made, self.free[5])
        for b in range(NB):
            mm = self.nc.tensor.transpose(self.bank[5][:, 4 * b:4 * b + 4], r0[:, b * P:b * P + P], self.const[0:4, C_IDENT, 0:4])
        acol = self.tiny[:, 16:32]
        acol_made = self.free[5] = self.v.did(self.v.after(self.pe.did(mm)).tensor_copy(acol, self.bank[5][:, 0:16]))
        place = [(1, 0), (2, 0), (3, 0), (2, 384)]
        at = [0, 512, 1024, 896]
        h_made = [None, None]
        for i in range(2):
            vt = s(4 + i)
            vt_made = self.tokens_first(self.u[:, MV + i, :], vt, 5, f.at(self.c_ev))
            read = f.at(self.c_dve)
            for e in range(2):
                h = 2 * i + e
                rows = slice(e * HD, e * HD + HD)
                mb = self.bank[4 * (h % 2)]
                wt = self.scr[:, 7 + 3 * (h % 2):10 + 3 * (h % 2), :].rearrange("p a t -> p (a t)")
                self.pe.after(big_made, hot_made, qk_made, self.free[4 * (h % 2)])
                mb_made = self.pe.did(self.mm(mb[:], hot[:, h, :], r1))
                self.pe.after(self.free[1])
                for j in range(NB):
                    bank, col = place[j]
                    mm = self.mm(self.bank[bank][:, col:col + T - j * P], self.u[rows, MK + i, j * P:j * P + P],
                                 self.u[rows, MQ + i, j * P:T], j != 3)
                s_made = self.pe.did(mm)
                md = s(13)
                m = self.tt(md.rearrange("p (b t) -> p b t", b=NB), mb[:].rearrange("p (b t) -> p b t", b=NB),
                            self.const[:, C_LATER:C_LATER + 1, :].to_broadcast([P, NB, P]), ALU.add,
                            mb_made, f.at(self.c_act))
                self.a.after(m, acol_made, f.at(self.c_pe, 0 if h < 2 else 0))
                for j in range(NB):
                    bias = acol[:, 4 * j + h:4 * j + h + 1]
                    i1 = self.a.queue.activation(wt[:, at[j]:at[j] + P], md[:, j * P:j * P + P], ACT.Exp, bias=bias, scale=-1.0)
                    if j < NB - 1:
                        i1 = self.a.queue.activation(wt[:, at[j] + P:at[j] + T - j * P], mb[:, (j + 1) * P:T], ACT.Exp,
                                                     bias=bias, scale=-1.0)
                w_made = self.a.did(i1)
                self.free[4 * (h % 2)] = w_made
                self.v.after(s_made, w_made)
                for bank, lo, n in ((1, 0, 512), (2, 512, 512), (3, 1024, 256)):
                    i2 = self.v.queue.scalar_tensor_tensor(wt[:, lo:lo + n], self.bank[bank][:, 0:n], HD ** -0.5,
                                                           wt[:, lo:lo + n], ALU.mult, ALU.mult)
                m = self.free[1] = self.v.did(i2)
                self.pe.after(m, vt_made, self.free[6], self.free[7])
                for j in range(NB):
                    src = wt[:, at[j]:at[j] + T - j * P]
                    self.mm(self.bank[6][rows, j * P:T], vt[:, j * P + e * HD:j * P + e * HD + HD], src, j == 0, j == 3)
                    mm = self.mm(self.bank[7][rows, j * P:T], self.ones[:, 0:HD], src, j == 0, j == 3)
                nd_made = self.pe.did(mm)
            sp = self.spread(r2, 4, i, 5, m_made)
            enb, den = s(0), s(1)
            m = self.free[5] = self.act(enb, self.bank[5][:], ACT.Exp, sp, f.at(self.c_dve), scale=-1.0)
            m = self.free[7] = self.act(den, self.bank[7][:], ACT.Abs, nd_made)
            m = self.tt(den, den, enb, ALU.max, m)
            m = self.v.did(self.v.after(m).reciprocal(den, den))
            h_made[i] = self.free[6] = self.tt(s(14 + i), self.bank[6][:], den, ALU.mult, m)
        rows = s(2)
        m = self.head_rstd([s(14), s(15)], rows, 5, *h_made)
        for i in range(2):
            sg = self.act(self.u[:, MO + i, :], self.u[:, MO + i, :], ACT.Sigmoid, f.at(self.c_ev))
            sp = self.spread(rows, 4, i, 4 * i, m)
            self.into_mix(i, s(14 + i), self.gain_col(R_MN, l), 4 * i, self.u[:, MO + i, :], sp, sg)


    def diff_attention(self, l):
        f, s, d = self.flow, lambda k: self.scr[:, k, :], self.dram
        cos, sin = self.u[:, 2, :], self.u[:, 3, :]
        everything = [f.at(c) for c in (self.c_ev, self.c_mm, self.c_dve, self.c_act, self.c_pe)]
        a = self.a.after(*everything)
        self.a.did(a.dma_start(self.u[:, 2:4, :].rearrange("p a t -> p (a t)"), d["rot"]), self.c_tab, 16)
        lv = self.u[:, 4, 0:4 * HD]
        loaded = self.a.did(a.dma_start(lv, d["diff_lambda"][l:l + 1].rearrange("l a n -> l (a n)").to_broadcast([P, 4 * HD])),
                            self.c_tab, 16)
        lv = lv.rearrange("p (a b n) -> p a b n", a=2, b=2)
        pr = self.u[:, 5, 0:2 * HD].rearrange("p (a n) -> p a n", a=2)
        t = self.tiny
        m = self.tt(pr, lv[:, :, 0, :], lv[:, :, 1, :], ALU.mult, loaded, *everything)
        m = self.v.did(self.v.after(m).tensor_reduce(t[:, 32:34], pr, AX.X, ALU.add))
        m = self.act(t[:, 34:36], t[:, 32:34], ACT.Exp, m)
        m = self.tt(t[:, 36:37], t[:, 35:36], t[:, 34:35], ALU.subtract, m)
        init = 0.8 - 0.6 * math.exp(-0.3 * l)
        lam_made = self.ts(t[:, 37:38], t[:, 36:37], -init, None, ALU.add, None, m)
        rows = s(15)
        rstd = self.head_rstd([self.u[:, AQ + j, :] for j in range(8)], rows, 0, *everything)
        n_it = 0
        o_read = None
        for h in range(4):
            turned = []
            for k, (src, gain) in enumerate(((AQ, R_QN), (AK, R_KN))):
                u = self.u[:, src + h, :]
                sp = self.spread(rows, 16, 4 * k + h, 0, rstd)
                n, t1, t2 = s(6), s(7), self.ta[k]
                r = s(2 * k + h % 2)
                m = self.free[0] = self.stt(n, u, self.gain_col(gain, l), self.bank[0][:], ALU.mult, ALU.mult,
                                            sp, f.at(self.c_pe))
                self.pe.after(m, self.free[1])
                pm = self.pe.did(self.mm(self.bank[1][:], self.c(C_ROT_A), n))
                m1 = self.tt(t1, n, cos, ALU.mult, m, loaded)
                m2 = self.free[1] = self.tt(t2[:], self.bank[1][:], sin, ALU.mult, pm)
                turned.append(self.tt(r, t1, t2[:], ALU.add, m1, m2))
            vt = s(4 + h % 2)
            vt_made = self.tokens_first(self.u[:, AV + h, :], vt, 6, f.at(self.c_pe))
            for qb in range(NB):
                w = (qb + 1) * P
                two = n_it % 2
                n_it += 1
                banks = (2 + 2 * two, 3 + 2 * two)
                self.pe.after(*turned, self.free[banks[0]], self.free[banks[1]])
                for e, bank in enumerate(banks):
                    part = slice(e * HD, e * HD + HD)
                    self.mm(self.bank[bank][:, 0:w], s(0 + h % 2)[part, qb * P:w], s(2 + h % 2)[part, 0:w], True, False)
                    mm = self.mm(self.bank[bank][:, qb * P:w], self.c(C_IDENT), self.c(C_CAUSAL), False, True)
                m = self.pe.did(mm)
                st = self.tiny[:, 40 + 8 * two:48 + 8 * two]
                p = [s(8 + 2 * two), s(9 + 2 * two)]
                self.v.after(m, f.at(self.c_act))
                for e, bank in enumerate(banks):
                    i1 = self.v.queue.tensor_reduce(st[:, e:e + 1], self.bank[bank][:, 0:w], AX.X, ALU.max, negate=True)
                m = self.v.did(i1)
                self.a.after(m, f.at(self.c_pe))
                for e, bank in enumerate(banks):
                    i1 = self.a.queue.activation(p[e][:, 0:w], self.bank[bank][:, 0:w], ACT.Exp, bias=st[:, e:e + 1],
                                                 accum_out=st[:, 2 + e:3 + e])
                    m = self.free[bank] = self.a.did(i1)
                m = self.v.did(self.v.after(m).reciprocal(st[:, 4:6], st[:, 2:4]))
                m2 = self.tt(st[:, 6:7], st[:, 5:6], t[:, 37:38], ALU.mult, m, lam_made)
                m = self.ts(p[0][:, 0:w], p[0][:, 0:w], st[:, 4:5], None, ALU.mult, None, m)
                m = self.stt(p[0][:, 0:w], p[1][:, 0:w], st[:, 6:7], p[0][:, 0:w], ALU.mult, ALU.add, m, m2)
                self.pe.after(m, self.free[6])
                for b in range(qb + 1):
                    mm = self.nc.tensor.transpose(self.bank[6][:, b * P:b * P + P], p[0][:, b * P:b * P + P], self.c(C_IDENT))
                m = self.pe.did(mm)
                at = s(12 + two)
                m = self.free[6] = self.act(at[:, 0:w], self.bank[6][:, 0:w], ACT.Copy, m, f.at(self.c_pe))
                self.pe.after(m, vt_made, o_read)
                for b in range(qb + 1):
                    mm = self.mm(self.bank[7][:, qb * P:w], vt[:, b * P:b * P + P], at[:, b * P:b * P + P],
                                 qb == 0 and b == 0, b == qb)
                o_made = self.pe.did(mm)
            o, sq = self.ta[0], self.tb[0]
            m = self.act(o[:], self.bank[7][:], ACT.Copy, o_made, f.at(self.c_dve))
            m2 = self.act(sq[:], self.bank[7][:], ACT.Square, o_made, f.at(self.c_dve), f.at(self.c_pe))
            o_read = m2
            self.pe.after(m2, self.free[0])
            m3 = self.pe.did(self.mm(self.bank[0][:], self.ones[:], sq[:]))
            r = self.tb[1]
            m3 = self.free[0] = self.ts(r[:], self.bank[0][:], 1.0 / (2 * HD), EPS, ALU.mult, ALU.add, m3, f.at(self.c_act))
            m3 = self.act(r[:], r[:], ACT.Sqrt, m3)
            m3 = self.v.did(self.v.after(m3).reciprocal(r[:], r[:]))
            m3 = self.tt(o[:], o[:], r[:], ALU.mult, m3, m)
            m3 = self.ts(o[:], o[:], self.gain_col(R_SUB, l), 1.0 - init, ALU.mult, ALU.mult, m3)
            self.mix_made[2 + h] = self.split(o[:], None, self.mh[:, 2 + h, :], self.ml[:, 2 + h, :], m3)


    def lower_bounds(self):
        lb, p = self.lb, [self.cols[:, R_LB + 2 * l:R_LB + 2 * l + 2] for l in range(DEPTH)]
        t = self.tiny
        m = self.tt(t[:, 0:2], p[0], p[1], ALU.max, self.flow.at(self.c_dve))
        for l in range(DEPTH):
            m2 = self.tt(t[:, 2 + 2 * l:4 + 2 * l], p[l], t[:, 0:2], ALU.subtract, m)
        m = self.act(t[:, 6:10], t[:, 2:6], ACT.Exp, m2)
        m = self.tt(t[:, 10:12], t[:, 6:8], t[:, 8:10], ALU.add, m)
        m = self.v.did(self.v.after(m).reciprocal(t[:, 12:14], t[:, 10:12]))
        for l in range(DEPTH):
            m2 = self.tt(t[:, 2 + 2 * l:4 + 2 * l], t[:, 6 + 2 * l:8 + 2 * l], t[:, 12:14], ALU.mult, m)
        m = self.tt(lb[:, 0:2], t[:, 2:4], t[:, 2:4], ALU.subtract, m2)
        m = self.tt(t[:, 0:2], t[:, 2:4], t[:, 4:6], ALU.add, m)
        m = self.tt(lb[:, 2:4], t[:, 0:2], t[:, 2:4], ALU.subtract, m)
        self.ts(lb[:, 4:8], lb[:, 0:4], -1.0, 1.0, ALU.mult, ALU.add, m)

    def hgrn(self, l):
        f, s = self.flow, lambda k: self.scr[:, k, :]
        everything = [f.at(c) for c in (self.c_ev, self.c_mm, self.c_dve, self.c_act, self.c_pe)]
        blocks = lambda t: t.rearrange("p (b t) -> p b t", b=NB)
        keep = s(13)
        m = self.v.did(self.v.after(*everything).memset(keep, 1.0))
        keep_made = self.v.did(self.v.after(m).memset(blocks(keep)[:, :, 0:1], 0.0))
        for i in range(2):
            q, k, fp = self.u[:, HQ + i, :], self.u[:, HF + i, :], s(1)
            lb, one_lb = self.lb[:, 2 * l + i:2 * l + i + 1], self.lb[:, 4 + 2 * l + i:5 + 2 * l + i]
            q_made = self.act(q, q, ACT.Silu, *everything)
            m = self.act(fp, k, ACT.Sigmoid, f.at(self.c_dve))
            mk = self.act(k, k, ACT.Sigmoid, m, scale=-1.0)
            m = self.ts(fp, fp, one_lb, lb, ALU.mult, ALU.add, m)
            k_made = self.ts(k, k, one_lb, None, ALU.mult, None, mk)
            m = self.act(fp, fp, ACT.Ln, m)
            b = s(0)
            b_made = self.v.did(self.v.after(m, keep_made).tensor_tensor_scan(b, keep, fp, 0.0, ALU.mult, ALU.add))
            vt = s(6)
            vt_made = self.tokens_first(self.u[:, HI + i, :], vt, 4, f.at(self.c_pe))
            at = [s(4), s(5)]
            self.pe.after(q_made, k_made, self.free[0], self.free[1])
            for e in range(2):
                for c in range(NB):
                    part, blk = slice(e * HD, e * HD + HD), slice(c * P, c * P + P)
                    mm = self.mm(self.bank[e][:, blk], k[part, blk], q[part, blk], c == 0, c == NB - 1)
            m = self.pe.did(mm)
            for e in range(2):
                m2 = self.free[e] = self.tt(blocks(at[e]), blocks(self.bank[e][:]),
                                            self.const[:, C_IDENT:C_IDENT + 1, :].to_broadcast([P, NB, P]), ALU.mult, m)
            at_made = m2
            dd = s(1)
            for n, half in enumerate(LEVELS):
                cut = lambda t: t.rearrange("p (m h b) -> p m h b", h=2, b=half)
                r = cut(b)[:, :, 0, half - 1:half].to_broadcast([P, T // (2 * half), half])
                self.v.after(b_made, f.at(self.c_dve))
                self.v.queue.tensor_tensor(cut(dd)[:, :, 1, :], cut(b)[:, :, 1, :], r, ALU.subtract)
                m = self.tt(cut(dd)[:, :, 0, :], r, cut(b)[:, :, 0, :], ALU.subtract)
                m = self.act(dd, dd, ACT.Exp, m)
                z = s(2 + n % 2)
                self.v.after(m, q_made, k_made, self.z_read[n % 2])
                self.v.queue.tensor_tensor(cut(z)[:, :, 1, :], cut(q)[:, :, 1, :], cut(dd)[:, :, 1, :], ALU.mult)
                m = self.tt(cut(z)[:, :, 0, :], cut(k)[:, :, 0, :], cut(dd)[:, :, 0, :], ALU.mult)
                pair = 2 * (n % 2)
                self.pe.after(m, self.free[pair], self.free[pair + 1])
                for e in range(2):
                    for c in range(NB):
                        part, blk = slice(e * HD, e * HD + HD), slice(c * P, c * P + P)
                        mm = self.mm(self.bank[pair + e][:, blk], z[part, blk], z[part, blk], c == 0, c == NB - 1)
                m = self.z_read[n % 2] = self.pe.did(mm)
                for e in range(2):
                    mask = self.level[:, n:n + 1, :].to_broadcast([P, NB, P])
                    v = self.v.after(m, at_made)
                    at_made = self.free[pair + e] = self.v.did(v.copy_predicated(blocks(at[e]), mask, blocks(self.bank[pair + e][:])))
            qs, ks, kt, st = s(8), s(9), s(7), s(10)
            m = self.act(qs, b, ACT.Exp, b_made, f.at(self.c_pe), f.at(self.c_dve))
            qs_made = self.tt(qs, qs, q, ALU.mult, m)
            last = blocks(b)[:, :, P - 1:P]
            m = self.tt(blocks(ks), last.to_broadcast([P, NB, P]), blocks(b), ALU.subtract, f.at(self.c_pe))
            m = self.act(ks, ks, ACT.Exp, m)
            m = self.tt(ks, ks, k, ALU.mult, m)
            kt_made = self.tokens_first(ks, kt, 4, m)
            dec = self.tiny[:, 16 + 4 * i:20 + 4 * i]
            dec_made = self.act(dec.rearrange("p (a b) -> p a b", b=1), last, ACT.Exp, b_made)
            self.pe.after(at_made, vt_made, self.free[6])
            for e in range(2):
                for c in range(NB):
                    blk = slice(c * P, c * P + P)
                    mm = self.mm(self.bank[6][e * HD:e * HD + HD, blk], vt[:, c * P + e * HD:c * P + e * HD + HD], at[e][:, blk],
                                 c == 0, False)
            for c in range(1, NB):
                blk, before = slice(c * P, c * P + P), slice((c - 1) * P, c * P)
                self.pe.after(kt_made, self.free[7])
                m = self.pe.did(self.mm(self.bank[7][:, 0:P], kt[:, before], vt[:, before]))
                new = st[:, P:2 * P]
                m = self.free[7] = self.tt(new, self.bank[7][:, 0:P], self.c(C_BLOCK), ALU.mult, m, f.at(self.c_dve))
                if c == 1:
                    m = self.v.did(self.v.after(m, f.at(self.c_pe)).tensor_copy(st[:, 0:P], new))
                else:
                    m = self.stt(st[:, 0:P], st[:, 0:P], dec[:, c - 1:c], new, ALU.mult, ALU.add, m, dec_made, f.at(self.c_pe))
                self.pe.after(m, qs_made)
                mm = self.pe.did(self.mm(self.bank[6][:, blk], st[:, 0:P], qs[:, blk], False, c == NB - 1))
            self.h_made[i] = self.free[6] = self.v.did(self.v.after(mm).tensor_copy(s(11 + i), self.bank[6][:]))
        rows = s(14)
        m = self.head_rstd([s(11), s(12)], rows, 5, *self.h_made)
        for i in range(2):
            g = self.u[:, HG + i, :]
            sg = self.act(g, g, ACT.Silu, f.at(self.c_ev))
            sp = self.spread(rows, 4, i, 4 + i, m)
            self.into_mix(6 + i, s(11 + i), self.gain_col(R_HN, l), 4 + i, g, sp, sg)

    def mixers(self, l):
        self.mix_made = [None] * KC
        self.h_made = [None] * 2
        self.z_read = [None] * 2
        every = self.flow.at(self.c_ev)
        self.free = [every] * 8
        self.mlstm(l)
        self.diff_attention(l)
        self.hgrn(l)



    def rotary_tables(self, cos, sin, t, *marks):
        pos = self.ta[0][:].bitcast(I32)
        a = self.a.after(*marks)
        loaded = self.a.did(a.dma_start(pos, self.dram["positions_2"].to_broadcast([P, T])), self.c_tab, 16)
        ang = self.ta[1]
        m = self.v.did(self.v.after(loaded, *marks).tensor_copy(t, pos))
        ang_made = self.ts(ang[:], t, self.freq[:, 0:1], None, ALU.mult, None, m)
        whole = 12582912.0
        c1, c2 = 6.28125, float(np.float32(round((TWO_PI - 6.28125) * 2 ** 22) / 2 ** 22))
        parts = (c1, c2, TWO_PI - c1 - c2)
        made = []
        for dst, turn, shift in ((sin, 0.0, 0.0), (cos, 0.25, math.pi / 2)):
            m = self.ts(t, ang[:], 1 / TWO_PI, turn, ALU.mult, ALU.add, ang_made, self.flow.at(self.c_dve))
            m = self.ts(t, t, whole, whole, ALU.add, ALU.subtract, m)
            src = ang[:]
            for c in parts:
                m = self.stt(dst, t, -c, src, ALU.mult, ALU.add, m)
                src = dst
            if shift:
                m = self.ts(dst, dst, shift, None, ALU.add, None, m)
            m = self.ts(dst, dst, 3.1415925, -3.1415925, ALU.min, ALU.max, m)
            made.append(self.act(dst, dst, ACT.Sin, m))
        return made[-1]

    def attention_b(self):
        f, s, d, nc = self.flow, lambda k: self.scr[:, k, :], self.dram, self.nc
        everything = [f.at(c) for c in (self.c_ev, self.c_mm, self.c_dve, self.c_act, self.c_pe)]
        self.free = [f.at(self.c_ev)] * 8
        cos, sin = s(0), s(1)
        tables = self.rotary_tables(cos, sin, s(2), *everything)
        stats = s(3)[:, 0:192].rearrange("p (k g b h) -> p k g b h", k=2, g=3, b=4)
        stat_made = None
        n_s = 0
        weighed = []
        for i in range(4):
            for g in range(3):
                q, k, v = [self.qkv[:, 12 * n + 4 * g + i, :] for n in range(3)]
                block = (lambda t, b: t[:, b * P:b * P + P]) if g == 0 else (lambda t, b: t[:, b::4])
                turned = []
                for n, u in enumerate((q, k)):
                    self.pe.after(self.free[0], f.at(self.c_ev), self.kv_loaded)
                    m = self.pe.did(self.mm(self.bank[0][:], self.c(C_ROT_B), u))
                    t1, t2 = s(4 + n), s(6 + n)
                    scale = HD ** -0.5 if n == 0 else 1.0
                    m1 = self.stt(t1, u, scale, cos, ALU.mult, ALU.mult, tables, f.at(self.c_pe))
                    m2 = self.free[0] = self.stt(t2, self.bank[0][:], scale, sin, ALU.mult, ALU.mult, m)
                    turned.append(self.tt(u, t1, t2, ALU.add, m1, m2))
                vt = s(8 + g % 2)
                self.pe.after(self.free[1], self.kv_loaded)
                for b in range(NB):
                    mm = nc.tensor.transpose(self.bank[1][:, b * P:b * P + P], block(v, b), self.c(C_IDENT))
                m = self.pe.did(mm)
                vt_made = self.free[1] = self.act(vt, self.bank[1][:], ACT.Copy, m, f.at(self.c_pe))
                if g == 0:
                    pairs = [(0, 0, C_CAUSAL)] + [x for b in range(1, NB) for x in ((b, b - 1, C_PAST), (b, b, C_CAUSAL))]
                else:
                    pairs = [(b, b, C_CAUSAL if g == 1 else C_CAUSAL4) for b in range(NB)]
                for e in range(2):
                    part, h = slice(e * HD, e * HD + HD), 2 * i + e
                    two = n_s % 2
                    n_s += 1
                    banks = (2 + 2 * two, 3 + 2 * two)
                    spots, col = [], 0
                    for n, (qb, kb, mask) in enumerate(pairs):
                        if g == 0 and n == 3:
                            col = T
                        spots.append((banks[col // T], col % T))
                        col += P
                    self.pe.after(*turned, self.free[banks[0]], self.free[banks[1]])
                    for n, (qb, kb, mask) in enumerate(pairs):
                        bank, at = spots[n]
                        dst = self.bank[bank][:, at:at + P]
                        self.mm(dst, block(q, qb)[part], block(k, kb)[part], at == 0, False)
                        mm = self.mm(dst, self.c(C_IDENT), self.c(mask), False, n == len(pairs) - 1)
                    m = self.pe.did(mm)
                    spans = []
                    for qb in range(NB):
                        mine = [n for n in range(len(pairs)) if pairs[n][0] == qb]
                        spans.append((*spots[mine[0]], P * len(mine)))
                    self.v.after(m)
                    for qb, (bank, at, w) in enumerate(spans):
                        i1 = self.v.queue.tensor_reduce(stats[:, 0, g, qb, h:h + 1], self.bank[bank][:, at:at + w], AX.X,
                                                        ALU.max, negate=True)
                    m = self.v.did(i1)
                    p = self.scr[:, 10 + 2 * two:12 + 2 * two, :].rearrange("p a t -> p (a t)")
                    self.a.after(m, f.at(self.c_pe))
                    col, cols = 0, {}
                    for qb, (bank, at, w) in enumerate(spans):
                        i1 = self.a.queue.activation(p[:, col:col + w], self.bank[bank][:, at:at + w], ACT.Exp,
                                                     bias=stats[:, 0, g, qb, h:h + 1], accum_out=stats[:, 1, g, qb, h:h + 1])
                        col += w
                    m = self.free[banks[0]] = self.free[banks[1]] = self.a.did(i1)
                    self.pe.after(m, self.free[6])
                    done = 0
                    while done < len(pairs):
                        n = min(4, len(pairs) - done)
                        self.pe.after(self.free[6])
                        for c in range(n):
                            mm = nc.tensor.transpose(self.bank[6][:, c * P:c * P + P], p[:, (done + c) * P:(done + c + 1) * P],
                                                     self.c(C_IDENT))
                        m = self.pe.did(mm)
                        m = self.free[6] = self.act(p[:, done * P:(done + n) * P], self.bank[6][:, 0:n * P], ACT.Copy, m)
                        done += n
                    self.pe.after(m, vt_made, self.free[7])
                    for n, (qb, kb, mask) in enumerate(pairs):
                        mm = self.mm(self.bank[7][part, qb * P:qb * P + P], vt[:, kb * P + e * HD:kb * P + e * HD + HD],
                                     p[:, n * P:n * P + P], n == 0, n == len(pairs) - 1)
                    m = self.pe.did(mm)
                if g == 0:
                    self.free[7] = self.v.did(self.v.after(m).tensor_copy(q, self.bank[7][:]))
                else:
                    self.free[7] = self.v.did(self.v.after(m).tensor_copy(
                        q.rearrange("p (j r) -> p r j", r=4), self.bank[7][:].rearrange("p (r j) -> p r j", r=4)))
        rows = [[s(4 + 3 * k + g)[0:8, :] for g in range(3)] for k in range(2)]
        m = [f.at(self.c_dve), f.at(self.c_act), f.at(self.c_pe)]
        for k in range(2):
            for g in range(3):
                bank = 2 + (3 * k + g) % 2
                self.pe.after(*m, self.free[bank])
                for b in range(NB):
                    mm = nc.tensor.transpose(self.bank[bank][0:8, b * P:b * P + P], stats[:, k, g, b, :], self.c(C_IDENT))
                t = self.pe.did(mm)
                src, dst = self.bank[bank][0:8, :], rows[k][g]
                if g:
                    src, dst = src.rearrange("p (r j) -> p r j", r=4), dst.rearrange("p (j r) -> p r j", r=4)
                row_made = self.free[bank] = self.v.did(self.v.after(t, *m).tensor_copy(dst, src))
        top, z = s(10)[0:8, :], s(11)[0:8, :]
        m = self.tt(top, rows[0][0], rows[0][1], ALU.min, row_made)
        m = self.tt(top, top, rows[0][2], ALU.min, m)
        for g in range(3):
            w, den = rows[0][g], rows[1][g]
            n = self.tt(w, top, w, ALU.subtract, m)
            n = self.act(w, w, ACT.Exp, n)
            if g == 0:
                zm = self.tt(z, w, den, ALU.mult, n)
            else:
                n = self.tt(den, w, den, ALU.mult, n)
                zm = self.tt(z, z, den, ALU.add, n, zm)
        m = self.v.did(self.v.after(zm).reciprocal(z, z))
        for g in range(3):
            w_made = self.tt(rows[0][g], rows[0][g], z, ALU.mult, m)
        self.o_made = []
        for i in range(4):
            t, acc = self.ta[i % 2], self.tb[i % 2]
            for g in range(3):
                sp = self.spread(rows[0][g], 8, i, 2 + (3 * i + g) % 4, w_made)
                bank = 2 + (3 * i + g) % 4
                o = self.qkv[:, 4 * g + i, :]
                if g == 0:
                    m = self.free[bank] = self.tt(acc[:], self.bank[bank][:], o, ALU.mult, sp, f.at(self.c_dve), f.at(self.c_act))
                else:
                    n = self.free[bank] = self.tt(t[:], self.bank[bank][:], o, ALU.mult, sp, f.at(self.c_dve))
                    m = self.tt(acc[:], acc[:], t[:], ALU.add, n)
            self.o_made.append(self.split(acc[:], None, self.oh[:, i, :], self.ol[:, i, :], m))

    def gate_rows(self, l):
        w_in = self.dram["w_in"][l]
        w = HD

        def loads(j):
            out = []
            for s in range(2):
                src = w_in[:, GATES + 4 * s:GATES + 4 * s + 4].rearrange("(k p) n -> p k n", p=P)
                out.append((lambda raw, s=s: raw[:, 0:KC * w].rearrange("p (k n) -> p k n", n=w)[:, :, 32 * s:32 * s + 4], src))
            return out

        def gate(slot):
            bank = self.bank[2 * slot]
            for k in range(KC):
                hi = self.whi[slot][:, k * w:k * w + w]
                lo = self.wlo[slot][:, k * w:k * w + w]
                self.nc.tensor.matmul(bank[0:w, :], hi, self.xh[:, k, :], start=k == 0, stop=False)
                self.nc.tensor.matmul(bank[0:w, :], hi, self.xl[:, k, :], start=False, stop=False)
                mm = self.nc.tensor.matmul(bank[0:w, :], lo, self.xh[:, k, :], start=False, stop=k == KC - 1)
            self.gates_bank, self.gates_mark = bank, self.pe.did(mm, self.c_mm, 2)
            v = self.v.after(self.gates_mark, self.rs_made)
            v.tensor_tensor(self.spare[0:4, 13, :], bank[0:4, :], self.rs[0:4, :], ALU.mult)
            self.v.did(v.tensor_tensor(self.spare[0:4, 14, :], bank[32:36, :], self.rs[0:4, :], ALU.mult), self.c_ev, 2)
        self.dense(f"gates{l}", loads, None, None, gate=gate)

    def block_one(self, l):
        d = self.dram
        w_in = self.halves(d["w_in"][l], KC, 2 * P)
        self.dst_free = None
        ev, per = self.scaled(self.u)
        self.dense(f"in_m{l}", lambda j: w_in(j * (2 * P)), self.operand(self.xh, self.xl), ev, per)
        self.gate_rows(l)
        ev, per = self.scaled(self.u, AQ)
        self.dense(f"in_ah{l}", lambda j: w_in(j * (2 * P) + M_COLS), self.operand(self.xh, self.xl), ev, per)
        self.mixers(l)
        self.clear_sum()
        ev, per = self.to_residual(R_NORM2 + l * KC)
        w_out = self.halves(d["w_out"][l], KC, 2 * P)
        mix = list(self.mix_made)
        self.dense(f"out{l}", lambda j: w_out(j * 2 * P), self.operand(self.mh, self.ml), ev, per,
                   ready=lambda k: [mix[k]])
        self.rs_made = self.finish_norm(self.flow.at(self.c_dve))
        self.relu_ffn(l, R_NORM1 + KC if l == 0 else R_GAIN2)

    def block_two(self):
        d, f = self.dram, self.flow
        self.split_made = [f.at(self.c_dve)] * KC
        gain = lambda l, g: R_GAIN2 + (l * 6 + g) * KC
        self.swiglu_ffn("a", 0, 0, gain(0, 1), gain(0, 2))
        self.pool_mixer()
        self.post_norm(gain(0, 3), gain(0, 4))
        self.swiglu_ffn("b", 0, 1, gain(0, 5), R_KV)
        self.keys_and_values()
        m = f.at(self.c_mm)
        for j in range(KC):
            self.split_made[j] = self.split(self.x[:, j, :], self.gain_col(gain(1, 0), j),
                                            self.xh[:, j, :], self.xl[:, j, :], m)
        self.a.after(self.spilled)
        self.v.after(self.spilled)
        self.swiglu_ffn("c", 1, 0, gain(1, 1), gain(1, 2))
        made = list(self.split_made)
        w = self.halves(d["attn_w_q_2"][0], KC, 2 * P)
        a = self.a.after(f.at(self.c_dve), f.at(self.c_mm), self.spilled)
        self.kv_loaded = self.a.did(a.dma_start(self.qkv[:, 12:36, :], d["kv"].rearrange("j p t -> p j t")), self.c_kv, 16)
        ev, per = self.scaled(self.qkv)
        self.dense("q", lambda j: w(j * 2 * P), self.operand(self.xh, self.xl), ev, per, ready=lambda k: [made[k]])
        self.attention_b()
        w_o = self.halves(d["attn_w_o_2"][0], OW // P, 2 * P)
        ev, per = self.to_f(False, True, 2)
        self.clear_sum()
        o = list(self.o_made)
        self.dense("o", lambda j: w_o(j * 2 * P), self.operand(self.oh, self.ol), ev, per, ready=lambda k: [o[k]])
        self.post_norm(gain(1, 3), gain(1, 4))
        self.swiglu_ffn("d", 1, 1, gain(1, 5), None)

    def run(self):
        self.load_constants()
        self.lower_bounds()
        self.load_x()
        self.a.did(self.a.after(self.flow.at(self.c_raw[0], -32)).activation(self.whi[0][:], self.raw[0][:], ACT.Copy), self.c_hi)
        for l in range(DEPTH):
            self.block_one(l)
        self.block_two()
        self.store_x()


def build(nc, dram):
    Kernel(nc, dram).run()


_INS = ["x", "norm1_g", "w_in", "mlstm_conv_w", "mlstm_gate_b", "mlstm_norm_g", "diff_q_norm_g", "diff_k_norm_g",
        "diff_lambda", "diff_subln_g", "hgrn_lb_param", "hgrn_norm_g", "w_out", "norm2_g", "w_up", "w_down",
        "positions_2", "norm_gain_2", "ffn_w_gate_2", "ffn_w_up_2", "ffn_w_down_2", "pool_w_in_2", "pool_w_group_2",
        "pool_scale_2", "pool_w_out_2", "kv_norm_gain_2", "w_k_2", "w_v_2", "attn_w_q_2", "attn_w_o_2"]


def kernel(**inputs):
    import concourse.bacc as bacc
    from concourse.bass_utils import run_bass_kernel_spmd

    nc = bacc.Bacc("TRN2", target_bir_lowering=False, num_devices=1)
    arrays = {name: np.ascontiguousarray(inputs[name]) for name in _INS}
    arrays.update(zip(("const", "sel", "freq", "rot", "inv_count", "level"), constants()))
    dram = {name: nc.dram_tensor(f"in_{name}", a.shape, mybir.dt.from_np(a.dtype), kind="ExternalInput").ap()
            for name, a in arrays.items()}
    dram["kv"] = nc.dram_tensor("kv", (24, P, T), F32).ap()
    dram["out"] = nc.dram_tensor("out", (1, T, D), F32, kind="ExternalOutput").ap()
    build(nc, dram)
    result = run_bass_kernel_spmd(nc, [{f"in_{name}": a for name, a in arrays.items()}], core_ids=[0])
    return result.results[0]["out"]
```

```python
import math
from contextlib import ExitStack, contextmanager

import numpy as np

import concourse.bass as bass
from concourse import mybir

F32 = mybir.dt.float32
F32R = mybir.dt.float32r
BF16 = mybir.dt.bfloat16
U8 = mybir.dt.uint8
I32 = mybir.dt.int32
ALU = mybir.AluOpType
ACT = mybir.ActivationFunctionType
AX = mybir.AxisListType

P = 128
D = 1024
T = 512
DEPTH = 2
KC = D // P
HD = 64
NB = T // P
M_TILES, A_TILES, H_TILES = 2, 4, 2
M_COLS = 4 * 256 + 8
D_IN = M_COLS + 3 * 512 + 4 * 256
GATES = 4 * 256
F1 = 4 * D
F1_GROUPS = (16, 16)
F2 = 2816
F2_GROUPS = (12, 10)
QKV = 3 * 8 * HD
OW = 8 * HD
EPS = 1e-6
NEG = -1e30
POOL_WINDOWS = (2, 4, 8, 16)
LEVELS = (1, 2, 4, 8, 16, 32, 64)
SLOT = 2048
TWO_PI = 2 * math.pi

MQ, MK, MV, MO = 0, 2, 4, 6
AQ, AK, AV = 8, 12, 16
HQ, HF, HI, HG = 20, 22, 24, 26
U_TILES = 28

C_IDENT, C_BLOCK, C_LATER, C_ROT_A, C_ROT_B, C_IND, C_CAUSAL, C_PAST, C_CAUSAL4 = range(9)
N_CONST, N_KEPT = 9, 6
CAUSAL, PAST, CAUSAL4 = range(3)

R_NORM1, R_NORM2, R_GAIN2 = 0, 16, 32
R_KV, R_POOL, R_CONV, R_LB, R_MN, R_QN, R_KN, R_HN, R_SUB = [P + r for r in (0, 8, 16, 48, 52, 54, 56, 58, 60)]
N_ROWS = P + 62


def constants():
    c = np.zeros((P, N_CONST, P), np.float32)
    k, q = np.arange(P)[None, :], np.arange(P)[:, None]
    c[:, C_IDENT] = np.eye(P)
    c[:, C_BLOCK] = (k // HD) == (q // HD)
    c[:, C_CAUSAL] = np.where(k <= q, 0, NEG)
    c[:, C_PAST] = np.where(k >= q, 0, NEG)
    c[:, C_CAUSAL4] = np.where((k <= q) & (k % 4 == q % 4), 0, NEG)
    c[:, C_LATER] = np.where(q > k, -NEG, 0)
    for m, half, width in ((C_ROT_A, 8, 16), (C_ROT_B, 32, 64)):
        for p in range(P):
            r = p % HD
            if r < half:
                c[p + half, m, p] = -1
            elif r < width:
                c[p - half, m, p] = 1
    for j in range(8):
        for p in range(P):
            c[p, C_IND, 16 * j + 2 * j + p // HD] = 1
    sel = np.zeros((16, 8, P), np.float32)
    for j in range(8):
        sel[2 * j, j, :HD] = 1
        sel[2 * j + 1, j, HD:] = 1
    half = 8
    inv_a = (np.float32(500000.0) ** (-np.arange(half, dtype=np.float32) / np.float32(half))).astype(np.float32)
    inv_b = (np.float32(10000.0) ** (-np.arange(0, HD, 2, dtype=np.float32) / np.float32(HD))).astype(np.float32)
    p = np.arange(P)
    freq = inv_b[p % 32][:, None].astype(np.float32)
    ang = np.arange(T, dtype=np.float32)[None, :] * inv_a[:, None]
    rot = np.zeros((P, 2, T), np.float32)
    turned = p % HD < 2 * half
    rot[:, 0] = np.where(turned[:, None], np.cos(ang)[p % half], 1)
    rot[:, 1] = np.where(turned[:, None], np.sin(ang)[p % half], 0)
    t = np.arange(T)
    inv_count = np.stack([1.0 / np.minimum(t + 1, w) for w in POOL_WINDOWS]).astype(np.float32)
    level = np.zeros((P, len(LEVELS), P), np.float32)
    s, u = np.arange(P)[:, None], np.arange(P)[None, :]
    for n, b in enumerate(LEVELS):
        level[:, n] = (s // (2 * b) == u // (2 * b)) & (s // b % 2 == 0) & (u // b % 2 == 1)
    return c.reshape(P, -1), sel.reshape(16, -1), freq, rot.reshape(P, -1), inv_count, level.reshape(P, -1)


class Count:

    def __init__(self, handle):
        self.handle, self.n = handle, 0


class Mark:

    def __init__(self, count, n, loops):
        self.count, self.n, self.loops = count, n, loops


class Flow:

    def __init__(self, nc):
        self.nc, self.loops, self.counts, self.engines = nc, [], [], []

    def count(self, name):
        c = Count(self.nc.alloc_semaphore(name))
        self.counts.append(c)
        return c

    def at(self, count, back=0):
        return Mark(count, count.n - back, tuple(self.loops))

    def value(self, mark):
        v = mark.n
        for loop in mark.loops:
            per = loop["per"].get(mark.count, 0)
            if per:
                v = v + (loop["turn"] * per if loop in self.loops else per * (loop["turns"] - 1))
        return v

    @contextmanager
    def turns(self, turns, per):
        entry = {c: c.n for c in self.counts}
        for e in self.engines:
            e.forget()
        with self.nc.Fori(0, turns) as turn:
            loop = {"turn": turn, "turns": turns, "per": per}
            self.loops.append(loop)
            yield turn
            self.loops.pop()
        for e in self.engines:
            e.forget()
        for c in self.counts:
            got = c.n - entry[c]
            assert got == per.get(c, 0), f"{c.handle}: a turn counts {got}, not {per.get(c, 0)}"
            c.n = entry[c] + got * turns


class Engine:

    def __init__(self, flow, queue, count, fixed=None):
        self.flow, self.queue, self.count, self.fixed = flow, queue, count, fixed
        self.passed = {}
        flow.engines.append(self)

    def forget(self):
        self.passed = {}

    def after(self, *marks):
        moving = False
        for m in marks:
            if m is None:
                continue
            v = self.flow.value(m)
            if isinstance(v, int):
                if self.passed.get(m.count, 0) >= v:
                    continue
                self.passed[m.count] = v
            else:
                moving = True
            self.queue.wait_ge(m.count.handle, v)
        if moving and self.fixed is not None:
            self.queue.wait_ge(self.fixed.handle, 1)
        return self.queue

    def did(self, instruction, count=None, by=1):
        count = count or self.count
        instruction.then_inc(count.handle, by)
        count.n += by
        return self.flow.at(count)


def weave(*streams):
    streams = list(streams)
    while streams:
        for s in list(streams):
            for _ in range(s[1]):
                if next(s[0], s) is s:
                    streams.remove(s)
                    break
        yield


def finish(steps):
    for _ in steps:
        pass


def tile(buf, j):
    if isinstance(j, int):
        return buf[:, j, :]
    return buf[:, bass.ds(j, 1), :].rearrange("p a t -> p (a t)")


BASE = 16512
TILE = T * 4
RING_AT = BASE
X_AT = RING_AT + 6 * SLOT * 4
XH_AT = X_AT + KC * TILE
XL_AT = XH_AT + KC * TILE
BIG_AT = XL_AT + KC * TILE
SMALL_AT = BIG_AT + 44 * TILE
END = 229344


def plan():
    out = []
    for l in range(DEPTH):
        out += [(f"in_m{l}", 4, KC, 2), (f"gates{l}", 1, KC, 0), (f"in_ah{l}", 10, KC, 2), (f"out{l}", KC // 2, KC, 2)]
        for g, n in enumerate(F1_GROUPS):
            out += [(f"up{l}{g}", n // 2, KC, 2), (f"down{l}{g}", KC, n, 1)]

    def ffn(name):
        return [x for g, n in enumerate(F2_GROUPS)
                for x in ((f"gateup{name}{g}", n, KC, 2), (f"back{name}{g}", KC, n, 1))]
    out += ffn("a")
    out += [("pool_in", KC // 2, KC, 2), ("pool_group", 4, 2, 2), ("pool_out", KC // 2, KC, 2)]
    out += ffn("b")
    out += [("k", 6, KC, 2), ("v", 6, KC, 2)]
    out += ffn("c")
    out += [("q", 6, KC, 2), ("o", KC // 2, OW // P, 2)]
    out += ffn("d")
    return out


PLAN = plan()


def words(phase):
    _, _, nk, tiles = phase
    return nk * (tiles * P if tiles else HD)


class Kernel:

    def __init__(self, nc, dram):
        self.nc, self.dram = nc, dram
        f = self.flow = Flow(nc)
        at = nc.alloc_sbuf_tensor_at

        self.raw = [at(f"raw{s}", [P, SLOT], F32, offset=RING_AT + s * SLOT * 4) for s in range(2)]
        self.whi = [at(f"whi{s}", [P, SLOT], F32R, offset=RING_AT + (2 + s) * SLOT * 4) for s in range(2)]
        self.wlo = [at(f"wlo{s}", [P, SLOT], F32R, offset=RING_AT + (4 + s) * SLOT * 4) for s in range(2)]
        self.x = at("x", [P, KC, T], F32, offset=X_AT)
        self.xh = at("xh", [P, KC, T], F32R, offset=XH_AT)
        self.xl = at("xl", [P, KC, T], F32R, offset=XL_AT)
        self.scr = at("scr", [P, 2 * KC, T], F32, offset=XH_AT)
        self.u = at("u", [P, U_TILES, T], F32, offset=BIG_AT)
        self.mh = at("mh", [P, KC, T], F32R, offset=BIG_AT + 28 * TILE)
        self.ml = at("ml", [P, KC, T], F32R, offset=BIG_AT + 36 * TILE)
        self.spare = at("spare", [P, 2 * KC, T], F32, offset=BIG_AT + 28 * TILE)
        self.ah = at("ah", [P, 16, T], F32R, offset=BIG_AT)
        self.al = at("al", [P, 16, T], F32R, offset=BIG_AT + 16 * TILE)
        self.al2 = at("al2", [P, 12, T], F32R, offset=BIG_AT + 12 * TILE)
        self.f = at("f", [P, KC, T], F32, offset=BIG_AT + 26 * TILE)
        self.qkv = at("qkv", [P, 36, T], F32, offset=BIG_AT)
        self.oh = at("oh", [P, 4, T], F32R, offset=BIG_AT + 36 * TILE)
        self.ol = at("ol", [P, 4, T], F32R, offset=BIG_AT + 40 * TILE)
        self.small = SMALL_AT
        self.const = self.keep("const", [P, N_KEPT, P], F32)
        self.sel = self.keep("sel", [16, 8, P], F32)
        self.ones = self.keep("ones", [P, P], F32)
        self.cols = self.keep("cols", [P, N_ROWS], F32)
        self.rs = self.keep("rs", [P, T], F32)
        self.sqacc = self.keep("sqacc", [P, T], F32)
        self.ta = [self.keep(f"ta{i}", [P, T], F32) for i in range(2)]
        self.tb = [self.keep(f"tb{i}", [P, T], F32) for i in range(2)]
        self.level = self.keep("level", [P, len(LEVELS), P], U8)
        self.half = self.keep("half", [P, 4, P], BF16)
        self.freq = self.keep("freq", [P, 1], F32)
        self.gate_b = self.keep("gate_b", [4, 4], F32)
        self.lb = self.keep("lb", [P, 8], F32)
        self.tiny = self.keep("tiny", [P, 64], F32)
        assert self.small <= END, self.small - END
        self.bank = [nc.alloc_psum_tensor(f"bank{i}", [P, T], F32) for i in range(8)]

        self.c_pe, self.c_dve, self.c_act, self.c_pool = [f.count(n) for n in ("pe", "dve", "act", "pool")]
        self.c_fixed = f.count("fixed")
        self.c_raw = [f.count("raw_landed0"), f.count("raw_landed1")]
        self.c_hi, self.c_lo, self.c_mm, self.c_ev = [f.count(n) for n in ("hi_made", "lo_made", "tiles_done", "tiles_read")]
        self.c_tab, self.c_kv = f.count("tables_loaded"), f.count("keys_values_loaded")
        self.c_load, self.c_spill, self.c_out = f.count("loaded"), f.count("spilled"), f.count("stored")
        self.pe = Engine(f, nc.tensor, self.c_pe)
        self.v = Engine(f, nc.vector, self.c_dve)
        self.a = Engine(f, nc.scalar, self.c_act, self.c_fixed)
        self.g = Engine(f, nc.gpsimd, self.c_pool)
        self.sp = Engine(f, nc.sync, self.c_load)
        nc.scalar.sem_inc(self.c_fixed.handle, 1)
        for e, c, n in ((nc.gpsimd, self.c_lo, 2), (nc.tensor, self.c_mm, 4), (nc.vector, self.c_ev, 4)):
            e.sem_inc(c.handle, n)
            c.n = n
        self.unit = 0
        self.phase = 0
        self.banks_lent = False
        self.norm_due = None
        self.made_before = None
        self.split_made = [None] * KC
        self.free = [None] * 8

    def keep(self, name, shape, dtype):
        size = math.prod(shape[1:]) * {U8: 1, BF16: 2}.get(dtype, 4)
        t = self.nc.alloc_sbuf_tensor_at(name, shape, dtype, offset=self.small)
        self.small += -(-size // 32) * 32
        return t

    def c(self, which):
        return self.const[:, which, :]

    def ident16(self):
        return self.half[:, 0, :]

    def mask16(self, which):
        return self.half[:, 1 + which, :]


    def dense(self, *args, **kw):
        finish(self.dense_steps(*args, **kw))

    def dense_steps(self, name, loads, rhs, evacuate, per=None, ready=None, gate=None, straight=False):
        if self.banks_lent:
            self.pe.after(*self.free[0:4])
            self.banks_lent = False
        phase = PLAN[self.phase]
        assert phase[0] == name, (phase[0], name)
        _, count, nk, tiles = phase
        own = words(phase)
        last = self.phase + 1 == len(PLAN)
        after = own if last else words(PLAN[self.phase + 1])
        self.phase += 1
        base = {self.c_mm: 2, self.c_ev: 2, self.c_hi: 1, self.c_lo: 1}
        both = {c: 2 * n for c, n in base.items()}
        both.update({self.c_raw[0]: 32, self.c_raw[1]: 32})
        for c, n in (per or {}).items():
            both[c] = both.get(c, 0) + 2 * n

        def one(j, first=False, final=False):
            f, slot = self.flow, self.unit % 2
            for view, source in loads(j):
                sp = self.sp.after(f.at(self.c_lo, 1))
                self.sp.did(sp.dma_start(view(self.raw[slot]), source), self.c_raw[slot], 16)
            if not final:
                a = self.a.after(f.at(self.c_raw[1 - slot], -32), f.at(self.c_mm))
                n = max(own, after)
                self.a.did(a.activation(self.whi[1 - slot][:, 0:n], self.raw[1 - slot][:, 0:n], ACT.Copy), self.c_hi)
            g = self.g.after(f.at(self.c_hi, 0 if final else 1))
            self.g.did(g.tensor_tensor(self.wlo[slot][:, 0:own], self.raw[slot][:, 0:own],
                                       self.whi[slot][:, 0:own].bitcast(F32), ALU.subtract), self.c_lo)
            self.pe.after(f.at(self.c_lo), f.at(self.c_ev, 2))
            if tiles == 0:
                gate(slot)
                self.unit += 1
                yield
                return
            w = tiles * P

            def chunk(t, k):
                hi = self.whi[slot][:, k * w + t * P:k * w + t * P + P]
                lo = self.wlo[slot][:, k * w + t * P:k * w + t * P + P]
                bank = self.bank[2 * slot + t][:]
                xh, xl = rhs(k)
                self.nc.tensor.matmul(bank, hi, xh, start=k == 0, stop=False)
                self.nc.tensor.matmul(bank, hi, xl, start=False, stop=False)
                mm = self.nc.tensor.matmul(bank, lo, xh, start=False, stop=k == nk - 1)
                if k == nk - 1 or (tiles == 1 and k == nk // 2 - 1):
                    return self.pe.did(mm, self.c_mm)

            marks = [None] * tiles
            if first and ready is not None:
                for k in range(nk):
                    self.pe.after(*ready(k))
                    for t in range(tiles):
                        marks[t] = chunk(t, k)
                    yield
            else:
                for t in range(tiles):
                    for k in range(nk):
                        marks[t] = chunk(t, k)
                        yield
            if self.norm_due is not None:
                self.rs_made = self.finish_norm(self.norm_due)
                self.norm_due = None
            self.made_before = f.at(self.c_dve)
            for t in range(tiles):
                evacuate(j, t, self.bank[2 * slot + t], marks[t])
            self.unit += 1

        j = 0
        if ready is not None or self.norm_due is not None:
            yield from one(0, first=True, final=last and count == 1)
            j = 1
        pairs = (count - j - 1) // 2
        if pairs < 2 or count <= 4 or straight:
            pairs = 0
        if pairs:
            with self.flow.turns(pairs, both) as i:
                finish(one(i * 2 + j))
                finish(one(i * 2 + (j + 1)))
            j += 2 * pairs
        while j < count:
            yield from one(j, final=last and j == count - 1)
            j += 1


    def square(self, src, mark):
        f, sq = self.flow, self.tb[1]
        m = self.a.did(self.a.after(mark, f.at(self.c_dve)).activation(sq[:], src, ACT.Square))
        v = self.v.after(m, f.at(self.c_dve))
        return self.v.did(v.tensor_tensor(self.sqacc[:], self.sqacc[:], sq[:], ALU.add))

    def clear_sum(self):
        self.v.did(self.v.after(self.flow.at(self.c_pe)).memset(self.sqacc[:], 0.0))

    def split(self, src, gain, hi, lo, mark, wait=()):
        a = self.a.after(mark, *wait)
        m = self.a.did(a.activation(hi, src, ACT.Copy, scale=gain) if gain is not None
                       else a.activation(hi, src, ACT.Copy))
        v = self.v.after(m, mark, *wait)
        if gain is not None:
            i = v.scalar_tensor_tensor(lo, src, gain, hi.bitcast(F32), ALU.mult, ALU.subtract)
        else:
            i = v.tensor_tensor(lo, src, hi.bitcast(F32), ALU.subtract)
        return self.v.did(i)

    def finish_norm(self, mark):
        nc, f = self.nc, self.flow
        col, bc = self.bank[6], self.bank[7]
        self.pe.after(mark, self.free[6], self.free[7])
        for b in range(NB):
            mm = nc.tensor.matmul(col[:, b:b + 1], self.sqacc[:, b * P:b * P + P], self.ones[:, 0:1],
                                  start=b == 0, stop=b == NB - 1, skip_group_check=True)
        m = self.pe.did(mm)
        t = self.tiny
        m = self.v.did(self.v.after(m).tensor_scalar(t[:, 0:4], col[:, 0:4], 1.0 / D, EPS, ALU.mult, ALU.add))
        m = self.a.did(self.a.after(m).activation(t[:, 4:8], t[:, 0:4], ACT.Sqrt))
        m = self.v.did(self.v.after(m).reciprocal(t[:, 8:12], t[:, 4:8]))
        self.v.after(m, f.at(self.c_act))
        diag = self.ta[0]
        for b in range(NB):
            i = self.v.queue.tensor_scalar(diag[:, b * P:b * P + P], self.c(C_IDENT), t[:, 8 + b:9 + b], None, ALU.mult)
        m = self.v.did(i)
        self.pe.after(m)
        for b in range(NB):
            mm = nc.tensor.matmul(bc[:, b * P:b * P + P], self.ones[:], diag[:, b * P:b * P + P],
                                  start=b == 0, stop=b == NB - 1, skip_group_check=True)
        m = self.pe.did(mm)
        m = self.v.did(self.v.after(m).tensor_copy(self.rs[:], bc[:]))
        self.free[6] = self.free[7] = m
        return m


    def halves(self, weights, nk, w, row=0):
        def loads(col):
            h = nk // 2
            out = []
            for s in range(2):
                rows = weights[row + s * h * P:row + (s + 1) * h * P, :].rearrange("(k p) n -> p k n", p=P)
                cols = rows[:, :, bass.ds(col, w)] if not isinstance(col, int) else rows[:, :, col:col + w]
                out.append((lambda raw, s=s: raw[:, s * h * w:(s + 1) * h * w].rearrange("p (k n) -> p k n", n=w), cols))
            return out
        return loads

    def operand(self, hi, lo, first=0):
        return lambda k: (hi[:, first + k, :], lo[:, first + k, :])

    def to_residual(self, gain, last=True, tiles=2):
        def evacuate(j, t, bank, mark):
            f = self.flow
            jj = j * tiles + t
            x = tile(self.x, jj)
            v = self.v.after(mark, f.at(self.c_act), f.at(self.c_dve))
            m = self.v.did(v.tensor_tensor(x, bank[:], x, ALU.add), self.c_ev, 3 - tiles)
            if last:
                self.square(x, m)
                self.split(x, self.gain_col(gain, jj), tile(self.xh, jj), tile(self.xl, jj), m)
        n = tiles if last else 0
        return evacuate, {self.c_dve: 2 * n, self.c_act: 2 * n}

    def gain_col(self, row, j):
        if isinstance(j, int):
            return self.cols[:, row + j:row + j + 1]
        return self.cols[:, bass.ds(j + row, 1)]

    def scaled(self, dst, first=0):
        def evacuate(j, t, bank, mark):
            v = self.v.after(mark, self.rs_made, self.dst_free)
            self.v.did(v.tensor_tensor(tile(dst, j * 2 + (t + first)), bank[:], self.rs[:], ALU.mult), self.c_ev)
        return evacuate, {}

    def relu_squared(self, j, t, bank, mark):
        f, r, s = self.flow, self.ta[t], self.tb[t]
        v = self.v.after(mark, self.rs_made, f.at(self.c_act))
        m = self.v.did(v.scalar_tensor_tensor(r[:], bank[:], 0.0, self.rs[:], ALU.max, ALU.mult), self.c_ev)
        m = self.a.did(self.a.after(m, f.at(self.c_dve)).activation(s[:], r[:], ACT.Square))
        self.split(s[:], None, tile(self.ah, j * 2 + t), tile(self.al, j * 2 + t), m)

    def swiglu(self, j, t, bank, mark):
        f, r = self.flow, self.ta[t]
        v = self.v.after(mark, self.rs_made, f.at(self.c_act), f.at(self.c_dve))
        m = self.v.did(v.tensor_tensor(r[:], bank[:], self.rs[:], ALU.mult), self.c_ev)
        if t == 0:
            self.silu_made = self.a.did(self.a.after(m, f.at(self.c_dve)).activation(self.tb[0][:], r[:], ACT.Silu))
        else:
            m = self.v.did(self.v.after(m, self.silu_made).tensor_tensor(r[:], r[:], self.tb[0][:], ALU.mult))
            self.split(r[:], None, tile(self.ah, j), tile(self.al2, j), m)

    def to_f(self, add, last, tiles):
        def evacuate(j, t, bank, mark):
            f = self.flow
            dst = tile(self.f, j * tiles + t)
            v = self.v.after(mark, f.at(self.c_act), f.at(self.c_dve))
            i = v.tensor_tensor(dst, bank[:], dst, ALU.add) if add else v.tensor_copy(dst, bank[:])
            m = self.v.did(i, self.c_ev, 3 - tiles)
            if last:
                self.square(dst, m)
        n = tiles if last else 0
        return evacuate, {self.c_dve: n, self.c_act: n}


    def load_constants(self):
        nc, d = self.nc, self.dram
        sp, f = self.sp, self.flow
        rows = self.u[:, 26, 0:2 * P].rearrange("p (a n) -> p a n", a=2)

        def load(dst, src):
            sp.did(nc.sync.dma_start(dst, src), self.c_load, 16)
        masks = self.u[:, 23, 0:3 * P]
        load(self.const[:].rearrange("p a b -> p (a b)"), d["const"][:, 0:N_KEPT * P])
        load(masks, d["const"][:, N_KEPT * P:N_CONST * P])
        load(self.sel[:].rearrange("p a b -> p (a b)"), d["sel"])
        level = self.u[:, 24:26, :].rearrange("p a t -> p (a t)")[:, 0:len(LEVELS) * P]
        load(level, d["level"])
        load(self.freq[:], d["freq"])
        long = lambda a: a.rearrange("l (c p) -> (l c) p", p=P)
        for at, src in ((R_NORM1, long(d["norm1_g"])), (R_NORM2, long(d["norm2_g"])),
                        (R_GAIN2, d["norm_gain_2"].rearrange("l g (c p) -> (l g c) p", p=P))):
            load(rows[at:at + src.shape[0], 0, :], src)
        second = ((R_KV, d["kv_norm_gain_2"].rearrange("(c p) -> c p", p=P)), (R_POOL, long(d["pool_scale_2"])),
                  (R_CONV, d["mlstm_conv_w"].rearrange("l k (c p) -> (l k c) p", p=P)),
                  (R_LB, long(d["hgrn_lb_param"])), (R_SUB, d["diff_subln_g"]))
        for at, src in second:
            load(rows[at - P:at - P + src.shape[0], 1, :], src)
        for at, name in ((R_MN, "mlstm_norm_g"), (R_QN, "diff_q_norm_g"), (R_KN, "diff_k_norm_g"), (R_HN, "hgrn_norm_g")):
            for h in range(2):
                load(rows[at - P:at - P + 2, 1, h * HD:h * HD + HD], d[name])
        with nc.allow_non_contiguous_dma(reason="sixteen numbers"):
            load(self.gate_b[:].rearrange("h (a b) -> h a b", a=1), d["mlstm_gate_b"].rearrange("l g (h a) -> h a (l g)", a=1))
        self.v.did(nc.vector.memset(self.ones[:], 1.0))
        m = f.at(self.c_dve)
        self.pe.after(m, f.at(self.c_load))
        bank = self.bank[5]
        nc.tensor.transpose(bank[:, 0:P], rows[:, 0, :], self.c(C_IDENT))
        n = N_ROWS - P
        t = self.pe.did(nc.tensor.transpose(bank[:, P:P + n], rows[0:n, 1, :], self.const[0:n, C_IDENT, 0:n]))
        m = self.v.did(self.v.after(t).tensor_copy(self.cols[:], bank[:, 0:N_ROWS]))
        self.v.queue.tensor_copy(self.half[:, 0, :], self.c(C_IDENT))
        self.v.queue.tensor_copy(self.half[:, 1:4, :].rearrange("p a b -> p (a b)"), masks)
        self.v.queue.tensor_copy(self.level[:].rearrange("p a b -> p (a b)"), level)
        self.v.after(m)
        for l in range(DEPTH):
            for g in (1, 5):
                r = R_GAIN2 + (l * 6 + g) * KC
                nc.vector.tensor_scalar(self.cols[:, r:r + KC], self.cols[:, r:r + KC], 0.5, None, ALU.mult)
        self.free[5] = self.v.did(nc.vector.tensor_scalar(self.cols[:, R_QN:R_QN + 2], self.cols[:, R_QN:R_QN + 2],
                                                          HD ** -0.5, None, ALU.mult))

    def load_x(self):
        nc, f = self.nc, self.flow
        xt = self.u[:, 0:8, :].rearrange("p (b h) t -> p b (h t)", b=NB)
        m = self.sp.did(nc.sync.dma_start(xt, self.dram["x"][0].rearrange("(b p) d -> p b d", p=P)), self.c_spill, 16)
        self.clear_sum()
        self.pe.after(m)
        for j in range(KC):
            bank = self.bank[4 + j % 2]
            self.pe.after(self.free[4 + j % 2])
            for b in range(NB):
                mm = nc.tensor.transpose(bank[:, b * P:b * P + P], xt[:, b, j * P:j * P + P], self.c(C_IDENT))
            m = self.pe.did(mm)
            x = self.x[:, j, :]
            m = self.free[4 + j % 2] = self.v.did(self.v.after(m).tensor_copy(x, bank[:]))
            self.square(x, m)
            self.split(x, self.gain_col(R_NORM1, j), self.xh[:, j, :], self.xl[:, j, :], m)
        self.norm_due = f.at(self.c_dve)
        self.split_made = [f.at(self.c_dve)] * KC

    def store_x(self):
        nc = self.nc
        out = self.u[:, 0:8, :].rearrange("p (b h) t -> p b (h t)", b=NB)
        for j in range(KC):
            bank = self.bank[4 + j % 2]
            self.pe.after(self.x_made[j], self.free[4 + j % 2])
            for b in range(NB):
                mm = nc.tensor.transpose(bank[:, b * P:b * P + P], self.x[:, j, b * P:b * P + P], self.c(C_IDENT))
            m = self.pe.did(mm)
            m = self.free[4 + j % 2] = self.a.did(self.a.after(m).activation(
                out[:, :, j * P:j * P + P], bank[:].rearrange("p (b t) -> p b t", b=NB), ACT.Copy))
            sp = self.sp.after(m)
            m = self.sp.did(sp.dma_start(self.dram["out"][0].rearrange("(b p) d -> p b d", p=P)[:, :, j * P:j * P + P],
                                         out[:, :, j * P:j * P + P]), self.c_out, 16)
        self.sp.after(m)

    def post_norm(self, gain, next_gain):
        f = self.flow
        rs = self.finish_norm(f.at(self.c_dve))
        self.clear_sum()
        summed = [f.at(self.c_dve)] * 2
        self.x_made = []
        read = [None] * 2
        for j in range(KC):
            t, x = self.ta[j % 2], self.x[:, j, :]
            m = self.stt(t[:], self.f[:, j, :], self.gain_col(gain, j), self.rs[:], ALU.mult, ALU.mult, rs, read[j % 2])
            m = read[j % 2] = self.tt(x, x, t[:], ALU.add, m)
            self.x_made.append(m)
            if next_gain is not None:
                self.split_made[j] = self.split(x, self.gain_col(next_gain, j), self.xh[:, j, :], self.xl[:, j, :], m)
                sq = self.tb[j % 2]
                m = self.act(sq[:], x, ACT.Square, summed[j % 2])
                g = self.g.after(m, *summed)
                summed[j % 2] = self.g.did(g.tensor_tensor(self.sqacc[:], self.sqacc[:], sq[:], ALU.add))
        if next_gain is not None:
            self.norm_due = f.at(self.c_pool)

    def made(self, n, last):
        before, after = self.made_before, self.flow.at(self.c_dve)
        return lambda k: [before if k < n - last else after]

    def relu_ffn(self, l, next_gain):
        d, f = self.dram, self.flow
        ready = self.made(KC, 2)
        first = 0
        for g, n in enumerate(F1_GROUPS):
            up = self.halves(d["w_up"][l], KC, 2 * P)
            self.dense(f"up{l}{g}", lambda j: up(j * (2 * P) + first * P), self.operand(self.xh, self.xl),
                       self.relu_squared, {self.c_act: 4, self.c_dve: 2}, ready=ready if g == 0 else None)
            last = g == len(F1_GROUPS) - 1
            down = self.halves(d["w_down"][l], n, P, first * P)
            made = self.made(n, 2)
            if last:
                self.clear_sum()
            ev, per = self.to_residual(next_gain, last, 1)
            self.dense(f"down{l}{g}", lambda j: down(j * P), self.operand(self.ah, self.al), ev, per,
                       ready=made)
            first += n
        self.norm_due = f.at(self.c_dve)
        ready = self.made(KC, 1)
        self.split_made = [ready(k)[0] for k in range(KC)]

    def swiglu_ffn(self, name, l, i, gain, next_gain):
        d, f = self.dram, self.flow
        wg, wu, wd = d["ffn_w_gate_2"][l, i], d["ffn_w_up_2"][l, i], d["ffn_w_down_2"][l, i]
        first = 0
        for g, n in enumerate(F2_GROUPS):
            def loads(j):
                out = []
                for s, w in enumerate((wg, wu)):
                    col = j * P + first * P
                    rows = w.rearrange("(k p) n -> p k n", p=P)
                    cols = rows[:, :, col:col + P] if isinstance(col, int) else rows[:, :, bass.ds(col, P)]
                    out.append((lambda raw, s=s: raw[:].rearrange("p (k s n) -> p k s n", s=2, n=P)[:, :, s, :], cols))
                return out
            ready = None
            if g == 0:
                made = list(self.split_made)
                ready = lambda k: [made[k]]
            self.dense(f"gateup{name}{g}", loads, self.operand(self.xh, self.xl), self.swiglu,
                       {self.c_act: 2, self.c_dve: 2}, ready=ready)
            last = g == len(F2_GROUPS) - 1
            down = self.halves(wd, n, P, first * P)
            made = self.made(n, 1)
            if last:
                self.clear_sum()
            ev, per = self.to_f(g > 0, last, 1)
            self.dense(f"back{name}{g}", lambda j: down(j * P), self.operand(self.ah, self.al2), ev, per,
                       ready=made)
            first += n
        self.post_norm(gain, next_gain)

    def pool_mixer(self):
        d, f, nc = self.dram, self.flow, self.nc
        made = list(self.split_made)
        w_in = self.halves(d["pool_w_in_2"][0], KC, 2 * P)
        self.dst_free = None
        self.pooled = []

        ev, _ = self.scaled(self.u)

        def evacuate(j, t, bank, mark):
            ev(j, t, bank, mark)
            u, s = self.u[:, 2 * j + t, :], [self.u[:, 8 + 2 * t, :], self.u[:, 9 + 2 * t, :]]
            v, src = self.v, u
            m = f.at(self.c_ev)
            w = 1
            n = 0
            while w < POOL_WINDOWS[j]:
                dst = s[n % 2]
                v.after(m)
                nc.vector.tensor_copy(dst[:, 0:w], src[:, 0:w])
                m = v.did(nc.vector.tensor_tensor(dst[:, w:T], src[:, w:T], src[:, 0:T - w], ALU.add))
                src = dst
                w *= 2
                n += 1
            dst = s[n % 2]
            m = v.did(v.after(m, self.inv_loaded[j]).tensor_tensor(dst, src, self.inv[:, j, :], ALU.mult))
            m = v.did(v.after(m, f.at(self.c_act)).tensor_tensor(dst, dst, u, ALU.subtract))
            self.pooled.append(self.split(dst, None, self.mh[:, 2 * j + t, :], self.ml[:, 2 * j + t, :], m))
        self.inv = self.u[:, 14:18, :]
        self.inv_loaded = []
        for g in range(4):
            a = self.a.after(f.at(self.c_dve))
            src = d["inv_count"][g:g + 1, :].to_broadcast([P, T])
            self.inv_loaded.append(self.a.did(a.dma_start(self.inv[:, g, :], src), self.c_spill, 16))
        self.inv_loaded = [self.inv_loaded[-1]] * 4
        self.dense("pool_in", lambda j: w_in(j * 2 * P), self.operand(self.xh, self.xl), evacuate,
                   ready=lambda k: [made[k]])
        wg = d["pool_w_group_2"][0]
        grouped = []

        def ev_group(j, t, bank, mark):
            jj = 2 * j + t
            r = self.ta[t]
            v = self.v.after(mark, f.at(self.c_act), f.at(self.c_dve))
            m = self.v.did(v.tensor_scalar(r[:], bank[:], self.gain_col(R_POOL, jj), None, ALU.mult), self.c_ev)
            grouped.append(self.split(r[:], None, self.xh[:, jj, :], self.xl[:, jj, :], m))
        pooled = self.pooled
        jnow = [0]

        def loads_group(j):
            jnow[0] = j
            return self.halves(wg[j], 2, 2 * P)(0)
        self.dense("pool_group", loads_group, lambda k: (self.mh[:, 2 * jnow[0] + k, :], self.ml[:, 2 * jnow[0] + k, :]),
                   ev_group, ready=lambda k: [pooled[-1]])
        self.clear_sum()
        w_out = self.halves(d["pool_w_out_2"][0], KC, 2 * P)
        ev, per = self.to_f(False, True, 2)
        self.dense("pool_out", lambda j: w_out(j * 2 * P), self.operand(self.xh, self.xl), ev, per,
                   ready=lambda k: [grouped[k]])

    def keys_and_values(self):
        d, f = self.dram, self.flow
        made = list(self.split_made)
        self.dst_free = None
        for n, name in enumerate(("k", "v")):
            w = self.halves(d[f"w_{name}_2"], KC, 2 * P)
            ev, per = self.scaled(self.qkv, 12 * n)
            self.dense(name, lambda j: w(j * 2 * P), self.operand(self.xh, self.xl), ev, per,
                       ready=(lambda k: [made[k]]) if n == 0 else None)
        sp = self.sp.after(f.at(self.c_ev))
        self.spilled = self.sp.did(sp.dma_start(d["kv"].rearrange("j p t -> p j t"), self.qkv[:, 0:24, :]), self.c_spill, 16)


    def act(self, out, in_, fn, *marks, **kw):
        return self.a.did(self.a.after(*marks).activation(out, in_, fn, **kw))

    def tt(self, out, a, b, op, *marks):
        return self.v.did(self.v.after(*marks).tensor_tensor(out, a, b, op))

    def ts(self, out, a, s1, s2, op0, op1, *marks):
        v = self.v.after(*marks)
        return self.v.did(v.tensor_scalar(out, a, s1, s2, op0, op1) if op1 is not None
                          else v.tensor_scalar(out, a, s1, None, op0))

    def stt(self, out, a, s, b, op0, op1, *marks):
        return self.v.did(self.v.after(*marks).scalar_tensor_tensor(out, a, s, b, op0, op1))

    def mm(self, out, lhsT, rhs, start=True, stop=True):
        return self.nc.tensor.matmul(out, lhsT, rhs, start=start, stop=stop, skip_group_check=True)

    def tokens_first(self, src, dst, bank, *marks):
        self.pe.after(*marks, self.free[bank])
        for b in range(NB):
            mm = self.nc.tensor.transpose(self.bank[bank][:, b * P:b * P + P], src[:, b * P:b * P + P], self.c(C_IDENT))
        m = self.pe.did(mm)
        self.free[bank] = m = self.act(dst, self.bank[bank][:], ACT.Copy, m)
        return m

    def head_rstd(self, tiles, rows, bank, squares, *marks):
        n = 2 * len(tiles)
        ps = self.bank[bank]
        w = 16 if n > 4 else 4
        self.pe.after(self.free[bank])
        read = [None] * len(squares)
        for j, t in enumerate(tiles):
            i = j % len(squares)
            m = self.act(squares[i], t, ACT.Square, *marks, read[i])
            yield
            self.pe.after(m)
            m = read[i] = self.pe.did(self.mm(ps[0:w, :], self.const[:, C_IND, 16 * j:16 * j + w], squares[i],
                                              j == 0, j == len(tiles) - 1))
            yield
        m = self.free[bank] = self.ts(rows[0:w, :], ps[0:w, :], 1.0 / HD, EPS, ALU.mult, ALU.add, m, *marks)
        yield
        m = self.act(rows[0:w, :], rows[0:w, :], ACT.Sqrt, m)
        yield
        return self.v.did(self.v.after(m).reciprocal(rows[0:w, :], rows[0:w, :]))

    def spread(self, rows, n, j, bank, *marks):
        self.pe.after(*marks, self.free[bank])
        return self.pe.did(self.mm(self.bank[bank][:], self.sel[0:n, j, :], rows[0:n, :]))

    def into_mix(self, j, t, gain, bank, factor, *marks):
        m = self.free[bank] = self.stt(t, t, gain, self.bank[bank][:], ALU.mult, ALU.mult, *marks)
        if factor is not None:
            m = self.tt(t, t, factor, ALU.mult, m)
        self.mix_made[j] = self.split(t, None, self.mh[:, j, :], self.ml[:, j, :], m)


    def mlstm(self, l):
        f, sp = self.flow, lambda k: self.spare[:, k, :]
        s_bank, row_bank, num_bank, den_bank = 4, 5, 6, 7
        begin = [f.at(self.c_ev), f.at(self.c_mm), f.at(self.c_dve), f.at(self.c_act)]
        for b in (s_bank, row_bank, num_bank, den_bank):
            self.free[b] = f.at(self.c_dve)
        weights = [self.spare[:, 4 * b:4 * b + 4, :] for b in range(2)]
        enb, den, md, rows = sp(10), sp(11), sp(12), sp(12)
        r0, r1, r2 = [self.spare[0:4, k, :] for k in (13, 14, 15)]
        ones, hot = self.tb[0][0:4, :], self.tb[1][0:4, :].rearrange("p (h n) -> p h n", h=4)
        o = self.v.did(self.v.after(*begin).memset(ones, 1.0))
        for h in range(4):
            hot_made = self.v.did(self.v.queue.tensor_copy(hot[:, h, :], self.const[0:4, C_IDENT, h:h + 1].to_broadcast([4, P])))
        m = self.ts(r0, r0, self.gate_b[0:4, 2 * l:2 * l + 1], None, ALU.add, None, *begin)
        m = self.ts(r1, r1, self.gate_b[0:4, 2 * l + 1:2 * l + 2], None, ALU.add, None, m)
        m = self.stt(r2, r1, -1.0, r1, ALU.mult, ALU.max, m)
        yield
        m = self.act(r2, r2, ACT.Exp, m, scale=-1.0)
        yield
        m = self.act(r2, r2, ACT.Ln, m, bias=1.0)
        yield
        m = self.stt(r1, r1, 0.0, r2, ALU.min, ALU.subtract, m)
        m = self.v.did(self.v.after(m, o).tensor_tensor_scan(r2, ones, r1, 0.0, ALU.mult, ALU.add))
        a_made = self.tt(r0, r0, r2, ALU.subtract, m)
        big_made = self.v.did(self.v.after(a_made).tensor_tensor_scan(r1, r0, r0, 0.0, ALU.max, ALU.max))
        m_made = self.tt(r2, r2, r1, ALU.add, big_made)
        yield
        self.pe.after(a_made, self.free[row_bank])
        for b in range(NB):
            mm = self.nc.tensor.transpose(self.bank[row_bank][:, 4 * b:4 * b + 4], r0[:, b * P:b * P + P],
                                          self.const[0:4, C_IDENT, 0:4])
        acol = self.tiny[:, 16:32]
        t = self.pe.did(mm)
        yield
        acol_made = self.free[row_bank] = self.v.did(self.v.after(t).tensor_copy(acol, self.bank[row_bank][:, 0:16]))
        qk_made = [None] * 4
        for j in (0, 2, 1, 3):
            u, t = self.u[:, MQ + j, :], self.ta[j // 2]
            w = lambda k: self.gain_col(R_CONV + (l * 4 + k) * 4, j)
            m = self.ts(t[:], u, w(3), None, ALU.mult, None, qk_made[j - 1] if j % 2 else None, *begin)
            for shift in (1, 2, 3):
                m = self.stt(t[:, shift:], u[:, 0:T - shift], w(3 - shift), t[:, shift:], ALU.mult, ALU.add, m)
            yield
            qk_made[j] = self.act(u, t[:], ACT.Silu, m)
            yield
        h_made = [None, None]
        md_read, weights_read = None, [None, None]
        for i in range(2):
            vt = sp(8 + i)
            vt_made = self.tokens_first(self.u[:, MV + i, :], vt, row_bank, *begin)
            yield
            for e in range(2):
                h = 2 * i + e
                part = slice(e * HD, e * HD + HD)
                mb, wt = self.bank[row_bank], weights[e]
                self.pe.after(big_made, hot_made, self.free[row_bank])
                mb_made = self.pe.did(self.mm(mb[:], hot[:, h, :], r1))
                yield
                m = self.tt(md.rearrange("p (b t) -> p b t", b=NB), mb[:].rearrange("p (b t) -> p b t", b=NB),
                            self.const[:, C_LATER:C_LATER + 1, :].to_broadcast([P, NB, P]), ALU.add, mb_made, md_read)
                yield
                self.a.after(m, acol_made, weights_read[e])
                for j in range(NB):
                    bias = acol[:, 4 * j + h:4 * j + h + 1]
                    i1 = self.a.queue.activation(wt[:, j, j * P:j * P + P], md[:, j * P:j * P + P], ACT.Exp, bias=bias, scale=-1.0)
                    if j < NB - 1:
                        i1 = self.a.queue.activation(wt[:, j, (j + 1) * P:T], mb[:, (j + 1) * P:T], ACT.Exp,
                                                     bias=bias, scale=-1.0)
                w_made = md_read = self.free[row_bank] = self.a.did(i1)
                yield

                def scores(b):
                    self.pe.after(qk_made[i], qk_made[2 + i], self.free[s_bank])
                    for j in range(b + 1):
                        mm = self.mm(self.bank[s_bank][:, j * P:j * P + P], self.u[part, MK + i, j * P:j * P + P],
                                     self.u[part, MQ + i, b * P:b * P + P], j == 0, j == b)
                    return self.pe.did(mm)
                s_made = scores(0)
                yield
                for b in range(NB):
                    view = wt[:, 0:b + 1, b * P:b * P + P]
                    m = self.free[s_bank] = self.stt(
                        view, self.bank[s_bank][:, 0:(b + 1) * P].rearrange("p (j t) -> p j t", t=P), HD ** -0.5, view,
                        ALU.mult, ALU.mult, s_made, w_made)
                    yield
                    if b + 1 < NB:
                        s_made = scores(b + 1)
                        yield
                    self.pe.after(m, vt_made, self.free[num_bank], self.free[den_bank])
                    for j in range(b + 1):
                        src = wt[:, j, b * P:b * P + P]
                        first, final = b == 0 and j == 0, b == NB - 1 and j == b
                        self.mm(self.bank[num_bank][part, b * P:b * P + P], vt[:, j * P + e * HD:j * P + e * HD + HD], src, first, final)
                        mm = self.mm(self.bank[den_bank][part, b * P:b * P + P], self.ones[:, 0:HD], src, first, final)
                    nd_made = weights_read[e] = self.pe.did(mm)
                    yield
            sr = self.spread(r2, 4, i, row_bank, m_made)
            yield
            m = self.free[row_bank] = self.act(enb, self.bank[row_bank][:], ACT.Exp, sr, h_made[0], *begin, scale=-1.0)
            m = self.free[den_bank] = self.act(den, self.bank[den_bank][:], ACT.Abs, nd_made)
            yield
            m = self.tt(den, den, enb, ALU.max, m)
            m = self.v.did(self.v.after(m).reciprocal(den, den))
            h = self.u[:, MV + i, :]
            h_made[i] = self.free[num_bank] = self.tt(h, self.bank[num_bank][:], den, ALU.mult, m, vt_made)
            yield
        m = yield from self.head_rstd([self.u[:, MV + i, :] for i in range(2)], rows, row_bank,
                                      [self.ta[0][:], self.ta[1][:]], *h_made, md_read)
        for i in range(2):
            sg = self.act(self.u[:, MO + i, :], self.u[:, MO + i, :], ACT.Sigmoid, *begin)
            sr = self.spread(rows, 4, i, s_bank + i, m)
            yield
            self.into_mix(i, self.u[:, MV + i, :], self.gain_col(R_MN, l), s_bank + i, self.u[:, MO + i, :], sr, sg)


    def diff_attention(self, l, begin):
        f, s, d = self.flow, lambda k: self.scr[:, k, :], self.dram
        cos, sin = self.u[:, 2, :], self.u[:, 3, :]
        a = self.a.after(*begin)
        self.a.did(a.dma_start(self.u[:, 2:4, :].rearrange("p a t -> p (a t)"), d["rot"]), self.c_tab, 16)
        lv = s(4)[:, 0:4 * HD]
        loaded = self.a.did(a.dma_start(lv, d["diff_lambda"][l:l + 1].rearrange("l a n -> l (a n)").to_broadcast([P, 4 * HD])),
                            self.c_tab, 16)
        lv = lv.rearrange("p (a b n) -> p a b n", a=2, b=2)
        pr = s(5)[:, 0:2 * HD].rearrange("p (a n) -> p a n", a=2)
        t = self.tiny
        rows = s(12)
        rstd = yield from self.head_rstd([self.u[:, AQ + j, :] for j in range(8)], rows, 2, [s(k) for k in range(4)], *begin)
        m = self.tt(pr, lv[:, :, 0, :], lv[:, :, 1, :], ALU.mult, loaded, *begin)
        m = self.v.did(self.v.after(m).tensor_reduce(t[:, 32:34], pr, AX.X, ALU.add))
        yield
        m = self.act(t[:, 34:36], t[:, 32:34], ACT.Exp, m)
        yield
        m = self.tt(t[:, 36:37], t[:, 35:36], t[:, 34:35], ALU.subtract, m)
        init = 0.8 - 0.6 * math.exp(-0.3 * l)
        lam_made = self.ts(t[:, 37:38], t[:, 36:37], -init, None, ALU.add, None, m)
        yield
        yield from weave(*[(self.diff_heads(l, h, init, [s(6 * h + k) for k in range(6)], (2 + 3 * h, 3 + 3 * h, 4 + 3 * h),
                                            (cos, sin, loaded), rows, rstd, lam_made), 1) for h in range(2)])

    def diff_heads(self, l, stream, init, bufs, banks, tables, rows, rstd, lam_made):
        q_rot, k_rot, vt, at, p0, p1 = bufs
        p = (p0, p1)
        s_banks, o_bank = banks[0:2], banks[2]
        cos, sin, loaded = tables
        neg_lam = self.tiny[:, 37:38]
        st = self.tiny[:, 40 + 8 * stream:48 + 8 * stream]
        at_read, last = None, lam_made
        for h in (stream, stream + 2):
            turned = []
            for k, (src, gain, r) in enumerate(((AQ, R_QN, q_rot), (AK, R_KN, k_rot))):
                u, bank = self.u[:, src + h, :], s_banks[k]
                sr = self.spread(rows, 16, 4 * k + h, bank, rstd)
                yield
                m = self.free[bank] = self.stt(u, u, self.gain_col(gain, l), self.bank[bank][:], ALU.mult, ALU.mult, sr)
                yield
                self.pe.after(m, self.free[bank])
                pm = self.pe.did(self.mm(self.bank[bank][:], self.c(C_ROT_A), u))
                yield
                m2 = self.free[bank] = self.tt(r, self.bank[bank][:], sin, ALU.mult, pm, loaded, last, at_read)
                m1 = self.tt(u, u, cos, ALU.mult, m, loaded)
                turned.append(self.tt(r, r, u, ALU.add, m1, m2))
                yield
            vt_made = self.tokens_first(self.u[:, AV + h, :], vt, o_bank, rstd, at_read)
            yield
            for qb in range(NB):
                w = (qb + 1) * P
                self.pe.after(*turned, self.free[s_banks[0]], self.free[s_banks[1]])
                for e, bank in enumerate(s_banks):
                    part = slice(e * HD, e * HD + HD)
                    self.mm(self.bank[bank][:, 0:w], q_rot[part, qb * P:w], k_rot[part, 0:w], True, False)
                    mm = self.mm(self.bank[bank][:, qb * P:w], self.ident16(), self.mask16(CAUSAL), False, True)
                m = self.pe.did(mm)
                yield
                self.v.after(m, last)
                for e, bank in enumerate(s_banks):
                    i1 = self.v.queue.tensor_reduce(st[:, e:e + 1], self.bank[bank][:, 0:w], AX.X, ALU.max, negate=True)
                m = self.v.did(i1)
                yield
                self.a.after(m, last)
                for e, bank in enumerate(s_banks):
                    i1 = self.a.queue.activation(p[e][:, 0:w], self.bank[bank][:, 0:w], ACT.Exp, bias=st[:, e:e + 1],
                                                 accum_out=st[:, 2 + e:3 + e])
                m = self.free[s_banks[0]] = self.free[s_banks[1]] = self.a.did(i1)
                yield
                m = self.v.did(self.v.after(m).reciprocal(st[:, 4:6], st[:, 2:4]))
                m2 = self.tt(st[:, 6:7], st[:, 5:6], neg_lam, ALU.mult, m, lam_made)
                m = self.ts(p0[:, 0:w], p0[:, 0:w], st[:, 4:5], None, ALU.mult, None, m)
                m = last = self.stt(p0[:, 0:w], p1[:, 0:w], st[:, 6:7], p0[:, 0:w], ALU.mult, ALU.add, m, m2)
                yield
                bank = s_banks[0]
                self.pe.after(m, self.free[bank])
                for b in range(qb + 1):
                    mm = self.nc.tensor.transpose(self.bank[bank][:, b * P:b * P + P], p0[:, b * P:b * P + P], self.c(C_IDENT))
                m = last = self.pe.did(mm)
                yield
                m = self.free[bank] = self.act(at[:, 0:w], self.bank[bank][:, 0:w], ACT.Copy, m, at_read)
                yield
                self.pe.after(m, vt_made, self.free[o_bank])
                for b in range(qb + 1):
                    mm = self.mm(self.bank[o_bank][:, qb * P:w], vt[:, b * P:b * P + P], at[:, b * P:b * P + P],
                                 qb == 0 and b == 0, b == qb)
                o_made = at_read = self.pe.did(mm)
                yield
            o, sq, r = p0, p1, at
            m2 = self.act(sq, self.bank[o_bank][:], ACT.Square, o_made, last)
            m = self.free[o_bank] = self.act(o, self.bank[o_bank][:], ACT.Copy, o_made, last)
            yield
            bank = s_banks[1]
            self.pe.after(m2, self.free[bank])
            m3 = self.pe.did(self.mm(self.bank[bank][:], self.ones[:], sq))
            yield
            m3 = self.free[bank] = self.ts(r, self.bank[bank][:], 1.0 / (2 * HD), EPS, ALU.mult, ALU.add, m3, at_read)
            yield
            m3 = self.act(r, r, ACT.Sqrt, m3)
            yield
            m3 = self.v.did(self.v.after(m3).reciprocal(r, r))
            m3 = self.tt(o, o, r, ALU.mult, m3, m)
            m3 = self.ts(o, o, self.gain_col(R_SUB, l), 1.0 - init, ALU.mult, ALU.mult, m3)
            last = self.mix_made[2 + h] = self.split(o, None, self.mh[:, 2 + h, :], self.ml[:, 2 + h, :], m3)
            yield


    def lower_bounds(self):
        lb, p = self.lb, [self.cols[:, R_LB + 2 * l:R_LB + 2 * l + 2] for l in range(DEPTH)]
        t = self.tiny
        m = self.tt(t[:, 0:2], p[0], p[1], ALU.max, self.flow.at(self.c_dve))
        for l in range(DEPTH):
            m2 = self.tt(t[:, 2 + 2 * l:4 + 2 * l], p[l], t[:, 0:2], ALU.subtract, m)
        m = self.act(t[:, 6:10], t[:, 2:6], ACT.Exp, m2)
        m = self.tt(t[:, 10:12], t[:, 6:8], t[:, 8:10], ALU.add, m)
        m = self.v.did(self.v.after(m).reciprocal(t[:, 12:14], t[:, 10:12]))
        for l in range(DEPTH):
            m2 = self.tt(t[:, 2 + 2 * l:4 + 2 * l], t[:, 6 + 2 * l:8 + 2 * l], t[:, 12:14], ALU.mult, m)
        m = self.tt(lb[:, 0:2], t[:, 2:4], t[:, 2:4], ALU.subtract, m2)
        m = self.tt(t[:, 0:2], t[:, 2:4], t[:, 4:6], ALU.add, m)
        m = self.tt(lb[:, 2:4], t[:, 0:2], t[:, 2:4], ALU.subtract, m)
        self.ts(lb[:, 4:8], lb[:, 0:4], -1.0, 1.0, ALU.mult, ALU.add, m)

    def hgrn(self, l, begin):
        f = self.flow
        u, s, sp = lambda k: self.u[:, k, :], lambda k: self.scr[:, k, :], lambda k: self.spare[:, k, :]
        b, dd, z, at, vt, kt = u(0), u(1), [u(4), u(5)], [u(6), u(7)], sp(7), sp(15)
        qs, ks, st, keep = self.ta[0][:], self.ta[1][:], self.tb[0], self.tb[1][:]
        rows, out = s(15), [s(13), s(14)]
        x_bank, y_bank = 0, 1
        blocks = lambda t: t.rearrange("p (b t) -> p b t", b=NB)
        m = self.v.did(self.v.after(*begin).memset(keep, 1.0))
        keep_made = self.v.did(self.v.after(m).memset(blocks(keep)[:, :, 0:1], 0.0))
        dd_read = b_read = at_read = ks_read = st_read = None
        z_read = [None, None]
        h_made = []
        for i in range(2):
            q, k, fp = u(HQ + i), u(HF + i), dd
            lb, one_lb = self.lb[:, 2 * l + i:2 * l + i + 1], self.lb[:, 4 + 2 * l + i:5 + 2 * l + i]
            q_made = self.act(q, q, ACT.Silu, *begin)
            m = self.act(fp, k, ACT.Sigmoid, dd_read)
            mk = self.act(k, k, ACT.Sigmoid, m, scale=-1.0)
            yield
            m = self.ts(fp, fp, one_lb, lb, ALU.mult, ALU.add, m)
            k_made = self.ts(k, k, one_lb, None, ALU.mult, None, mk)
            yield
            m = self.act(fp, fp, ACT.Ln, m)
            yield
            b_made = self.v.did(self.v.after(m, keep_made, b_read).tensor_tensor_scan(b, keep, fp, 0.0, ALU.mult, ALU.add))
            vt_made = self.tokens_first(u(HI + i), vt, x_bank, at_read, *begin)
            yield
            self.pe.after(q_made, k_made, self.free[x_bank], self.free[y_bank])
            for e in range(2):
                for c in range(NB):
                    part, blk = slice(e * HD, e * HD + HD), slice(c * P, c * P + P)
                    mm = self.mm(self.bank[e][:, blk], k[part, blk], q[part, blk], c == 0, c == NB - 1)
            m = self.pe.did(mm)
            yield
            at_made = [None, None]
            for e in range(2):
                at_made[e] = self.free[e] = self.tt(blocks(at[e]), blocks(self.bank[e][:]),
                                                    self.const[:, C_IDENT:C_IDENT + 1, :].to_broadcast([P, NB, P]),
                                                    ALU.mult, m, at_read)
            dd_read = b_made
            for n, half in enumerate(LEVELS):
                cut = lambda t: t.rearrange("p (m h b) -> p m h b", h=2, b=half)
                r = cut(b)[:, :, 0, half - 1:half].to_broadcast([P, T // (2 * half), half])
                self.v.after(b_made, dd_read)
                self.v.queue.tensor_tensor(cut(dd)[:, :, 1, :], cut(b)[:, :, 1, :], r, ALU.subtract)
                m = self.tt(cut(dd)[:, :, 0, :], r, cut(b)[:, :, 0, :], ALU.subtract)
                yield
                m = self.act(dd, dd, ACT.Exp, m)
                yield
                zn = z[n % 2]
                self.v.after(m, q_made, k_made, z_read[n % 2])
                self.v.queue.tensor_tensor(cut(zn)[:, :, 1, :], cut(q)[:, :, 1, :], cut(dd)[:, :, 1, :], ALU.mult)
                m = dd_read = self.tt(cut(zn)[:, :, 0, :], cut(k)[:, :, 0, :], cut(dd)[:, :, 0, :], ALU.mult)
                yield
                for e in range(2):
                    self.pe.after(m, self.free[e])
                    for c in range(NB):
                        part, blk = slice(e * HD, e * HD + HD), slice(c * P, c * P + P)
                        mm = self.mm(self.bank[e][:, blk], zn[part, blk], zn[part, blk], c == 0, c == NB - 1)
                    zm = z_read[n % 2] = self.pe.did(mm)
                    yield
                    mask = self.level[:, n:n + 1, :].to_broadcast([P, NB, P])
                    v = self.v.after(zm, at_made[e])
                    at_made[e] = self.free[e] = self.v.did(v.copy_predicated(blocks(at[e]), mask, blocks(self.bank[e][:])))
            m = self.act(qs, b, ACT.Exp, b_made, ks_read, st_read, *begin)
            last = blocks(b)[:, :, P - 1:P]
            dec = self.tiny[:, 16 + 4 * i:20 + 4 * i]
            dec_made = self.act(dec.rearrange("p (a b) -> p a b", b=1), last, ACT.Exp, b_made)
            qs_made = self.tt(qs, qs, q, ALU.mult, m)
            m = self.tt(blocks(ks), last.to_broadcast([P, NB, P]), blocks(b), ALU.subtract, ks_read)
            b_read = m
            yield
            m = self.act(ks, ks, ACT.Exp, m, dec_made)
            yield
            m = self.tt(ks, ks, k, ALU.mult, m)
            yield
            kt_made = self.tokens_first(ks, kt, x_bank, m, st_read)
            ks_read = kt_made
            yield
            self.pe.after(*at_made, vt_made, self.free[x_bank])
            for e in range(2):
                for c in range(NB):
                    blk = slice(c * P, c * P + P)
                    mm = self.mm(self.bank[x_bank][e * HD:e * HD + HD, blk], vt[:, c * P + e * HD:c * P + e * HD + HD],
                                 at[e][:, blk], c == 0, False)
            at_read = self.pe.did(mm)
            for c in range(1, NB):
                blk, before = slice(c * P, c * P + P), slice((c - 1) * P, c * P)
                self.pe.after(kt_made, vt_made, self.free[y_bank])
                m = self.pe.did(self.mm(self.bank[y_bank][:, 0:P], kt[:, before], vt[:, before]))
                yield
                new = st[:, P:2 * P]
                m = self.free[y_bank] = self.tt(new, self.bank[y_bank][:, 0:P], self.c(C_BLOCK), ALU.mult, m, at_read)
                if c == 1:
                    m = self.v.did(self.v.after(m, st_read).tensor_copy(st[:, 0:P], new))
                else:
                    m = self.stt(st[:, 0:P], st[:, 0:P], dec[:, c - 1:c], new, ALU.mult, ALU.add, m, dec_made, st_read)
                yield
                self.pe.after(m, qs_made)
                st_read = at_read = self.pe.did(self.mm(self.bank[x_bank][:, blk], st[:, 0:P], qs[:, blk], False, c == NB - 1))
                yield
            h_made.append(self.v.did(self.v.after(st_read).tensor_copy(out[i], self.bank[x_bank][:])))
            self.free[x_bank] = h_made[-1]
            yield
        m = yield from self.head_rstd(out, rows, x_bank, [b, dd], *h_made)
        for i in range(2):
            g = u(HG + i)
            sg = self.act(g, g, ACT.Silu, *begin)
            sr = self.spread(rows, 4, i, i, m)
            yield
            self.into_mix(6 + i, out[i], self.gain_col(R_HN, l), i, g, sr, sg)

    def mixers(self, l):
        f = self.flow
        begin = [f.at(c) for c in (self.c_ev, self.c_mm, self.c_dve, self.c_act, self.c_pe)]
        self.free = [f.at(self.c_ev)] * 4 + [f.at(self.c_dve)] * 4
        finish(weave((self.diff_attention(l, begin), 1), (self.hgrn(l, begin), 1)))
        self.banks_lent = True



    def rotary_tables(self):
        cos, sin, t, ang = [self.spare[:, k, :] for k in (8, 9, 10, 11)]
        pos = self.spare[:, 12, :].bitcast(I32)
        begin = [self.flow.at(c) for c in (self.c_mm, self.c_dve, self.c_act)]
        a = self.a.after(*begin)
        loaded = self.a.did(a.dma_start(pos, self.dram["positions_2"].to_broadcast([P, T])), self.c_tab, 16)
        m = self.v.did(self.v.after(loaded, *begin).tensor_copy(t, pos))
        ang_made = self.ts(ang, t, self.freq[:, 0:1], None, ALU.mult, None, m)
        whole = 12582912.0
        c1, c2 = 6.28125, float(np.float32(round((TWO_PI - 6.28125) * 2 ** 22) / 2 ** 22))
        parts = (c1, c2, TWO_PI - c1 - c2)
        read = ang_made
        for dst, turn, shift in ((sin, 0.0, 0.0), (cos, 0.25, math.pi / 2)):
            m = self.ts(t, ang, 1 / TWO_PI, turn, ALU.mult, ALU.add, read)
            m = self.ts(t, t, whole, whole, ALU.add, ALU.subtract, m)
            src = ang
            for c in parts:
                m = read = self.stt(dst, t, -c, src, ALU.mult, ALU.add, m)
                src = dst
            if shift:
                m = self.ts(dst, dst, shift, None, ALU.add, None, m)
            m = self.ts(dst, dst, 3.1415925, -3.1415925, ALU.min, ALU.max, m)
            m = self.act(dst, dst, ACT.Sin, m)
        self.tables = cos, sin, m

    def attention_b_groups(self, pairs_of_heads, bufs, banks, stats, begin):
        f, nc = self.flow, self.nc
        t1, t2, vt = bufs[0:3]
        p_bufs = [self.scr[:, k:k + 2, :].rearrange("p a t -> p (a t)") for k in bufs[3:5]]
        s_banks, turn_bank, o_bank = banks[0:2], banks[2], banks[3]
        cos, sin, tables = self.tables
        p_read, vt_read = [None, None], None
        for i in pairs_of_heads:
            for g in range(3):
                q, k, v = [self.qkv[:, 12 * n + 4 * g + i, :] for n in range(3)]
                block = (lambda t, b: t[:, b * P:b * P + P]) if g == 0 else (lambda t, b: t[:, b::4])
                turned = []
                for n, u in enumerate((q, k)):
                    bank = s_banks[n]
                    self.pe.after(self.free[bank], self.kv_loaded, *begin)
                    m = self.pe.did(self.mm(self.bank[bank][:], self.c(C_ROT_B), u))
                    yield
                    scale = HD ** -0.5 if n == 0 else 1.0
                    last = turned[-1] if turned else (tables,)[0]
                    m1 = self.stt(t1, u, scale, cos, ALU.mult, ALU.mult, tables, m, last, *begin)
                    m2 = self.free[bank] = self.stt(t2, self.bank[bank][:], scale, sin, ALU.mult, ALU.mult, m)
                    turned.append(self.tt(u, t1, t2, ALU.add, m1, m2))
                    yield
                self.pe.after(self.free[turn_bank], self.kv_loaded)
                for b in range(NB):
                    mm = nc.tensor.transpose(self.bank[turn_bank][:, b * P:b * P + P], block(v, b), self.c(C_IDENT))
                m = self.pe.did(mm)
                yield
                vt_made = self.free[turn_bank] = self.act(vt, self.bank[turn_bank][:], ACT.Copy, m, vt_read, *begin)
                if g == 0:
                    pairs = [(0, 0, CAUSAL)] + [x for b in range(1, NB) for x in ((b, b - 1, PAST), (b, b, CAUSAL))]
                else:
                    pairs = [(b, b, CAUSAL if g == 1 else CAUSAL4) for b in range(NB)]
                spots, col = [], 0
                for n in range(len(pairs)):
                    if g == 0 and n == 3:
                        col = T
                    spots.append((s_banks[col // T], col % T))
                    col += P
                used = sorted({bank for bank, _ in spots})
                spans = []
                for qb in range(NB):
                    mine = [n for n in range(len(pairs)) if pairs[n][0] == qb]
                    spans.append((*spots[mine[0]], P * len(mine)))

                def scores(e):
                    part = slice(e * HD, e * HD + HD)
                    self.pe.after(*turned, *[self.free[bank] for bank in used])
                    for n, (qb, kb, mask) in enumerate(pairs):
                        bank, at = spots[n]
                        dst = self.bank[bank][:, at:at + P]
                        self.mm(dst, block(q, qb)[part], block(k, kb)[part], at == 0, False)
                        mm = self.mm(dst, self.ident16(), self.mask16(mask), False, n == len(pairs) - 1)
                    return self.pe.did(mm)
                s_made = scores(0)
                yield
                for e in range(2):
                    part, h = slice(e * HD, e * HD + HD), 2 * i + e
                    self.v.after(s_made)
                    for qb, (bank, at, w) in enumerate(spans):
                        i1 = self.v.queue.tensor_reduce(stats[:, 0, g, qb, h:h + 1], self.bank[bank][:, at:at + w], AX.X,
                                                        ALU.max, negate=True)
                    m = self.v.did(i1)
                    yield
                    p = p_bufs[e]
                    self.a.after(m, p_read[e], *begin)
                    col = 0
                    for qb, (bank, at, w) in enumerate(spans):
                        i1 = self.a.queue.activation(p[:, col:col + w], self.bank[bank][:, at:at + w], ACT.Exp,
                                                     bias=stats[:, 0, g, qb, h:h + 1], accum_out=stats[:, 1, g, qb, h:h + 1])
                        col += w
                    m = p_made = self.a.did(i1)
                    for bank in used:
                        self.free[bank] = m
                    yield
                    if e == 0:
                        s_made = scores(1)
                        yield
                    done = 0
                    while done < len(pairs):
                        n = min(4, len(pairs) - done)
                        self.pe.after(p_made, self.free[turn_bank])
                        for c in range(n):
                            mm = nc.tensor.transpose(self.bank[turn_bank][:, c * P:c * P + P],
                                                     p[:, (done + c) * P:(done + c + 1) * P], self.c(C_IDENT))
                        m = self.pe.did(mm)
                        yield
                        m = self.free[turn_bank] = self.act(p[:, done * P:(done + n) * P], self.bank[turn_bank][:, 0:n * P],
                                                            ACT.Copy, m)
                        yield
                        done += n
                    self.pe.after(m, vt_made, self.free[o_bank])
                    for n, (qb, kb, mask) in enumerate(pairs):
                        mm = self.mm(self.bank[o_bank][part, qb * P:qb * P + P], vt[:, kb * P + e * HD:kb * P + e * HD + HD],
                                     p[:, n * P:n * P + P], n == 0, n == len(pairs) - 1)
                    m = p_read[e] = vt_read = self.pe.did(mm)
                    yield
                if g == 0:
                    self.free[o_bank] = self.v.did(self.v.after(m).tensor_copy(q, self.bank[o_bank][:]))
                else:
                    self.free[o_bank] = self.v.did(self.v.after(m).tensor_copy(
                        q.rearrange("p (j r) -> p r j", r=4), self.bank[o_bank][:].rearrange("p (r j) -> p r j", r=4)))

    def attention_b(self):
        f, s, nc = self.flow, lambda k: self.scr[:, k, :], self.nc
        begin = [f.at(c) for c in (self.c_ev, self.c_mm, self.c_dve, self.c_act)]
        self.free = [f.at(self.c_ev)] * 8
        stats = s(15)[:, 0:192].rearrange("p (k g b h) -> p k g b h", k=2, g=3, b=4)
        finish(weave(*[(self.attention_b_groups((2 * n, 2 * n + 1), [self.ta[n][:], self.tb[n][:], s(8 + n), 4 * n, 4 * n + 2],
                                                [4 * n + b for b in range(4)], stats, begin), 1) for n in range(2)]))
        rows = [[s(4 + 3 * k + g)[0:8, :] for g in range(3)] for k in range(2)]
        m = [f.at(self.c_dve), f.at(self.c_act), f.at(self.c_pe)]
        for k in range(2):
            for g in range(3):
                bank = 2 + (3 * k + g) % 2
                self.pe.after(*m, self.free[bank])
                for b in range(NB):
                    mm = nc.tensor.transpose(self.bank[bank][0:8, b * P:b * P + P], stats[:, k, g, b, :], self.c(C_IDENT))
                t = self.pe.did(mm)
                src, dst = self.bank[bank][0:8, :], rows[k][g]
                if g:
                    src, dst = src.rearrange("p (r j) -> p r j", r=4), dst.rearrange("p (j r) -> p r j", r=4)
                row_made = self.free[bank] = self.v.did(self.v.after(t, *m).tensor_copy(dst, src))
        top, z = s(10)[0:8, :], s(11)[0:8, :]
        m = self.tt(top, rows[0][0], rows[0][1], ALU.min, row_made)
        m = self.tt(top, top, rows[0][2], ALU.min, m)
        for g in range(3):
            w, den = rows[0][g], rows[1][g]
            n = self.tt(w, top, w, ALU.subtract, m)
            n = self.act(w, w, ACT.Exp, n)
            if g == 0:
                zm = self.tt(z, w, den, ALU.mult, n)
            else:
                n = self.tt(den, w, den, ALU.mult, n)
                zm = self.tt(z, z, den, ALU.add, n, zm)
        m = self.v.did(self.v.after(zm).reciprocal(z, z))
        for g in range(3):
            w_made = self.tt(rows[0][g], rows[0][g], z, ALU.mult, m)
        self.o_made = []
        for i in range(4):
            t, acc = self.ta[i % 2], self.tb[i % 2]
            for g in range(3):
                sp = self.spread(rows[0][g], 8, i, 2 + (3 * i + g) % 4, w_made)
                bank = 2 + (3 * i + g) % 4
                o = self.qkv[:, 4 * g + i, :]
                if g == 0:
                    m = self.free[bank] = self.tt(acc[:], self.bank[bank][:], o, ALU.mult, sp, f.at(self.c_dve), f.at(self.c_act))
                else:
                    n = self.free[bank] = self.tt(t[:], self.bank[bank][:], o, ALU.mult, sp, f.at(self.c_dve))
                    m = self.tt(acc[:], acc[:], t[:], ALU.add, n)
            self.o_made.append(self.split(acc[:], None, self.oh[:, i, :], self.ol[:, i, :], m))
        self.banks_lent = True

    def gate_rows(self, l):
        w_in = self.dram["w_in"][l]
        w = HD

        def loads(j):
            out = []
            for s in range(2):
                src = w_in[:, GATES + 4 * s:GATES + 4 * s + 4].rearrange("(k p) n -> p k n", p=P)
                out.append((lambda raw, s=s: raw[:, 0:KC * w].rearrange("p (k n) -> p k n", n=w)[:, :, 32 * s:32 * s + 4], src))
            return out

        def gate(slot):
            bank = self.bank[2 * slot]
            for k in range(KC):
                hi = self.whi[slot][:, k * w:k * w + w]
                lo = self.wlo[slot][:, k * w:k * w + w]
                self.nc.tensor.matmul(bank[0:w, :], hi, self.xh[:, k, :], start=k == 0, stop=False)
                self.nc.tensor.matmul(bank[0:w, :], hi, self.xl[:, k, :], start=False, stop=False)
                mm = self.nc.tensor.matmul(bank[0:w, :], lo, self.xh[:, k, :], start=False, stop=k == KC - 1)
            self.gates_bank, self.gates_mark = bank, self.pe.did(mm, self.c_mm, 2)
            v = self.v.after(self.gates_mark, self.rs_made)
            v.tensor_tensor(self.spare[0:4, 13, :], bank[0:4, :], self.rs[0:4, :], ALU.mult)
            self.v.did(v.tensor_tensor(self.spare[0:4, 14, :], bank[32:36, :], self.rs[0:4, :], ALU.mult), self.c_ev, 2)
        self.dense(f"gates{l}", loads, None, None, gate=gate)

    def block_one(self, l):
        d = self.dram
        w_in = self.halves(d["w_in"][l], KC, 2 * P)
        self.dst_free = None
        ev, per = self.scaled(self.u)
        made = list(self.split_made)
        self.dense(f"in_m{l}", lambda j: w_in(j * (2 * P)), self.operand(self.xh, self.xl), ev, per,
                   ready=lambda k: [made[k]])
        self.gate_rows(l)
        ev, per = self.scaled(self.u, AQ)
        self.mix_made = [None] * KC
        rest = self.dense_steps(f"in_ah{l}", lambda j: w_in(j * (2 * P) + M_COLS), self.operand(self.xh, self.xl),
                                ev, per, straight=True)
        finish(weave((self.mlstm(l), 1), (rest, 2)))
        self.mixers(l)
        self.clear_sum()
        ev, per = self.to_residual(R_NORM2 + l * KC)
        w_out = self.halves(d["w_out"][l], KC, 2 * P)
        mix = list(self.mix_made)
        self.dense(f"out{l}", lambda j: w_out(j * 2 * P), self.operand(self.mh, self.ml), ev, per,
                   ready=lambda k: [mix[k]])
        self.norm_due = self.flow.at(self.c_dve)
        self.relu_ffn(l, R_NORM1 + KC if l == 0 else R_GAIN2)

    def block_two(self):
        d, f = self.dram, self.flow
        self.split_made = [f.at(self.c_dve)] * KC
        gain = lambda l, g: R_GAIN2 + (l * 6 + g) * KC
        self.swiglu_ffn("a", 0, 0, gain(0, 1), gain(0, 2))
        self.pool_mixer()
        self.post_norm(gain(0, 3), gain(0, 4))
        self.swiglu_ffn("b", 0, 1, gain(0, 5), R_KV)
        self.keys_and_values()
        m = f.at(self.c_mm)
        for j in range(KC):
            self.split_made[j] = self.split(self.x[:, j, :], self.gain_col(gain(1, 0), j),
                                            self.xh[:, j, :], self.xl[:, j, :], m)
        self.a.after(self.spilled)
        self.v.after(self.spilled)
        self.rotary_tables()
        self.swiglu_ffn("c", 1, 0, gain(1, 1), gain(1, 2))
        made = list(self.split_made)
        w = self.halves(d["attn_w_q_2"][0], KC, 2 * P)
        a = self.a.after(f.at(self.c_dve), f.at(self.c_mm), self.spilled)
        self.kv_loaded = self.a.did(a.dma_start(self.qkv[:, 12:36, :], d["kv"].rearrange("j p t -> p j t")), self.c_kv, 16)
        ev, per = self.scaled(self.qkv)
        self.dense("q", lambda j: w(j * 2 * P), self.operand(self.xh, self.xl), ev, per, ready=lambda k: [made[k]])
        self.attention_b()
        w_o = self.halves(d["attn_w_o_2"][0], OW // P, 2 * P)
        ev, per = self.to_f(False, True, 2)
        self.clear_sum()
        o = list(self.o_made)
        self.dense("o", lambda j: w_o(j * 2 * P), self.operand(self.oh, self.ol), ev, per, ready=lambda k: [o[k]])
        self.post_norm(gain(1, 3), gain(1, 4))
        self.swiglu_ffn("d", 1, 1, gain(1, 5), None)

    def run(self):
        self.load_constants()
        self.lower_bounds()
        self.load_x()
        self.a.did(self.a.after(self.flow.at(self.c_raw[0], -32)).activation(self.whi[0][:], self.raw[0][:], ACT.Copy), self.c_hi)
        for l in range(DEPTH):
            self.block_one(l)
        self.block_two()
        self.store_x()


def build(nc, dram):
    Kernel(nc, dram).run()


_INS = ["x", "norm1_g", "w_in", "mlstm_conv_w", "mlstm_gate_b", "mlstm_norm_g", "diff_q_norm_g", "diff_k_norm_g",
        "diff_lambda", "diff_subln_g", "hgrn_lb_param", "hgrn_norm_g", "w_out", "norm2_g", "w_up", "w_down",
        "positions_2", "norm_gain_2", "ffn_w_gate_2", "ffn_w_up_2", "ffn_w_down_2", "pool_w_in_2", "pool_w_group_2",
        "pool_scale_2", "pool_w_out_2", "kv_norm_gain_2", "w_k_2", "w_v_2", "attn_w_q_2", "attn_w_o_2"]


def kernel(**inputs):
    import concourse.bacc as bacc
    from concourse.bass_utils import run_bass_kernel_spmd

    nc = bacc.Bacc("TRN2", target_bir_lowering=False, num_devices=1)
    arrays = {name: np.ascontiguousarray(inputs[name]) for name in _INS}
    arrays.update(zip(("const", "sel", "freq", "rot", "inv_count", "level"), constants()))
    dram = {name: nc.dram_tensor(f"in_{name}", a.shape, mybir.dt.from_np(a.dtype), kind="ExternalInput").ap()
            for name, a in arrays.items()}
    dram["kv"] = nc.dram_tensor("kv", (24, P, T), F32).ap()
    dram["out"] = nc.dram_tensor("out", (1, T, D), F32, kind="ExternalOutput").ap()
    build(nc, dram)
    result = run_bass_kernel_spmd(nc, [{f"in_{name}": a for name, a in arrays.items()}], core_ids=[0])
    return result.results[0]["out"]
```

```python
import math
from contextlib import ExitStack, contextmanager

import numpy as np

import concourse.bass as bass
from concourse import mybir

F32 = mybir.dt.float32
F32R = mybir.dt.float32r
BF16 = mybir.dt.bfloat16
U8 = mybir.dt.uint8
I32 = mybir.dt.int32
ALU = mybir.AluOpType
ACT = mybir.ActivationFunctionType
AX = mybir.AxisListType

P = 128
D = 1024
T = 512
DEPTH = 2
KC = D // P
HD = 64
NB = T // P
M_TILES, A_TILES, H_TILES = 2, 4, 2
M_COLS = 4 * 256 + 8
D_IN = M_COLS + 3 * 512 + 4 * 256
GATES = 4 * 256
F1 = 4 * D
F1_GROUPS = (16, 16)
F2 = 2816
F2_GROUPS = (12, 10)
QKV = 3 * 8 * HD
OW = 8 * HD
EPS = 1e-6
NEG = -1e30
POOL_WINDOWS = (2, 4, 8, 16)
LEVELS = (1, 2, 4, 8, 16, 32, 64)
SLOT = 2048
TWO_PI = 2 * math.pi

MQ, MK, MV, MO = 0, 2, 4, 6
AQ, AK, AV = 8, 12, 16
HQ, HF, HI, HG = 20, 22, 24, 26
U_TILES = 28

C_IDENT, C_BLOCK, C_LATER, C_ROT_A, C_ROT_B, C_IND, C_CAUSAL, C_PAST, C_CAUSAL4 = range(9)
N_CONST, N_KEPT = 9, 6
CAUSAL, PAST, CAUSAL4 = range(3)

R_NORM1, R_NORM2, R_GAIN2 = 0, 16, 32
R_KV, R_POOL, R_CONV, R_LB, R_MN, R_QN, R_KN, R_HN, R_SUB = [P + r for r in (0, 8, 16, 48, 52, 54, 56, 58, 60)]
N_ROWS = P + 62


def constants():
    c = np.zeros((P, N_CONST, P), np.float32)
    k, q = np.arange(P)[None, :], np.arange(P)[:, None]
    c[:, C_IDENT] = np.eye(P)
    c[:, C_BLOCK] = (k // HD) == (q // HD)
    c[:, C_CAUSAL] = np.where(k <= q, 0, NEG)
    c[:, C_PAST] = np.where(k >= q, 0, NEG)
    c[:, C_CAUSAL4] = np.where((k <= q) & (k % 4 == q % 4), 0, NEG)
    c[:, C_LATER] = np.where(q > k, -NEG, 0)
    for m, half, width in ((C_ROT_A, 8, 16), (C_ROT_B, 32, 64)):
        for p in range(P):
            r = p % HD
            if r < half:
                c[p + half, m, p] = -1
            elif r < width:
                c[p - half, m, p] = 1
    for j in range(8):
        for p in range(P):
            c[p, C_IND, 16 * j + 2 * j + p // HD] = 1
    sel = np.zeros((16, 8, P), np.float32)
    for j in range(8):
        sel[2 * j, j, :HD] = 1
        sel[2 * j + 1, j, HD:] = 1
    half = 8
    inv_a = (np.float32(500000.0) ** (-np.arange(half, dtype=np.float32) / np.float32(half))).astype(np.float32)
    inv_b = (np.float32(10000.0) ** (-np.arange(0, HD, 2, dtype=np.float32) / np.float32(HD))).astype(np.float32)
    p = np.arange(P)
    freq = inv_b[p % 32][:, None].astype(np.float32)
    ang = np.arange(T, dtype=np.float32)[None, :] * inv_a[:, None]
    rot = np.zeros((P, 2, T), np.float32)
    turned = p % HD < 2 * half
    rot[:, 0] = np.where(turned[:, None], np.cos(ang)[p % half], 1)
    rot[:, 1] = np.where(turned[:, None], np.sin(ang)[p % half], 0)
    t = np.arange(T)
    inv_count = np.stack([1.0 / np.minimum(t + 1, w) for w in POOL_WINDOWS]).astype(np.float32)
    level = np.zeros((P, len(LEVELS), P), np.float32)
    s, u = np.arange(P)[:, None], np.arange(P)[None, :]
    for n, b in enumerate(LEVELS):
        level[:, n] = (s // (2 * b) == u // (2 * b)) & (s // b % 2 == 0) & (u // b % 2 == 1)
    return c.reshape(P, -1), sel.reshape(16, -1), freq, rot.reshape(P, -1), inv_count, level.reshape(P, -1)


class Count:

    def __init__(self, handle):
        self.handle, self.n = handle, 0


class Mark:

    def __init__(self, count, n, loops):
        self.count, self.n, self.loops = count, n, loops


class Flow:

    def __init__(self, nc):
        self.nc, self.loops, self.counts, self.engines = nc, [], [], []

    def count(self, name):
        c = Count(self.nc.alloc_semaphore(name))
        self.counts.append(c)
        return c

    def at(self, count, back=0):
        return Mark(count, count.n - back, tuple(self.loops))

    def value(self, mark):
        v = mark.n
        for loop in mark.loops:
            per = loop["per"].get(mark.count, 0)
            if per:
                v = v + (loop["turn"] * per if loop in self.loops else per * (loop["turns"] - 1))
        return v

    @contextmanager
    def turns(self, turns, per):
        entry = {c: c.n for c in self.counts}
        for e in self.engines:
            e.forget()
        with self.nc.Fori(0, turns) as turn:
            loop = {"turn": turn, "turns": turns, "per": per}
            self.loops.append(loop)
            yield turn
            self.loops.pop()
        for e in self.engines:
            e.forget()
        for c in self.counts:
            got = c.n - entry[c]
            assert got == per.get(c, 0), f"{c.handle}: a turn counts {got}, not {per.get(c, 0)}"
            c.n = entry[c] + got * turns


class Engine:

    def __init__(self, flow, queue, count, fixed=None):
        self.flow, self.queue, self.count, self.fixed = flow, queue, count, fixed
        self.passed = {}
        flow.engines.append(self)

    def forget(self):
        self.passed = {}

    def after(self, *marks):
        moving = False
        for m in marks:
            if m is None:
                continue
            v = self.flow.value(m)
            if isinstance(v, int):
                if self.passed.get(m.count, 0) >= v:
                    continue
                self.passed[m.count] = v
            else:
                moving = True
            self.queue.wait_ge(m.count.handle, v)
        if moving and self.fixed is not None:
            self.queue.wait_ge(self.fixed.handle, 1)
        return self.queue

    def did(self, instruction, count=None, by=1):
        count = count or self.count
        instruction.then_inc(count.handle, by)
        count.n += by
        return self.flow.at(count)


def weave(*streams):
    streams = list(streams)
    while streams:
        for s in list(streams):
            for _ in range(s[1]):
                if next(s[0], s) is s:
                    streams.remove(s)
                    break
        yield


def every(n, steps):
    for i, _ in enumerate(steps):
        if i % n == n - 1:
            yield


def finish(steps):
    for _ in steps:
        pass


def tile(buf, j):
    if isinstance(j, int):
        return buf[:, j, :]
    return buf[:, bass.ds(j, 1), :].rearrange("p a t -> p (a t)")


BASE = 16512
TILE = T * 4
RING_AT = BASE
X_AT = RING_AT + 6 * SLOT * 4
XH_AT = X_AT + KC * TILE
XL_AT = XH_AT + KC * TILE
BIG_AT = XL_AT + KC * TILE
SMALL_AT = BIG_AT + 44 * TILE
END = 229344


def plan():
    out = []
    for l in range(DEPTH):
        out += [(f"in_m{l}", 4, KC, 2), (f"gates{l}", 1, KC, 0), (f"in_ah{l}", 10, KC, 2), (f"out{l}", KC // 2, KC, 2)]
        for g, n in enumerate(F1_GROUPS):
            out += [(f"up{l}{g}", n // 2, KC, 2), (f"down{l}{g}", KC, n, 1)]

    def ffn(name):
        return [x for g, n in enumerate(F2_GROUPS)
                for x in ((f"gateup{name}{g}", n, KC, 2), (f"back{name}{g}", KC, n, 1))]
    out += ffn("a")
    out += [("pool_in", KC // 2, KC, 2), ("pool_group", 4, 2, 2), ("pool_out", KC // 2, KC, 2)]
    out += ffn("b")
    out += [("k", 6, KC, 2), ("v", 6, KC, 2)]
    out += ffn("c")
    out += [("q", 6, KC, 2), ("o", KC // 2, OW // P, 2)]
    out += ffn("d")
    return out


PLAN = plan()


def words(phase):
    _, _, nk, tiles = phase
    return nk * (tiles * P if tiles else HD)


class Kernel:

    def __init__(self, nc, dram):
        self.nc, self.dram = nc, dram
        f = self.flow = Flow(nc)
        at = nc.alloc_sbuf_tensor_at

        self.raw = [at(f"raw{s}", [P, SLOT], F32, offset=RING_AT + s * SLOT * 4) for s in range(2)]
        self.whi = [at(f"whi{s}", [P, SLOT], F32R, offset=RING_AT + (2 + s) * SLOT * 4) for s in range(2)]
        self.wlo = [at(f"wlo{s}", [P, SLOT], F32R, offset=RING_AT + (4 + s) * SLOT * 4) for s in range(2)]
        self.x = at("x", [P, KC, T], F32, offset=X_AT)
        self.xh = at("xh", [P, KC, T], F32R, offset=XH_AT)
        self.xl = at("xl", [P, KC, T], F32R, offset=XL_AT)
        self.scr = at("scr", [P, 2 * KC, T], F32, offset=XH_AT)
        self.u = at("u", [P, U_TILES, T], F32, offset=BIG_AT)
        self.mh = at("mh", [P, KC, T], F32R, offset=BIG_AT + 28 * TILE)
        self.ml = at("ml", [P, KC, T], F32R, offset=BIG_AT + 36 * TILE)
        self.spare = at("spare", [P, 2 * KC, T], F32, offset=BIG_AT + 28 * TILE)
        self.ah = at("ah", [P, 16, T], F32R, offset=BIG_AT)
        self.al = at("al", [P, 16, T], F32R, offset=BIG_AT + 16 * TILE)
        self.al2 = at("al2", [P, 12, T], F32R, offset=BIG_AT + 12 * TILE)
        self.f = at("f", [P, KC, T], F32, offset=BIG_AT + 26 * TILE)
        self.qkv = at("qkv", [P, 36, T], F32, offset=BIG_AT)
        self.oh = at("oh", [P, 4, T], F32R, offset=BIG_AT + 36 * TILE)
        self.ol = at("ol", [P, 4, T], F32R, offset=BIG_AT + 40 * TILE)
        self.small = SMALL_AT
        self.const = self.keep("const", [P, N_KEPT, P], F32)
        self.sel = self.keep("sel", [16, 8, P], F32)
        self.ones = self.keep("ones", [P, P], F32)
        self.cols = self.keep("cols", [P, N_ROWS], F32)
        self.rs = self.keep("rs", [P, T], F32)
        self.sqacc = self.keep("sqacc", [P, T], F32)
        self.ta = [self.keep(f"ta{i}", [P, T], F32) for i in range(2)]
        self.tb = [self.keep(f"tb{i}", [P, T], F32) for i in range(2)]
        self.level = self.keep("level", [P, len(LEVELS), P], U8)
        self.half = self.keep("half", [P, 4, P], BF16)
        self.freq = self.keep("freq", [P, 1], F32)
        self.gate_b = self.keep("gate_b", [4, 4], F32)
        self.lb = self.keep("lb", [P, 8], F32)
        self.tiny = self.keep("tiny", [P, 64], F32)
        assert self.small <= END, self.small - END
        self.bank = [nc.alloc_psum_tensor(f"bank{i}", [P, T], F32) for i in range(8)]

        self.c_pe, self.c_dve, self.c_act, self.c_pool = [f.count(n) for n in ("pe", "dve", "act", "pool")]
        self.c_fixed = f.count("fixed")
        self.c_raw = [f.count("raw_landed0"), f.count("raw_landed1")]
        self.c_hi, self.c_lo, self.c_mm, self.c_ev = [f.count(n) for n in ("hi_made", "lo_made", "tiles_done", "tiles_read")]
        self.c_tab, self.c_kv = f.count("tables_loaded"), f.count("keys_values_loaded")
        self.c_load, self.c_spill, self.c_out = f.count("loaded"), f.count("spilled"), f.count("stored")
        self.pe = Engine(f, nc.tensor, self.c_pe)
        self.v = Engine(f, nc.vector, self.c_dve)
        self.a = Engine(f, nc.scalar, self.c_act, self.c_fixed)
        self.g = Engine(f, nc.gpsimd, self.c_pool)
        self.sp = Engine(f, nc.sync, self.c_load)
        nc.scalar.sem_inc(self.c_fixed.handle, 1)
        for e, c, n in ((nc.gpsimd, self.c_lo, 2), (nc.tensor, self.c_mm, 4), (nc.vector, self.c_ev, 4)):
            e.sem_inc(c.handle, n)
            c.n = n
        self.unit = 0
        self.phase = 0
        self.banks_lent = False
        self.norm_due = None
        self.made_before = None
        self.split_made = [None] * KC
        self.free = [None] * 8

    def keep(self, name, shape, dtype):
        size = math.prod(shape[1:]) * {U8: 1, BF16: 2}.get(dtype, 4)
        t = self.nc.alloc_sbuf_tensor_at(name, shape, dtype, offset=self.small)
        self.small += -(-size // 32) * 32
        return t

    def c(self, which):
        return self.const[:, which, :]

    def ident16(self):
        return self.half[:, 0, :]

    def mask16(self, which):
        return self.half[:, 1 + which, :]


    def dense(self, *args, **kw):
        finish(self.dense_steps(*args, **kw))

    def dense_steps(self, name, loads, rhs, evacuate, per=None, ready=None, gate=None, straight=False,
                    order=None):
        phase = PLAN[self.phase]
        assert phase[0] == name, (phase[0], name)
        _, count, nk, tiles = phase
        own = words(phase)
        last = self.phase + 1 == len(PLAN)
        after = own if last else words(PLAN[self.phase + 1])
        self.phase += 1
        ks = order or tuple(range(nk))
        base = {self.c_mm: 2, self.c_ev: 2, self.c_hi: 1, self.c_lo: 1}
        both = {c: 2 * n for c, n in base.items()}
        both.update({self.c_raw[0]: 32, self.c_raw[1]: 32})
        for c, n in (per or {}).items():
            both[c] = both.get(c, 0) + 2 * n

        def one(j, first=False, final=False):
            f, slot = self.flow, self.unit % 2
            for view, source in (loads(j) if self.unit else ()):
                sp = self.sp.after(f.at(self.c_lo, 2))
                self.sp.did(sp.dma_start(view(self.raw[slot]), source), self.c_raw[slot], 16)
            if not final:
                n, nxt = after if isinstance(j, int) and j == count - 1 else own, 1 - slot
                a = self.a.after(f.at(self.c_raw[nxt], -32), f.at(self.c_mm))
                self.a.did(a.activation(self.whi[nxt][:, 0:n], self.raw[nxt][:, 0:n], ACT.Copy), self.c_hi)
                g = self.g.after(f.at(self.c_hi))
                self.g.did(g.tensor_tensor(self.wlo[nxt][:, 0:n], self.raw[nxt][:, 0:n],
                                           self.whi[nxt][:, 0:n].bitcast(F32), ALU.subtract), self.c_lo)
            self.pe.after(f.at(self.c_lo, 0 if final else 1), f.at(self.c_ev, 2))
            if self.banks_lent:
                self.pe.after(self.free[2 * slot], self.free[2 * slot + 1])
            if tiles == 0:
                gate(slot)
                self.unit += 1
                yield
                return
            w = tiles * P

            def chunk(t, k):
                hi = self.whi[slot][:, k * w + t * P:k * w + t * P + P]
                lo = self.wlo[slot][:, k * w + t * P:k * w + t * P + P]
                bank = self.bank[2 * slot + t][:]
                xh, xl = rhs(k)
                self.nc.tensor.matmul(bank, hi, xh, start=k == ks[0], stop=False)
                self.nc.tensor.matmul(bank, hi, xl, start=False, stop=False)
                mm = self.nc.tensor.matmul(bank, lo, xh, start=False, stop=k == ks[-1])
                if k == ks[-1] or (tiles == 1 and k == nk // 2 - 1):
                    return self.pe.did(mm, self.c_mm)

            marks = [None] * tiles
            if first and ready is not None:
                for k in ks:
                    while ready(k) is None:
                        yield
                    self.pe.after(*ready(k))
                    for t in range(tiles):
                        marks[t] = chunk(t, k)
                    yield
            else:
                for t in range(tiles):
                    for k in ks:
                        marks[t] = chunk(t, k)
                        yield
            if self.norm_due is not None:
                self.rs_made = self.finish_norm(self.norm_due)
                self.norm_due = None
            self.made_before = f.at(self.c_dve)
            for t in range(tiles):
                evacuate(j, t, self.bank[2 * slot + t], marks[t])
            self.unit += 1

        j = 0
        if ready is not None or self.norm_due is not None:
            yield from one(0, first=True, final=last and count == 1)
            j = 1
        pairs = (count - j - 1) // 2
        if pairs < 2 or count <= 4 or straight:
            pairs = 0
        if pairs:
            with self.flow.turns(pairs, both) as i:
                finish(one(i * 2 + j))
                finish(one(i * 2 + (j + 1)))
            j += 2 * pairs
        while j < count:
            yield from one(j, final=last and j == count - 1)
            j += 1


    def square(self, src, mark):
        f, sq = self.flow, self.tb[1]
        m = self.a.did(self.a.after(mark, f.at(self.c_dve)).activation(sq[:], src, ACT.Square))
        v = self.v.after(m, f.at(self.c_dve))
        return self.v.did(v.tensor_tensor(self.sqacc[:], self.sqacc[:], sq[:], ALU.add))

    def clear_sum(self):
        self.v.did(self.v.after(self.flow.at(self.c_pe)).memset(self.sqacc[:], 0.0))

    def split(self, src, gain, hi, lo, mark, wait=()):
        a = self.a.after(mark, *wait)
        m = self.a.did(a.activation(hi, src, ACT.Copy, scale=gain) if gain is not None
                       else a.activation(hi, src, ACT.Copy))
        v = self.v.after(m, mark, *wait)
        if gain is not None:
            i = v.scalar_tensor_tensor(lo, src, gain, hi.bitcast(F32), ALU.mult, ALU.subtract)
        else:
            i = v.tensor_tensor(lo, src, hi.bitcast(F32), ALU.subtract)
        return self.v.did(i)

    def finish_norm(self, mark):
        nc, f = self.nc, self.flow
        col, bc = self.bank[6], self.bank[7]
        self.pe.after(mark, self.free[6], self.free[7])
        for b in range(NB):
            mm = nc.tensor.matmul(col[:, b:b + 1], self.sqacc[:, b * P:b * P + P], self.ones[:, 0:1],
                                  start=b == 0, stop=b == NB - 1, skip_group_check=True)
        m = self.pe.did(mm)
        t = self.tiny
        m = self.v.did(self.v.after(m).tensor_scalar(t[:, 0:4], col[:, 0:4], 1.0 / D, EPS, ALU.mult, ALU.add))
        m = self.a.did(self.a.after(m).activation(t[:, 4:8], t[:, 0:4], ACT.Sqrt))
        m = self.v.did(self.v.after(m).reciprocal(t[:, 8:12], t[:, 4:8]))
        self.v.after(m, f.at(self.c_act))
        diag = self.ta[0]
        for b in range(NB):
            i = self.v.queue.tensor_scalar(diag[:, b * P:b * P + P], self.c(C_IDENT), t[:, 8 + b:9 + b], None, ALU.mult)
        m = self.v.did(i)
        self.pe.after(m)
        for b in range(NB):
            mm = nc.tensor.matmul(bc[:, b * P:b * P + P], self.ones[:], diag[:, b * P:b * P + P],
                                  start=b == 0, stop=b == NB - 1, skip_group_check=True)
        m = self.pe.did(mm)
        m = self.v.did(self.v.after(m).tensor_copy(self.rs[:], bc[:]))
        self.free[6] = self.free[7] = m
        return m


    def halves(self, weights, nk, w, row=0):
        def loads(col):
            h = nk // 2
            out = []
            for s in range(2):
                rows = weights[row + s * h * P:row + (s + 1) * h * P, :].rearrange("(k p) n -> p k n", p=P)
                cols = rows[:, :, bass.ds(col, w)] if not isinstance(col, int) else rows[:, :, col:col + w]
                out.append((lambda raw, s=s: raw[:, s * h * w:(s + 1) * h * w].rearrange("p (k n) -> p k n", n=w), cols))
            return out
        return loads

    def operand(self, hi, lo, first=0):
        return lambda k: (hi[:, first + k, :], lo[:, first + k, :])

    def to_residual(self, gain, last=True, tiles=2):
        def evacuate(j, t, bank, mark):
            f = self.flow
            jj = j * tiles + t
            x = tile(self.x, jj)
            v = self.v.after(mark, f.at(self.c_act), f.at(self.c_dve))
            m = self.v.did(v.tensor_tensor(x, bank[:], x, ALU.add), self.c_ev, 3 - tiles)
            if last:
                self.square(x, m)
                self.split(x, self.gain_col(gain, jj), tile(self.xh, jj), tile(self.xl, jj), m)
        n = tiles if last else 0
        return evacuate, {self.c_dve: 2 * n, self.c_act: 2 * n}

    def gain_col(self, row, j):
        if isinstance(j, int):
            return self.cols[:, row + j:row + j + 1]
        return self.cols[:, bass.ds(j + row, 1)]

    def scaled(self, dst, first=0):
        def evacuate(j, t, bank, mark):
            v = self.v.after(mark, self.rs_made, self.dst_free)
            self.v.did(v.tensor_tensor(tile(dst, j * 2 + (t + first)), bank[:], self.rs[:], ALU.mult), self.c_ev)
        return evacuate, {}

    def relu_squared(self, j, t, bank, mark):
        f, r, s = self.flow, self.ta[t], self.tb[t]
        v = self.v.after(mark, self.rs_made, f.at(self.c_act))
        m = self.v.did(v.scalar_tensor_tensor(r[:], bank[:], 0.0, self.rs[:], ALU.max, ALU.mult), self.c_ev)
        m = self.a.did(self.a.after(m, f.at(self.c_dve)).activation(s[:], r[:], ACT.Square))
        self.split(s[:], None, tile(self.ah, j * 2 + t), tile(self.al, j * 2 + t), m)

    def swiglu(self, j, t, bank, mark):
        f, r = self.flow, self.ta[t]
        v = self.v.after(mark, self.rs_made, f.at(self.c_act), f.at(self.c_dve))
        m = self.v.did(v.tensor_tensor(r[:], bank[:], self.rs[:], ALU.mult), self.c_ev)
        if t == 0:
            self.silu_made = self.a.did(self.a.after(m, f.at(self.c_dve)).activation(self.tb[0][:], r[:], ACT.Silu))
        else:
            m = self.v.did(self.v.after(m, self.silu_made).tensor_tensor(r[:], r[:], self.tb[0][:], ALU.mult))
            self.split(r[:], None, tile(self.ah, j), tile(self.al2, j), m)

    def to_f(self, add, last, tiles):
        def evacuate(j, t, bank, mark):
            f = self.flow
            dst = tile(self.f, j * tiles + t)
            v = self.v.after(mark, f.at(self.c_act), f.at(self.c_dve))
            i = v.tensor_tensor(dst, bank[:], dst, ALU.add) if add else v.tensor_copy(dst, bank[:])
            m = self.v.did(i, self.c_ev, 3 - tiles)
            if last:
                self.square(dst, m)
        n = tiles if last else 0
        return evacuate, {self.c_dve: n, self.c_act: n}


    def load_constants(self):
        nc, d = self.nc, self.dram
        sp, f = self.sp, self.flow
        rows = self.u[:, 26, 0:2 * P].rearrange("p (a n) -> p a n", a=2)

        def load(dst, src):
            sp.did(nc.sync.dma_start(dst, src), self.c_load, 16)
        masks = self.u[:, 23, 0:3 * P]
        load(self.const[:].rearrange("p a b -> p (a b)"), d["const"][:, 0:N_KEPT * P])
        load(masks, d["const"][:, N_KEPT * P:N_CONST * P])
        load(self.sel[:].rearrange("p a b -> p (a b)"), d["sel"])
        level = self.u[:, 24:26, :].rearrange("p a t -> p (a t)")[:, 0:len(LEVELS) * P]
        load(level, d["level"])
        load(self.freq[:], d["freq"])
        long = lambda a: a.rearrange("l (c p) -> (l c) p", p=P)
        for at, src in ((R_NORM1, long(d["norm1_g"])), (R_NORM2, long(d["norm2_g"])),
                        (R_GAIN2, d["norm_gain_2"].rearrange("l g (c p) -> (l g c) p", p=P))):
            load(rows[at:at + src.shape[0], 0, :], src)
        second = ((R_KV, d["kv_norm_gain_2"].rearrange("(c p) -> c p", p=P)), (R_POOL, long(d["pool_scale_2"])),
                  (R_CONV, d["mlstm_conv_w"].rearrange("l k (c p) -> (l k c) p", p=P)),
                  (R_LB, long(d["hgrn_lb_param"])), (R_SUB, d["diff_subln_g"]))
        for at, src in second:
            load(rows[at - P:at - P + src.shape[0], 1, :], src)
        for at, name in ((R_MN, "mlstm_norm_g"), (R_QN, "diff_q_norm_g"), (R_KN, "diff_k_norm_g"), (R_HN, "hgrn_norm_g")):
            for h in range(2):
                load(rows[at - P:at - P + 2, 1, h * HD:h * HD + HD], d[name])
        with nc.allow_non_contiguous_dma(reason="sixteen numbers"):
            load(self.gate_b[:].rearrange("h (a b) -> h a b", a=1), d["mlstm_gate_b"].rearrange("l g (h a) -> h a (l g)", a=1))
        self.v.did(nc.vector.memset(self.ones[:], 1.0))
        m = f.at(self.c_dve)
        self.pe.after(m, f.at(self.c_load))
        bank = self.bank[5]
        nc.tensor.transpose(bank[:, 0:P], rows[:, 0, :], self.c(C_IDENT))
        n = N_ROWS - P
        t = self.pe.did(nc.tensor.transpose(bank[:, P:P + n], rows[0:n, 1, :], self.const[0:n, C_IDENT, 0:n]))
        m = self.v.did(self.v.after(t).tensor_copy(self.cols[:], bank[:, 0:N_ROWS]))
        self.v.queue.tensor_copy(self.half[:, 0, :], self.c(C_IDENT))
        self.v.queue.tensor_copy(self.half[:, 1:4, :].rearrange("p a b -> p (a b)"), masks)
        self.v.queue.tensor_copy(self.level[:].rearrange("p a b -> p (a b)"), level)
        self.v.after(m)
        for l in range(DEPTH):
            for g in (1, 5):
                r = R_GAIN2 + (l * 6 + g) * KC
                nc.vector.tensor_scalar(self.cols[:, r:r + KC], self.cols[:, r:r + KC], 0.5, None, ALU.mult)
        self.free[5] = self.v.did(nc.vector.tensor_scalar(self.cols[:, R_QN:R_QN + 2], self.cols[:, R_QN:R_QN + 2],
                                                          HD ** -0.5, None, ALU.mult))

    def load_x(self):
        nc, f = self.nc, self.flow
        xt = self.u[:, 0:8, :].rearrange("p (b h) t -> p b (h t)", b=NB)
        self.clear_sum()
        cleared = f.at(self.c_dve)
        summed, low = [cleared] * 2, []
        for j in range(KC):
            bank = 4 + j % 4
            self.pe.after(self.x_loaded, self.free[bank])
            for b in range(NB):
                mm = nc.tensor.transpose(self.bank[bank][:, b * P:b * P + P], xt[:, b, j * P:j * P + P], self.c(C_IDENT))
            m = self.pe.did(mm)
            x = self.x[:, j, :]
            m = self.free[bank] = self.v.did(self.v.after(m).tensor_copy(x, self.bank[bank][:]))
            low.append((j, self.act(self.xh[:, j, :], x, ACT.Copy, m, scale=self.gain_col(R_NORM1, j))))
            sq = self.tb[j % 2]
            m = self.act(sq[:], x, ACT.Square, summed[j % 2])
            g = self.g.after(m, *summed)
            summed[j % 2] = self.g.did(g.tensor_tensor(self.sqacc[:], self.sqacc[:], sq[:], ALU.add))
            while len(low) > (1 if j < KC - 1 else 0):
                i, mark = low.pop(0)
                self.split_made[i] = self.stt(self.xl[:, i, :], self.x[:, i, :], self.gain_col(R_NORM1, i),
                                              self.xh[:, i, :].bitcast(F32), ALU.mult, ALU.subtract, mark)
        self.norm_due = f.at(self.c_pool)

    def store_x(self):
        nc = self.nc
        out = self.u[:, 0:8, :].rearrange("p (b h) t -> p b (h t)", b=NB)
        for j in range(KC):
            bank = self.bank[4 + j % 2]
            self.pe.after(self.x_made[j], self.free[4 + j % 2])
            for b in range(NB):
                mm = nc.tensor.transpose(bank[:, b * P:b * P + P], self.x[:, j, b * P:b * P + P], self.c(C_IDENT))
            m = self.pe.did(mm)
            m = self.free[4 + j % 2] = self.a.did(self.a.after(m).activation(
                out[:, :, j * P:j * P + P], bank[:].rearrange("p (b t) -> p b t", b=NB), ACT.Copy))
            sp = self.sp.after(m)
            m = self.sp.did(sp.dma_start(self.dram["out"][0].rearrange("(b p) d -> p b d", p=P)[:, :, j * P:j * P + P],
                                         out[:, :, j * P:j * P + P]), self.c_out, 16)
        self.sp.after(m)

    def post_norm(self, gain, next_gain):
        f = self.flow
        rs = self.finish_norm(f.at(self.c_dve))
        self.x_made = []
        read, summed = [None] * 2, [None] * 2
        low = None
        for j in range(KC):
            t, x = self.ta[j % 2], self.x[:, j, :]
            m = self.stt(t[:], self.f[:, j, :], self.gain_col(gain, j), self.rs[:], ALU.mult, ALU.mult, rs, read[j % 2])
            m = read[j % 2] = self.tt(x, x, t[:], ALU.add, m)
            self.x_made.append(m)
            if next_gain is None:
                continue
            hi = self.act(self.xh[:, j, :], x, ACT.Copy, m, scale=self.gain_col(next_gain, j))
            if j == 0:
                summed[1] = self.act(self.sqacc[:], x, ACT.Square, rs)
            else:
                sq = self.tb[j % 2]
                m = self.act(sq[:], x, ACT.Square, summed[j % 2])
                g = self.g.after(m, *summed)
                summed[j % 2] = self.g.did(g.tensor_tensor(self.sqacc[:], self.sqacc[:], sq[:], ALU.add))
            for i, mark in ([low] if low else []) + ([(j, hi)] if j == KC - 1 else []):
                self.split_made[i] = self.stt(self.xl[:, i, :], self.x[:, i, :], self.gain_col(next_gain, i),
                                              self.xh[:, i, :].bitcast(F32), ALU.mult, ALU.subtract, mark)
            low = (j, hi)
        if next_gain is not None:
            self.norm_due = f.at(self.c_pool)

    def made(self, n, last):
        before, after = self.made_before, self.flow.at(self.c_dve)
        return lambda k: [before if k < n - last else after]

    def relu_ffn(self, l, next_gain):
        d, f = self.dram, self.flow
        ready = self.made(KC, 2)
        first = 0
        for g, n in enumerate(F1_GROUPS):
            up = self.halves(d["w_up"][l], KC, 2 * P)
            self.dense(f"up{l}{g}", lambda j: up(j * (2 * P) + first * P), self.operand(self.xh, self.xl),
                       self.relu_squared, {self.c_act: 4, self.c_dve: 2}, ready=ready if g == 0 else None)
            last = g == len(F1_GROUPS) - 1
            down = self.halves(d["w_down"][l], n, P, first * P)
            made = self.made(n, 2)
            if last:
                self.clear_sum()
            ev, per = self.to_residual(next_gain, last, 1)
            self.dense(f"down{l}{g}", lambda j: down(j * P), self.operand(self.ah, self.al), ev, per,
                       ready=made)
            first += n
        self.norm_due = f.at(self.c_dve)
        ready = self.made(KC, 1)
        self.split_made = [ready(k)[0] for k in range(KC)]

    def swiglu_ffn(self, name, l, i, gain, next_gain, operand=None):
        d, f = self.dram, self.flow
        wg, wu, wd = d["ffn_w_gate_2"][l, i], d["ffn_w_up_2"][l, i], d["ffn_w_down_2"][l, i]
        first = 0
        for g, n in enumerate(F2_GROUPS):
            def loads(j):
                out = []
                for s, w in enumerate((wg, wu)):
                    col = j * P + first * P
                    rows = w.rearrange("(k p) n -> p k n", p=P)
                    cols = rows[:, :, col:col + P] if isinstance(col, int) else rows[:, :, bass.ds(col, P)]
                    out.append((lambda raw, s=s: raw[:].rearrange("p (k s n) -> p k s n", s=2, n=P)[:, :, s, :], cols))
                return out
            ready = None
            if g == 0:
                made = list(self.split_made)
                ready = lambda k: [made[k]]
            self.dense(f"gateup{name}{g}", loads, operand or self.operand(self.xh, self.xl), self.swiglu,
                       {self.c_act: 2, self.c_dve: 2}, ready=ready)
            last = g == len(F2_GROUPS) - 1
            down = self.halves(wd, n, P, first * P)
            made = self.made(n, 1)
            if last:
                self.clear_sum()
            ev, per = self.to_f(g > 0, last, 1)
            self.dense(f"back{name}{g}", lambda j: down(j * P), self.operand(self.ah, self.al2), ev, per,
                       ready=made)
            first += n
        self.post_norm(gain, next_gain)

    def pool_mixer(self):
        d, f, nc = self.dram, self.flow, self.nc
        made = list(self.split_made)
        w_in = self.halves(d["pool_w_in_2"][0], KC, 2 * P)
        self.dst_free = None
        self.pooled = []

        ev, _ = self.scaled(self.u)

        def evacuate(j, t, bank, mark):
            ev(j, t, bank, mark)
            u, s = self.u[:, 2 * j + t, :], [self.u[:, 8 + 2 * t, :], self.u[:, 9 + 2 * t, :]]
            v, src = self.v, u
            m = f.at(self.c_ev)
            w = 1
            n = 0
            while w < POOL_WINDOWS[j]:
                dst = s[n % 2]
                v.after(m)
                nc.vector.tensor_copy(dst[:, 0:w], src[:, 0:w])
                m = v.did(nc.vector.tensor_tensor(dst[:, w:T], src[:, w:T], src[:, 0:T - w], ALU.add))
                src = dst
                w *= 2
                n += 1
            dst = s[n % 2]
            m = v.did(v.after(m, self.inv_loaded[j]).tensor_tensor(dst, src, self.inv[:, j, :], ALU.mult))
            m = v.did(v.after(m, f.at(self.c_act)).tensor_tensor(dst, dst, u, ALU.subtract))
            self.pooled.append(self.split(dst, None, self.mh[:, 2 * j + t, :], self.ml[:, 2 * j + t, :], m))
        self.inv = self.u[:, 14:18, :]
        self.inv_loaded = []
        for g in range(4):
            a = self.a.after(f.at(self.c_dve))
            src = d["inv_count"][g:g + 1, :].to_broadcast([P, T])
            self.inv_loaded.append(self.a.did(a.dma_start(self.inv[:, g, :], src), self.c_spill, 16))
        self.inv_loaded = [self.inv_loaded[-1]] * 4
        self.dense("pool_in", lambda j: w_in(j * 2 * P), self.operand(self.xh, self.xl), evacuate,
                   ready=lambda k: [made[k]])
        wg = d["pool_w_group_2"][0]
        grouped = []

        def ev_group(j, t, bank, mark):
            jj = 2 * j + t
            r = self.ta[t]
            v = self.v.after(mark, f.at(self.c_act), f.at(self.c_dve))
            m = self.v.did(v.tensor_scalar(r[:], bank[:], self.gain_col(R_POOL, jj), None, ALU.mult), self.c_ev)
            grouped.append(self.split(r[:], None, self.xh[:, jj, :], self.xl[:, jj, :], m))
        pooled = self.pooled
        jnow = [0]

        def loads_group(j):
            jnow[0] = j
            return self.halves(wg[j], 2, 2 * P)(0)

        def pooled_rhs(k):
            jj = 2 * jnow[0] + k
            self.pe.after(pooled[jj])
            return self.mh[:, jj, :], self.ml[:, jj, :]
        self.dense("pool_group", loads_group, pooled_rhs, ev_group, ready=lambda k: [])
        self.clear_sum()
        w_out = self.halves(d["pool_w_out_2"][0], KC, 2 * P)
        ev, per = self.to_f(False, True, 2)
        self.dense("pool_out", lambda j: w_out(j * 2 * P), self.operand(self.xh, self.xl), ev, per,
                   ready=lambda k: [grouped[k]])

    def keys_and_values(self, next_gain):
        d, f = self.dram, self.flow
        made = list(self.split_made)
        self.dst_free = None
        w_k, w_v = [self.halves(d[name], KC, 2 * P) for name in ("w_k_2", "w_v_2")]
        def spill(tile):
            a = self.a.after(f.at(self.c_ev))
            self.spilled = self.a.did(a.dma_start(d["kv"][tile:tile + 2].rearrange("j p t -> p j t"),
                                                    self.qkv[:, tile:tile + 2, :]), self.c_spill, 16)
        for n, (name, w) in enumerate((("k", w_k), ("v", w_v))):
            scaled, _ = self.scaled(self.qkv, 12 * n)

            def evacuate(j, t, bank, mark):
                if t == 0 and (n or j):
                    spill(12 * n + 2 * j - 2)
                scaled(j, t, bank, mark)
            self.dense(name, lambda j: w(j * 2 * P), self.operand(self.xh, self.xl), evacuate, straight=True,
                       ready=(lambda k: [made[k]]) if n == 0 else None)
            if n == 0:
                m = self.x_made[-1]
                for j in range(KC):
                    self.split_made[j] = self.split(self.x[:, j, :], self.gain_col(next_gain, j),
                                                    self.mh[:, j, :], self.ml[:, j, :], m, (f.at(self.c_dve),) if j == 0 else ())
        spill(22)


    def act(self, out, in_, fn, *marks, **kw):
        return self.a.did(self.a.after(*marks).activation(out, in_, fn, **kw))

    def tt(self, out, a, b, op, *marks):
        return self.v.did(self.v.after(*marks).tensor_tensor(out, a, b, op))

    def ts(self, out, a, s1, s2, op0, op1, *marks):
        v = self.v.after(*marks)
        return self.v.did(v.tensor_scalar(out, a, s1, s2, op0, op1) if op1 is not None
                          else v.tensor_scalar(out, a, s1, None, op0))

    def stt(self, out, a, s, b, op0, op1, *marks):
        return self.v.did(self.v.after(*marks).scalar_tensor_tensor(out, a, s, b, op0, op1))

    def mm(self, out, lhsT, rhs, start=True, stop=True):
        return self.nc.tensor.matmul(out, lhsT, rhs, start=start, stop=stop, skip_group_check=True)

    def tokens_first(self, src, dst, bank, *marks):
        self.pe.after(*marks, self.free[bank])
        for b in range(NB):
            mm = self.nc.tensor.transpose(self.bank[bank][:, b * P:b * P + P], src[:, b * P:b * P + P], self.c(C_IDENT))
        m = self.pe.did(mm)
        self.free[bank] = m = self.act(dst, self.bank[bank][:], ACT.Copy, m)
        return m

    def head_rstd(self, tiles, rows, bank, squares, *marks):
        w, n = 2 * len(tiles), len(squares)
        ps = self.bank[bank]
        read = None
        for first in range(0, len(tiles), n):
            for j in range(first, min(first + n, len(tiles))):
                m = self.act(squares[j % n], tiles[j], ACT.Square, *marks, read)
            yield
            self.pe.after(m, self.free[bank])
            for j in range(first, min(first + n, len(tiles))):
                mm = self.mm(ps[0:w, :], self.const[:, C_IND, 16 * j:16 * j + w], squares[j % n], j == 0, j == len(tiles) - 1)
            read = self.pe.did(mm)
            yield
        m = self.free[bank] = self.v.did(self.v.after(read, *marks).tensor_copy(rows[0:w, :], ps[0:w, :]))
        yield
        self.pe.after(m)
        for b in range(NB):
            mm = self.nc.tensor.transpose(ps[:, b * w:b * w + w], rows[0:w, b * P:b * P + P], self.const[0:w, C_IDENT, 0:w])
        read = self.pe.did(mm)
        yield
        cols = squares[0][:, 0:NB * w]
        m = self.free[bank] = self.ts(cols, ps[:, 0:NB * w], 1.0 / HD, EPS, ALU.mult, ALU.add, read, *marks)
        yield
        m = self.act(cols, cols, ACT.Sqrt, m)
        yield
        m = self.v.did(self.v.after(m).reciprocal(cols, cols))
        yield
        self.pe.after(m, self.free[bank])
        for b in range(NB):
            mm = self.nc.tensor.transpose(ps[0:w, b * P:b * P + P], cols[:, b * w:b * w + w], self.c(C_IDENT))
        m = self.pe.did(mm)
        yield
        m = self.free[bank] = self.v.did(self.v.after(m, *marks).tensor_copy(rows[0:w, :], ps[0:w, :]))
        return m

    def spread(self, rows, n, j, bank, *marks):
        self.pe.after(*marks, self.free[bank])
        return self.pe.did(self.mm(self.bank[bank][:], self.sel[0:n, j, :], rows[0:n, :]))

    def into_mix(self, j, t, gain, bank, factor, *marks):
        m = self.free[bank] = self.stt(t, t, gain, self.bank[bank][:], ALU.mult, ALU.mult, *marks)
        if factor is not None:
            m = self.tt(t, t, factor, ALU.mult, m)
        self.mix_made[j] = self.split(t, None, self.mh[:, j, :], self.ml[:, j, :], m)


    def mlstm(self, l):
        f, sp = self.flow, lambda k: self.spare[:, k, :]
        s_bank, row_bank, num_bank, den_bank = 4, 5, 6, 7
        begin = [f.at(self.c_ev), f.at(self.c_mm), f.at(self.c_dve), f.at(self.c_act)]
        for b in (s_bank, row_bank, num_bank, den_bank):
            self.free[b] = f.at(self.c_dve)
        weights = [self.spare[:, 4 * b:4 * b + 4, :] for b in range(2)]
        enb, den, md, rows = sp(10), sp(11), sp(12), sp(12)
        r0, r1, r2 = [self.spare[0:4, k, :] for k in (13, 14, 15)]
        ones, hot = self.tb[0][0:4, :], self.tb[1][0:4, :].rearrange("p (h n) -> p h n", h=4)
        o = self.v.did(self.v.after(*begin).memset(ones, 1.0))
        for h in range(4):
            hot_made = self.v.did(self.v.queue.tensor_copy(hot[:, h, :], self.const[0:4, C_IDENT, h:h + 1].to_broadcast([4, P])))
        m = self.ts(r0, r0, self.gate_b[0:4, 2 * l:2 * l + 1], None, ALU.add, None, *begin)
        m = self.ts(r1, r1, self.gate_b[0:4, 2 * l + 1:2 * l + 2], None, ALU.add, None, m)
        m = self.stt(r2, r1, -1.0, r1, ALU.mult, ALU.max, m)
        yield
        m = self.act(r2, r2, ACT.Exp, m, scale=-1.0)
        yield
        m = self.act(r2, r2, ACT.Ln, m, bias=1.0)
        yield
        m = self.stt(r1, r1, 0.0, r2, ALU.min, ALU.subtract, m)
        m = self.v.did(self.v.after(m, o).tensor_tensor_scan(r2, ones, r1, 0.0, ALU.mult, ALU.add))
        a_made = self.tt(r0, r0, r2, ALU.subtract, m)
        big_made = self.v.did(self.v.after(a_made).tensor_tensor_scan(r1, r0, r0, 0.0, ALU.max, ALU.max))
        m_made = self.tt(r2, r2, r1, ALU.add, big_made)
        yield
        self.pe.after(a_made, self.free[row_bank])
        for b in range(NB):
            mm = self.nc.tensor.transpose(self.bank[row_bank][:, 4 * b:4 * b + 4], r0[:, b * P:b * P + P],
                                          self.const[0:4, C_IDENT, 0:4])
        acol = self.tiny[:, 16:32]
        t = self.pe.did(mm)
        yield
        acol_made = self.free[row_bank] = self.v.did(self.v.after(t).tensor_copy(acol, self.bank[row_bank][:, 0:16]))
        qk_made = [None] * 4
        for j in (0, 2, 1, 3):
            u, t = self.u[:, MQ + j, :], self.ta[j // 2]
            w = lambda k: self.gain_col(R_CONV + (l * 4 + k) * 4, j)
            m = self.ts(t[:], u, w(3), None, ALU.mult, None, qk_made[j - 1] if j % 2 else None, *begin)
            for shift in (1, 2, 3):
                m = self.stt(t[:, shift:], u[:, 0:T - shift], w(3 - shift), t[:, shift:], ALU.mult, ALU.add, m)
            qk_made[j] = self.act(u, t[:], ACT.Silu, m)
            yield
        h_made = [None, None]
        last = {"md": None, 0: None, 1: None}
        weighed = [None] * 4

        def weigh(h):
            mb, wt = self.bank[row_bank], weights[h % 2]
            self.pe.after(big_made, hot_made, self.free[row_bank])
            mb_made = self.pe.did(self.mm(mb[:], hot[:, h, :], r1))
            yield
            m = self.tt(md.rearrange("p (b t) -> p b t", b=NB), mb[:].rearrange("p (b t) -> p b t", b=NB),
                        self.const[:, C_LATER:C_LATER + 1, :].to_broadcast([P, NB, P]), ALU.add, mb_made, last["md"])
            yield
            self.a.after(m, acol_made, last[h % 2])
            for j in range(NB):
                bias = acol[:, 4 * j + h:4 * j + h + 1]
                i1 = self.a.queue.activation(wt[:, j, j * P:j * P + P], md[:, j * P:j * P + P], ACT.Exp, bias=bias, scale=-1.0)
                if j < NB - 1:
                    i1 = self.a.queue.activation(wt[:, j, (j + 1) * P:T], mb[:, (j + 1) * P:T], ACT.Exp,
                                                 bias=bias, scale=-1.0)
            weighed[h] = last["md"] = self.free[row_bank] = self.a.did(i1)
        finish(weigh(0))
        for i in range(2):
            vt = sp(8 + i)
            vt_made = self.tokens_first(self.u[:, MV + i, :], vt, row_bank, *begin)
            yield
            for e in range(2):
                h = 2 * i + e
                part = slice(e * HD, e * HD + HD)
                wt, w_made = weights[e], weighed[h]
                if h < 3:
                    ahead = weigh(h + 1)
                else:
                    ahead = iter(())

                def scores(b):
                    self.pe.after(qk_made[i], qk_made[2 + i], self.free[s_bank])
                    for j in range(b + 1):
                        mm = self.mm(self.bank[s_bank][:, j * P:j * P + P], self.u[part, MK + i, j * P:j * P + P],
                                     self.u[part, MQ + i, b * P:b * P + P], j == 0, j == b)
                    return self.pe.did(mm)
                s_made = scores(0)
                yield
                for b in range(NB):
                    view = wt[:, 0:b + 1, b * P:b * P + P]
                    m = self.free[s_bank] = self.stt(
                        view, self.bank[s_bank][:, 0:(b + 1) * P].rearrange("p (j t) -> p j t", t=P), HD ** -0.5, view,
                        ALU.mult, ALU.mult, s_made, w_made)
                    yield
                    if b + 1 < NB:
                        s_made = scores(b + 1)
                    self.pe.after(m, vt_made, self.free[num_bank], self.free[den_bank])
                    for j in range(b + 1):
                        src = wt[:, j, b * P:b * P + P]
                        first, final = b == 0 and j == 0, b == NB - 1 and j == b
                        self.mm(self.bank[num_bank][part, b * P:b * P + P], vt[:, j * P + e * HD:j * P + e * HD + HD], src, first, final)
                        mm = self.mm(self.bank[den_bank][part, b * P:b * P + P], self.ones[:, 0:HD], src, first, final)
                    nd_made = last[e] = self.pe.did(mm)
                    next(ahead, None)
                    yield
                finish(ahead)
            sr = self.spread(r2, 4, i, row_bank, m_made)
            yield
            m = self.free[row_bank] = self.act(enb, self.bank[row_bank][:], ACT.Exp, sr, h_made[0], *begin, scale=-1.0)
            m = self.free[den_bank] = self.act(den, self.bank[den_bank][:], ACT.Abs, nd_made)
            yield
            m = self.tt(den, den, enb, ALU.max, m)
            m = self.v.did(self.v.after(m).reciprocal(den, den))
            h = self.u[:, MV + i, :]
            h_made[i] = self.free[num_bank] = self.tt(h, self.bank[num_bank][:], den, ALU.mult, m, vt_made)
            yield
        m = yield from self.head_rstd([self.u[:, MV + i, :] for i in range(2)], rows, row_bank,
                                      [self.ta[0][:], self.ta[1][:]], *h_made, last["md"])
        for i in range(2):
            sg = self.act(self.u[:, MO + i, :], self.u[:, MO + i, :], ACT.Sigmoid, *begin)
            sr = self.spread(rows, 4, i, s_bank + i, m)
            yield
            self.into_mix(i, self.u[:, MV + i, :], self.gain_col(R_MN, l), s_bank + i, self.u[:, MO + i, :], sr, sg)


    def diff_attention(self, l):
        f, d = self.flow, self.dram
        begin = [f.at(c) for c in (self.c_ev, self.c_mm, self.c_dve, self.c_act, self.c_pe)]
        bufs = [self.u[:, k, :] for k in (0, 1, 4, 5, 6, 7)]
        cos, sin = self.u[:, 2, :], self.u[:, 3, :]
        a = self.a.after(*begin)
        self.a.did(a.dma_start(self.u[:, 2:4, :].rearrange("p a t -> p (a t)"), d["rot"]), self.c_tab, 16)
        lv = bufs[4][:, 0:4 * HD]
        loaded = self.a.did(a.dma_start(lv, d["diff_lambda"][l:l + 1].rearrange("l a n -> l (a n)").to_broadcast([P, 4 * HD])),
                            self.c_tab, 16)
        lv = lv.rearrange("p (a b n) -> p a b n", a=2, b=2)
        pr = bufs[5][:, 0:2 * HD].rearrange("p (a n) -> p a n", a=2)
        t = self.tiny
        rows = self.tb[0]
        rstd = yield from self.head_rstd([self.u[:, AQ + j, :] for j in range(8)], rows, 4, bufs[0:4], *begin)
        m = self.tt(pr, lv[:, :, 0, :], lv[:, :, 1, :], ALU.mult, loaded, *begin)
        m = self.v.did(self.v.after(m).tensor_reduce(t[:, 32:34], pr, AX.X, ALU.add))
        yield
        m = self.act(t[:, 34:36], t[:, 32:34], ACT.Exp, m)
        yield
        m = self.tt(t[:, 36:37], t[:, 35:36], t[:, 34:35], ALU.subtract, m)
        init = 0.8 - 0.6 * math.exp(-0.3 * l)
        self.ts(t[:, 38:39], self.gain_col(R_SUB, l), 1.0 - init, None, ALU.mult, None)
        lam_made = self.ts(t[:, 37:38], t[:, 36:37], -init, None, ALU.add, None, m)
        yield
        self.diff = lambda n, banks: self.diff_heads(l, n, init, bufs[3 * n:3 * n + 3], banks, (cos, sin, loaded),
                                                     rows, rstd, lam_made)

    def diff_heads(self, l, stream, init, bufs, banks, tables, rows, rstd, lam_made):
        at, p0, p1 = bufs
        p = (p0, p1)
        s_banks, o_bank = banks[0:2], banks[2]
        cos, sin, loaded = tables
        neg_lam = self.tiny[:, 37:39]
        st = self.tiny[:, 40 + 8 * stream:48 + 8 * stream]
        self.pe.after(self.flow.at(self.c_ev))
        at_read, last = None, lam_made
        for h in (stream, stream + 2):
            turned = []
            q_rot, k_rot, vt = [self.u[:, first + h, :] for first in (AQ, AK, AV)]
            both = [(0, q_rot, R_QN, p0, s_banks[0]), (1, k_rot, R_KN, p1, s_banks[1])]
            sr = [self.spread(rows, 16, 4 * k + h, bank, rstd) for k, u, gain, r, bank in both]
            yield
            scaled = []
            for k, u, gain, r, bank in both:
                m = self.free[bank] = self.stt(u, u, self.gain_col(gain, l), self.bank[bank][:], ALU.mult, ALU.mult, sr[k])
                scaled.append(m)
            yield
            pm = []
            for k, u, gain, r, bank in both:
                self.pe.after(scaled[k], self.free[bank])
                pm.append(self.pe.did(self.mm(self.bank[bank][:], self.c(C_ROT_A), u)))
            yield
            for k, u, gain, r, bank in both:
                m2 = self.free[bank] = self.tt(r, self.bank[bank][:], sin, ALU.mult, pm[k], loaded, last, at_read)
                m1 = self.tt(u, u, cos, ALU.mult, scaled[k], loaded)
                turned.append(self.tt(u, u, r, ALU.add, m1, m2))
            vt_made = self.tokens_first(vt, vt, o_bank, rstd)
            yield
            for qb in range(NB):
                w = (qb + 1) * P
                self.pe.after(*turned, self.free[s_banks[0]], self.free[s_banks[1]])
                for e, bank in enumerate(s_banks):
                    part = slice(e * HD, e * HD + HD)
                    self.mm(self.bank[bank][:, 0:w], q_rot[part, qb * P:w], k_rot[part, 0:w], True, False)
                    mm = self.mm(self.bank[bank][:, qb * P:w], self.ident16(), self.mask16(CAUSAL), False, True)
                m = self.pe.did(mm)
                yield
                self.v.after(m, last)
                for e, bank in enumerate(s_banks):
                    i1 = self.v.queue.tensor_reduce(st[:, e:e + 1], self.bank[bank][:, 0:w], AX.X, ALU.max, negate=True)
                m = self.v.did(i1)
                yield
                self.a.after(m, last)
                for e, bank in enumerate(s_banks):
                    i1 = self.a.queue.activation(p[e][:, 0:w], self.bank[bank][:, 0:w], ACT.Exp, bias=st[:, e:e + 1],
                                                 accum_out=st[:, 2 + e:3 + e])
                m = self.free[s_banks[0]] = self.free[s_banks[1]] = self.a.did(i1)
                yield
                m = self.v.did(self.v.after(m).reciprocal(st[:, 4:6], st[:, 2:4]))
                m2 = self.tt(st[:, 6:7], st[:, 5:6], neg_lam[:, 0:1], ALU.mult, m, lam_made)
                m = self.ts(p0[:, 0:w], p0[:, 0:w], st[:, 4:5], None, ALU.mult, None, m)
                m = last = self.stt(p0[:, 0:w], p1[:, 0:w], st[:, 6:7], p0[:, 0:w], ALU.mult, ALU.add, m, m2)
                yield
                bank = s_banks[0]
                self.pe.after(m, self.free[bank])
                for b in range(qb + 1):
                    mm = self.nc.tensor.transpose(self.bank[bank][:, b * P:b * P + P], p0[:, b * P:b * P + P], self.c(C_IDENT))
                m = last = self.pe.did(mm)
                yield
                m = self.free[bank] = self.act(at[:, 0:w], self.bank[bank][:, 0:w], ACT.Copy, m, at_read)
                yield
                self.pe.after(m, vt_made, self.free[o_bank])
                for b in range(qb + 1):
                    mm = self.mm(self.bank[o_bank][:, qb * P:w], vt[:, b * P:b * P + P], at[:, b * P:b * P + P],
                                 qb == 0 and b == 0, b == qb)
                o_made = at_read = self.pe.did(mm)
                yield
            o, sq, r = p0, p1, at
            m2 = self.act(sq, self.bank[o_bank][:], ACT.Square, o_made, last)
            m = self.free[o_bank] = self.act(o, self.bank[o_bank][:], ACT.Copy, o_made, last)
            yield
            bank = s_banks[1]
            ps, col = self.bank[bank], st[:, 0:4]
            self.pe.after(m2, self.free[bank])
            for b in range(NB):
                mm = self.mm(ps[:, b:b + 1], sq[:, b * P:b * P + P], self.ones[:, 0:1], b == 0, b == NB - 1)
            m3 = self.pe.did(mm)
            yield
            m3 = self.free[bank] = self.ts(col, ps[:, 0:NB], 1.0 / (2 * HD), EPS, ALU.mult, ALU.add, m3, last)
            yield
            m3 = self.act(col, col, ACT.Sqrt, m3)
            yield
            m3 = self.v.did(self.v.after(m3).reciprocal(col, col))
            self.v.after(m3, at_read)
            for b in range(NB):
                i1 = self.v.queue.tensor_scalar(r[:, b * P:b * P + P], self.c(C_IDENT), col[:, b:b + 1], None, ALU.mult)
            m3 = self.v.did(i1)
            yield
            self.pe.after(m3, self.free[bank])
            m3 = self.pe.did(self.mm(ps[:], self.ones[:], r))
            yield
            m3 = self.free[bank] = self.stt(o, o, neg_lam[:, 1:2], ps[:], ALU.mult, ALU.mult, m3, m)
            last = self.mix_made[2 + h] = self.split(o, None, self.mh[:, 2 + h, :], self.ml[:, 2 + h, :], m3)
            yield


    def lower_bounds(self):
        lb, p = self.lb, [self.cols[:, R_LB + 2 * l:R_LB + 2 * l + 2] for l in range(DEPTH)]
        t = self.tiny
        m = self.tt(t[:, 0:2], p[0], p[1], ALU.max, self.flow.at(self.c_dve))
        for l in range(DEPTH):
            m2 = self.tt(t[:, 2 + 2 * l:4 + 2 * l], p[l], t[:, 0:2], ALU.subtract, m)
        m = self.act(t[:, 6:10], t[:, 2:6], ACT.Exp, m2)
        m = self.tt(t[:, 10:12], t[:, 6:8], t[:, 8:10], ALU.add, m)
        m = self.v.did(self.v.after(m).reciprocal(t[:, 12:14], t[:, 10:12]))
        for l in range(DEPTH):
            m2 = self.tt(t[:, 2 + 2 * l:4 + 2 * l], t[:, 6 + 2 * l:8 + 2 * l], t[:, 12:14], ALU.mult, m)
        m = self.tt(lb[:, 0:2], t[:, 2:4], t[:, 2:4], ALU.subtract, m2)
        m = self.tt(t[:, 0:2], t[:, 2:4], t[:, 4:6], ALU.add, m)
        m = self.tt(lb[:, 2:4], t[:, 0:2], t[:, 2:4], ALU.subtract, m)
        self.ts(lb[:, 4:8], lb[:, 0:4], -1.0, 1.0, ALU.mult, ALU.add, m)

    def hgrn(self, l, banks):
        f = self.flow
        u, s = lambda k: self.u[:, k, :], lambda k: self.scr[:, k, :]
        begin = [f.at(self.c_ev), f.at(self.c_mm)]
        b, dd, z, at, kt = s(0), s(1), [s(2), s(3)], [s(4), s(5)], s(6)
        qs, ks, st, keep, rows, out = s(7), s(8), s(9), s(10), s(11), [s(12), s(13)]
        x_bank, y_bank = banks
        blocks = lambda t: t.rearrange("p (b t) -> p b t", b=NB)
        m = self.v.did(self.v.after(*begin).memset(keep, 1.0))
        keep_made = self.v.did(self.v.after(m).memset(blocks(keep)[:, :, 0:1], 0.0))
        dd_read = b_read = at_read = ks_read = st_read = None
        z_read = [None, None]
        h_made = []
        for i in range(2):
            q, k, fp = u(HQ + i), u(HF + i), dd
            lb, one_lb = self.lb[:, 2 * l + i:2 * l + i + 1], self.lb[:, 4 + 2 * l + i:5 + 2 * l + i]
            q_made = self.act(q, q, ACT.Silu, *begin)
            m = self.act(fp, k, ACT.Sigmoid, dd_read)
            mk = self.act(k, k, ACT.Sigmoid, m, scale=-1.0)
            yield
            m = self.ts(fp, fp, one_lb, lb, ALU.mult, ALU.add, m)
            k_made = self.ts(k, k, one_lb, None, ALU.mult, None, mk)
            yield
            m = self.act(fp, fp, ACT.Ln, m)
            yield
            b_made = self.v.did(self.v.after(m, keep_made, b_read).tensor_tensor_scan(b, keep, fp, 0.0, ALU.mult, ALU.add))
            vt = u(HI + i)
            vt_made = self.tokens_first(vt, vt, x_bank, *begin)
            yield
            self.pe.after(q_made, k_made, self.free[x_bank], self.free[y_bank])
            for e in range(2):
                for c in range(NB):
                    part, blk = slice(e * HD, e * HD + HD), slice(c * P, c * P + P)
                    mm = self.mm(self.bank[banks[e]][:, blk], k[part, blk], q[part, blk], c == 0, c == NB - 1)
            m = self.pe.did(mm)
            yield
            at_made = [None, None]
            for e in range(2):
                at_made[e] = self.free[banks[e]] = self.tt(blocks(at[e]), blocks(self.bank[banks[e]][:]),
                                                    self.const[:, C_IDENT:C_IDENT + 1, :].to_broadcast([P, NB, P]),
                                                    ALU.mult, m, at_read)
            dd_read = b_made

            def decayed(n):
                half = LEVELS[n]
                cut = lambda t: t.rearrange("p (m h b) -> p m h b", h=2, b=half)
                r = cut(b)[:, :, 0, half - 1:half].to_broadcast([P, T // (2 * half), half])
                self.v.after(b_made, dd_read)
                self.v.queue.tensor_tensor(cut(dd)[:, :, 1, :], cut(b)[:, :, 1, :], r, ALU.subtract)
                m = self.tt(cut(dd)[:, :, 0, :], r, cut(b)[:, :, 0, :], ALU.subtract)
                yield
                m = self.act(dd, dd, ACT.Exp, m)
                yield
                zn = z[n % 2]
                self.v.after(m, q_made, k_made, z_read[n % 2])
                self.v.queue.tensor_tensor(cut(zn)[:, :, 1, :], cut(q)[:, :, 1, :], cut(dd)[:, :, 1, :], ALU.mult)
                return self.tt(cut(zn)[:, :, 0, :], cut(k)[:, :, 0, :], cut(dd)[:, :, 0, :], ALU.mult)
            z_made = dd_read = yield from decayed(0)
            yield
            for n in range(len(LEVELS)):
                zn, product = z[n % 2], [None, None]
                for e in range(2):
                    self.pe.after(z_made, self.free[banks[e]])
                    for c in range(NB):
                        part, blk = slice(e * HD, e * HD + HD), slice(c * P, c * P + P)
                        mm = self.mm(self.bank[banks[e]][:, blk], zn[part, blk], zn[part, blk], c == 0, c == NB - 1)
                    product[e] = z_read[n % 2] = self.pe.did(mm)
                if n + 1 < len(LEVELS):
                    z_made = dd_read = yield from decayed(n + 1)
                else:
                    yield
                for e in range(2):
                    mask = self.level[:, n:n + 1, :].to_broadcast([P, NB, P])
                    v = self.v.after(product[e], at_made[e])
                    at_made[e] = self.free[banks[e]] = self.v.did(
                        v.copy_predicated(blocks(at[e]), mask, blocks(self.bank[banks[e]][:])))
                yield
            m = self.act(qs, b, ACT.Exp, b_made, ks_read, st_read, *begin)
            last = blocks(b)[:, :, P - 1:P]
            dec = self.tiny[:, 16 + 4 * i:20 + 4 * i]
            dec_made = self.act(dec.rearrange("p (a b) -> p a b", b=1), last, ACT.Exp, b_made)
            qs_made = self.tt(qs, qs, q, ALU.mult, m)
            m = self.tt(blocks(ks), last.to_broadcast([P, NB, P]), blocks(b), ALU.subtract, ks_read)
            b_read = m
            yield
            m = self.act(ks, ks, ACT.Exp, m, dec_made)
            yield
            m = self.tt(ks, ks, k, ALU.mult, m)
            yield
            kt_made = self.tokens_first(ks, kt, x_bank, m, st_read)
            ks_read = kt_made
            yield
            self.pe.after(*at_made, vt_made, self.free[x_bank])
            for e in range(2):
                for c in range(NB):
                    blk = slice(c * P, c * P + P)
                    mm = self.mm(self.bank[x_bank][e * HD:e * HD + HD, blk], vt[:, c * P + e * HD:c * P + e * HD + HD],
                                 at[e][:, blk], c == 0, False)
            at_read = self.pe.did(mm)
            for c in range(1, NB):
                blk, before = slice(c * P, c * P + P), slice((c - 1) * P, c * P)
                self.pe.after(kt_made, vt_made, self.free[y_bank])
                m = self.pe.did(self.mm(self.bank[y_bank][:, 0:P], kt[:, before], vt[:, before]))
                yield
                new = st[:, P:2 * P]
                m = self.free[y_bank] = self.tt(new, self.bank[y_bank][:, 0:P], self.c(C_BLOCK), ALU.mult, m, at_read)
                if c == 1:
                    m = self.v.did(self.v.after(m, st_read).tensor_copy(st[:, 0:P], new))
                else:
                    m = self.stt(st[:, 0:P], st[:, 0:P], dec[:, c - 1:c], new, ALU.mult, ALU.add, m, dec_made, st_read)
                yield
                self.pe.after(m, qs_made)
                st_read = at_read = self.pe.did(self.mm(self.bank[x_bank][:, blk], st[:, 0:P], qs[:, blk], False, c == NB - 1))
                yield
            h_made.append(self.v.did(self.v.after(st_read).tensor_copy(out[i], self.bank[x_bank][:])))
            self.free[x_bank] = h_made[-1]
            yield
        m = yield from self.head_rstd(out, rows, x_bank, [b, dd], *h_made)
        for i in range(2):
            g = u(HG + i)
            sg = self.act(g, g, ACT.Silu, *begin)
            sr = self.spread(rows, 4, i, banks[i], m)
            yield
            self.into_mix(6 + i, out[i], self.gain_col(R_HN, l), banks[i], g, sr, sg)

    def mixers(self, l, rest, out):
        f, first = self.flow, self.unit
        units = PLAN[self.phase][1]
        mine = 2 * ((first + units) % 2)
        self.diff = None

        def heads():
            yield from self.mlstm(l)
            while self.unit < first + 4:
                yield
            yield from self.diff_attention(l)
            while self.unit < first + 6:
                yield
            yield from self.diff(1, (5, 6, 7))

        def states():
            yield from self.hgrn(l, (mine, mine + 1))
            self.banks_lent = True
            self.clear_sum()
            yield from out()

        def others():
            yield from every(3, rest)
            for b in range(4):
                self.free[b] = f.at(self.c_ev)
            line = states()
            while self.diff is None:
                yield next(line)
            yield from weave((self.diff(0, (2 - mine, 3 - mine, 4)), 1), (line, 1))
        finish(weave((heads(), 1), (others(), 1)))
        self.banks_lent = False



    def rotary_tables(self):
        cos, sin, t, ang = [self.spare[:, k, :] for k in (8, 9, 10, 11)]
        pos = self.spare[:, 12, :].bitcast(I32)
        begin = [self.flow.at(c) for c in (self.c_mm, self.c_dve, self.c_act)]
        a = self.a.after(*begin)
        loaded = self.a.did(a.dma_start(pos, self.dram["positions_2"].to_broadcast([P, T])), self.c_tab, 16)
        m = self.v.did(self.v.after(loaded, *begin).tensor_copy(t, pos))
        ang_made = self.ts(ang, t, self.freq[:, 0:1], None, ALU.mult, None, m)
        whole = 12582912.0
        c1, c2 = 6.28125, float(np.float32(round((TWO_PI - 6.28125) * 2 ** 22) / 2 ** 22))
        parts = (c1, c2, TWO_PI - c1 - c2)
        read = ang_made
        for dst, turn, shift in ((sin, 0.0, 0.0), (cos, 0.25, math.pi / 2)):
            m = self.ts(t, ang, 1 / TWO_PI, turn, ALU.mult, ALU.add, read)
            m = self.ts(t, t, whole, whole, ALU.add, ALU.subtract, m)
            src = ang
            for c in parts:
                m = read = self.stt(dst, t, -c, src, ALU.mult, ALU.add, m)
                src = dst
            if shift:
                m = self.ts(dst, dst, shift, None, ALU.add, None, m)
            m = self.ts(dst, dst, 3.1415925, -3.1415925, ALU.min, ALU.max, m)
            m = self.act(dst, dst, ACT.Sin, m)
        self.tables = cos, sin, m

    def attention_b_groups(self, items, bufs, p_bufs, banks, stats, begin, first):
        f, nc = self.flow, self.nc
        t1, t2, vt = bufs
        s_banks, turn_bank, o_bank = banks[0:2], banks[2], banks[3]
        p_read, vt_read = [None, None], None
        while items:
            i, g = items.pop(0)
            while self.unit <= first + 2 * g + i // 2:
                yield
            cos, sin, tables = self.tables
            queries = f.at(self.c_ev)
            q, k, v = [self.qkv[:, 12 * n + 4 * g + i, :] for n in range(3)]
            block = (lambda t, b: t[:, b * P:b * P + P]) if g == 0 else (lambda t, b: t[:, b::4])
            turned, partners = [], []
            for n, u in enumerate((q, k)):
                self.pe.after(self.free[s_banks[n]], self.kv_loaded, queries, *begin)
                partners.append(self.pe.did(self.mm(self.bank[s_banks[n]][:], self.c(C_ROT_B), u)))
            self.pe.after(self.free[turn_bank], self.kv_loaded)
            for b in range(NB):
                mm = nc.tensor.transpose(self.bank[turn_bank][:, b * P:b * P + P], block(v, b), self.c(C_IDENT))
            m = self.pe.did(mm)
            yield
            vt_made = self.free[turn_bank] = self.act(vt, self.bank[turn_bank][:], ACT.Copy, m, vt_read, *begin)
            last = None
            for n, (u, scale) in enumerate(((q, HD ** -0.5), (k, 1.0))):
                bank = s_banks[n]
                m1 = self.stt(t1, u, scale, cos, ALU.mult, ALU.mult, tables, partners[n], last, self.kv_loaded, queries, *begin)
                m2 = self.free[bank] = self.stt(t2, self.bank[bank][:], scale, sin, ALU.mult, ALU.mult, partners[n])
                last = self.tt(u, t1, t2, ALU.add, m1, m2)
                turned.append(last)
            yield
            if g == 0:
                pairs = [(0, 0, CAUSAL)] + [x for b in range(1, NB) for x in ((b, b - 1, PAST), (b, b, CAUSAL))]
            else:
                pairs = [(b, b, CAUSAL if g == 1 else CAUSAL4) for b in range(NB)]
            spots, col = [], 0
            for n in range(len(pairs)):
                if g == 0 and n == 3:
                    col = T
                spots.append((s_banks[col // T], col % T))
                col += P
            used = sorted({bank for bank, _ in spots})
            spans = []
            for qb in range(NB):
                mine = [n for n in range(len(pairs)) if pairs[n][0] == qb]
                spans.append((*spots[mine[0]], P * len(mine)))

            def scores(e):
                part = slice(e * HD, e * HD + HD)
                self.pe.after(*turned, *[self.free[bank] for bank in used])
                for n, (qb, kb, mask) in enumerate(pairs):
                    bank, at = spots[n]
                    dst = self.bank[bank][:, at:at + P]
                    self.mm(dst, block(q, qb)[part], block(k, kb)[part], at == 0, False)
                    mm = self.mm(dst, self.ident16(), self.mask16(mask), False, n == len(pairs) - 1)
                return self.pe.did(mm)
            s_made = scores(0)
            yield
            for e in range(2):
                part, h = slice(e * HD, e * HD + HD), 2 * i + e
                self.v.after(s_made)
                for qb, (bank, at, w) in enumerate(spans):
                    i1 = self.v.queue.tensor_reduce(stats[:, 0, g, qb, h:h + 1], self.bank[bank][:, at:at + w], AX.X,
                                                    ALU.max, negate=True)
                m = self.v.did(i1)
                yield
                p = p_bufs[e]
                self.a.after(m, p_read[e], *begin)
                col = 0
                for qb, (bank, at, w) in enumerate(spans):
                    i1 = self.a.queue.activation(p[:, col:col + w], self.bank[bank][:, at:at + w], ACT.Exp,
                                                 bias=stats[:, 0, g, qb, h:h + 1], accum_out=stats[:, 1, g, qb, h:h + 1])
                    col += w
                m = p_made = self.a.did(i1)
                for bank in used:
                    self.free[bank] = m
                yield
                if e == 0:
                    s_made = scores(1)
                    yield
                done = 0
                while done < len(pairs):
                    n = min(4, len(pairs) - done)
                    self.pe.after(p_made, self.free[turn_bank])
                    for c in range(n):
                        mm = nc.tensor.transpose(self.bank[turn_bank][:, c * P:c * P + P],
                                                 p[:, (done + c) * P:(done + c + 1) * P], self.c(C_IDENT))
                    m = self.pe.did(mm)
                    yield
                    m = self.free[turn_bank] = self.act(p[:, done * P:(done + n) * P], self.bank[turn_bank][:, 0:n * P],
                                                        ACT.Copy, m)
                    yield
                    done += n
                self.pe.after(m, vt_made, self.free[o_bank])
                for n, (qb, kb, mask) in enumerate(pairs):
                    mm = self.mm(self.bank[o_bank][part, qb * P:qb * P + P], vt[:, kb * P + e * HD:kb * P + e * HD + HD],
                                 p[:, n * P:n * P + P], n == 0, n == len(pairs) - 1)
                m = p_read[e] = vt_read = self.pe.did(mm)
                yield
            if g == 0:
                self.free[o_bank] = self.v.did(self.v.after(m).tensor_copy(q, self.bank[o_bank][:]))
            else:
                self.free[o_bank] = self.v.did(self.v.after(m).tensor_copy(
                    q.rearrange("p (j r) -> p r j", r=4), self.bank[o_bank][:].rearrange("p (r j) -> p r j", r=4)))

    def attention_b(self, queries):
        f, s, nc = self.flow, lambda k: self.scr[:, k, :], self.nc
        spare = lambda k: self.spare[:, k, :]
        wide = lambda t: t.rearrange("p a t -> p (a t)")
        stats = spare(15)[:, 0:192].rearrange("p (k g b h) -> p k g b h", k=2, g=3, b=4)
        items = [(i, g) for g in range(3) for i in range(4)]
        first = self.unit

        def early():
            while self.unit == first:
                yield
            begin = [f.at(c) for c in (self.c_ev, self.c_dve)]
            yield from self.attention_b_groups(items, [self.ta[1][:], self.tb[1][:], spare(10)],
                                               [wide(self.spare[:, k:k + 2, :]) for k in (11, 13)], (4, 5, 6, 7), stats, begin, first)

        def late():
            yield from every(2, queries)
            begin = [f.at(c) for c in (self.c_ev, self.c_mm)]
            for b in range(4):
                self.free[b] = f.at(self.c_ev)
            yield from self.attention_b_groups(items, [self.ta[0][:], self.tb[0][:], s(8)],
                                               [wide(self.scr[:, k:k + 2, :]) for k in (0, 2)], (0, 1, 2, 3), stats, begin, first)
        finish(weave((early(), 1), (late(), 1)))
        rows = [[s(4 + 3 * k + g)[0:8, :] for g in range(3)] for k in range(2)]
        m = [f.at(self.c_dve), f.at(self.c_act), f.at(self.c_pe)]
        for k in range(2):
            for g in range(3):
                bank = 2 + (3 * k + g) % 2
                self.pe.after(*m, self.free[bank])
                for b in range(NB):
                    mm = nc.tensor.transpose(self.bank[bank][0:8, b * P:b * P + P], stats[:, k, g, b, :], self.c(C_IDENT))
                t = self.pe.did(mm)
                src, dst = self.bank[bank][0:8, :], rows[k][g]
                if g:
                    src, dst = src.rearrange("p (r j) -> p r j", r=4), dst.rearrange("p (j r) -> p r j", r=4)
                row_made = self.free[bank] = self.v.did(self.v.after(t, *m).tensor_copy(dst, src))
        top, z = s(10)[0:8, :], s(11)[0:8, :]
        m = self.tt(top, rows[0][0], rows[0][1], ALU.min, row_made)
        m = self.tt(top, top, rows[0][2], ALU.min, m)
        below = [self.tt(rows[0][g], top, rows[0][g], ALU.subtract, m) for g in range(3)]
        exps = [self.act(rows[0][g], rows[0][g], ACT.Exp, below[g]) for g in range(3)]
        for g in range(3):
            w, den = rows[0][g], rows[1][g]
            if g == 0:
                zm = self.tt(z, w, den, ALU.mult, exps[g])
            else:
                n = self.tt(den, w, den, ALU.mult, exps[g])
                zm = self.tt(z, z, den, ALU.add, n, zm)
        m = self.v.did(self.v.after(zm).reciprocal(z, z))
        for g in range(3):
            w_made = self.tt(rows[0][g], rows[0][g], z, ALU.mult, m)
        self.o_made = []
        for i in range(4):
            t, acc = self.ta[i % 2], self.tb[i % 2]
            for g in range(3):
                sp = self.spread(rows[0][g], 8, i, 2 + (3 * i + g) % 4, w_made)
                bank = 2 + (3 * i + g) % 4
                o = self.qkv[:, 4 * g + i, :]
                if g == 0:
                    m = self.free[bank] = self.tt(acc[:], self.bank[bank][:], o, ALU.mult, sp, f.at(self.c_dve), f.at(self.c_act))
                else:
                    n = self.free[bank] = self.tt(t[:], self.bank[bank][:], o, ALU.mult, sp, f.at(self.c_dve))
                    m = self.tt(acc[:], acc[:], t[:], ALU.add, n)
            self.o_made.append(self.split(acc[:], None, self.oh[:, i, :], self.ol[:, i, :], m))

    def gate_rows(self, l):
        w_in = self.dram["w_in"][l]
        w = HD

        def loads(j):
            out = []
            for s in range(2):
                src = w_in[:, GATES + 4 * s:GATES + 4 * s + 4].rearrange("(k p) n -> p k n", p=P)
                out.append((lambda raw, s=s: raw[:, 0:KC * w].rearrange("p (k n) -> p k n", n=w)[:, :, 32 * s:32 * s + 4], src))
            return out

        def gate(slot):
            bank = self.bank[2 * slot]
            for k in range(KC):
                hi = self.whi[slot][:, k * w:k * w + w]
                lo = self.wlo[slot][:, k * w:k * w + w]
                self.nc.tensor.matmul(bank[0:w, :], hi, self.xh[:, k, :], start=k == 0, stop=False)
                self.nc.tensor.matmul(bank[0:w, :], hi, self.xl[:, k, :], start=False, stop=False)
                mm = self.nc.tensor.matmul(bank[0:w, :], lo, self.xh[:, k, :], start=False, stop=k == KC - 1)
            self.gates_bank, self.gates_mark = bank, self.pe.did(mm, self.c_mm, 2)
            v = self.v.after(self.gates_mark, self.rs_made)
            v.tensor_tensor(self.spare[0:4, 13, :], bank[0:4, :], self.rs[0:4, :], ALU.mult)
            self.v.did(v.tensor_tensor(self.spare[0:4, 14, :], bank[32:36, :], self.rs[0:4, :], ALU.mult), self.c_ev, 2)
        self.dense(f"gates{l}", loads, None, None, gate=gate)

    def block_one(self, l):
        d = self.dram
        w_in = self.halves(d["w_in"][l], KC, 2 * P)
        self.dst_free = None
        ev, per = self.scaled(self.u)
        made = list(self.split_made)
        self.dense(f"in_m{l}", lambda j: w_in(j * (2 * P)), self.operand(self.xh, self.xl), ev, per,
                   ready=lambda k: [made[k]])
        self.gate_rows(l)
        ev, per = self.scaled(self.u, AQ)
        self.mix_made = [None] * KC
        if l == 0:
            self.lower_bounds()
        rest = self.dense_steps(f"in_ah{l}", lambda j: w_in(j * (2 * P) + M_COLS), self.operand(self.xh, self.xl),
                                ev, per, straight=True)
        residual, per2 = self.to_residual(R_NORM2 + l * KC)
        w_out = self.halves(d["w_out"][l], KC, 2 * P)
        out = lambda: self.dense_steps(f"out{l}", lambda j: w_out(j * 2 * P), self.operand(self.mh, self.ml), residual, per2,
                                       ready=lambda k: self.mix_made[k] and [self.mix_made[k]],
                                       order=(0, 1, 6, 7, 3, 2, 5, 4))
        self.mixers(l, rest, out)
        self.norm_due = self.flow.at(self.c_dve)
        self.relu_ffn(l, R_NORM1 + KC if l == 0 else R_GAIN2)

    def block_two(self):
        d, f = self.dram, self.flow
        self.split_made = [f.at(self.c_dve)] * KC
        gain = lambda l, g: R_GAIN2 + (l * 6 + g) * KC
        self.swiglu_ffn("a", 0, 0, gain(0, 1), gain(0, 2))
        self.pool_mixer()
        self.post_norm(gain(0, 3), gain(0, 4))
        self.swiglu_ffn("b", 0, 1, gain(0, 5), R_KV)
        self.keys_and_values(gain(1, 0))
        self.a.after(self.spilled)
        self.v.after(self.spilled)
        f_home, self.f = self.f, self.scr
        self.swiglu_ffn("c", 1, 0, gain(1, 1), gain(1, 2), self.operand(self.mh, self.ml))
        self.f = f_home
        made = list(self.split_made)
        w = self.halves(d["attn_w_q_2"][0], KC, 2 * P)
        scaled, _ = self.scaled(self.qkv)

        def reload(tile):
            self.kv_loaded = self.a.did(self.a.queue.dma_start(self.qkv[:, 12 + tile:14 + tile, :],
                                                               d["kv"][tile:tile + 2].rearrange("j p t -> p j t")), self.c_kv, 16)
        self.a.after(f.at(self.c_dve), f.at(self.c_mm), self.spilled)

        def evacuate(j, t, bank, mark):
            if t == 0:
                reload(2 * j)
                reload(12 + 2 * j)
            scaled(j, t, bank, mark)
            if j == 0 and t == 1:
                self.rotary_tables()
        self.attention_b(self.dense_steps("q", lambda j: w(j * 2 * P), self.operand(self.xh, self.xl), evacuate,
                                          ready=lambda k: [made[k]], straight=True))
        w_o = self.halves(d["attn_w_o_2"][0], OW // P, 2 * P)
        ev, per = self.to_f(False, True, 2)
        self.clear_sum()
        o = list(self.o_made)
        self.banks_lent = True
        self.dense("o", lambda j: w_o(j * 2 * P), self.operand(self.oh, self.ol), ev, per, ready=lambda k: [o[k]])
        self.banks_lent = False
        self.post_norm(gain(1, 3), gain(1, 4))
        self.swiglu_ffn("d", 1, 1, gain(1, 5), None)

    def run(self):
        xt = self.u[:, 0:8, :].rearrange("p (b h) t -> p b (h t)", b=NB)
        a = self.nc.scalar
        self.x_loaded = self.a.did(a.dma_start(xt, self.dram["x"][0].rearrange("(b p) d -> p b d", p=P)), self.c_tab, 16)
        for view, source in self.halves(self.dram["w_in"][0], KC, 2 * P)(0):
            self.sp.did(self.nc.sync.dma_start(view(self.raw[0]), source), self.c_raw[0], 16)
        self.load_constants()
        self.a.did(self.a.after(self.flow.at(self.c_raw[0])).activation(self.whi[0][:], self.raw[0][:], ACT.Copy), self.c_hi)
        self.g.did(self.g.after(self.flow.at(self.c_hi)).tensor_tensor(
            self.wlo[0][:], self.raw[0][:], self.whi[0][:].bitcast(F32), ALU.subtract), self.c_lo)
        self.load_x()
        for l in range(DEPTH):
            self.block_one(l)
        self.block_two()
        self.store_x()


def build(nc, dram):
    Kernel(nc, dram).run()


_INS = ["x", "norm1_g", "w_in", "mlstm_conv_w", "mlstm_gate_b", "mlstm_norm_g", "diff_q_norm_g", "diff_k_norm_g",
        "diff_lambda", "diff_subln_g", "hgrn_lb_param", "hgrn_norm_g", "w_out", "norm2_g", "w_up", "w_down",
        "positions_2", "norm_gain_2", "ffn_w_gate_2", "ffn_w_up_2", "ffn_w_down_2", "pool_w_in_2", "pool_w_group_2",
        "pool_scale_2", "pool_w_out_2", "kv_norm_gain_2", "w_k_2", "w_v_2", "attn_w_q_2", "attn_w_o_2"]


def kernel(**inputs):
    import concourse.bacc as bacc
    from concourse.bass_utils import run_bass_kernel_spmd

    nc = bacc.Bacc("TRN2", target_bir_lowering=False, num_devices=1)
    arrays = {name: np.ascontiguousarray(inputs[name]) for name in _INS}
    arrays.update(zip(("const", "sel", "freq", "rot", "inv_count", "level"), constants()))
    dram = {name: nc.dram_tensor(f"in_{name}", a.shape, mybir.dt.from_np(a.dtype), kind="ExternalInput").ap()
            for name, a in arrays.items()}
    dram["kv"] = nc.dram_tensor("kv", (24, P, T), F32).ap()
    dram["out"] = nc.dram_tensor("out", (1, T, D), F32, kind="ExternalOutput").ap()
    build(nc, dram)
    result = run_bass_kernel_spmd(nc, [{f"in_{name}": a for name, a in arrays.items()}], core_ids=[0])
    return result.results[0]["out"]
```
